# Optimizing a Trainium2 kernel written in Bass

```python
import math
import jax, jax.numpy as jnp
from jax import lax
import numpy as np

D_MODEL = 2048
BATCH = 1
SEQ = 256
DEPTH = 1

BRANCH_WIDTH = D_MODEL // 2
N_BRANCH = 3
ATTN_HEAD_DIM = 128
ATTN_HEADS = BRANCH_WIDTH // ATTN_HEAD_DIM
ATTN_WIDTH = ATTN_HEADS * ATTN_HEAD_DIM
MOBA_BLOCK = 256
MOBA_TOPK = 3
QUERY_CHUNK = 64
GLA_HEADS = 4
GLA_VAL_DIM = BRANCH_WIDTH // GLA_HEADS
GLA_KEY_DIM = GLA_VAL_DIM // 2
GLA_KEY_WIDTH = GLA_HEADS * GLA_KEY_DIM
GLA_VAL_WIDTH = GLA_HEADS * GLA_VAL_DIM
GLA_GATE_RANK = 16
GLA_GATE_TAU = 16.0
GLA_CHUNK = 64
CONV_WIDTH = BRANCH_WIDTH
CONV_K = 3
D_FF = -(-8 * D_MODEL // (3 * 256)) * 256
RMS_EPS = 1e-6
COL_SIZES = (ATTN_WIDTH, ATTN_WIDTH, ATTN_WIDTH,
             GLA_KEY_WIDTH, GLA_KEY_WIDTH, GLA_VAL_WIDTH,
             GLA_VAL_WIDTH, GLA_GATE_RANK,
             CONV_WIDTH, CONV_WIDTH, CONV_WIDTH,
             N_BRANCH * D_MODEL)
N_IN_COLS = sum(COL_SIZES)


def rms_norm(x, w):
    xf = x.astype(jnp.float32)
    y = xf * lax.rsqrt(jnp.mean(xf * xf, axis=-1, keepdims=True) + RMS_EPS)
    return (y * w.astype(jnp.float32)).astype(x.dtype)

def moba_attention(q, k, v):
    B_, S, H, dh = q.shape
    f32 = jnp.float32
    nb = -(-S // MOBA_BLOCK)
    s_pad = nb * MOBA_BLOCK
    topk = min(MOBA_TOPK, nb)
    pad = ((0, 0), (0, s_pad - S), (0, 0), (0, 0))
    kp = jnp.pad(k, pad)
    vp = jnp.pad(v, pad)
    kb = kp.reshape(B_, nb, MOBA_BLOCK, H, dh).transpose(0, 3, 1, 2, 4)
    vb = vp.reshape(B_, nb, MOBA_BLOCK, H, dh).transpose(0, 3, 1, 2, 4)
    k_mean = jnp.mean(kb.astype(f32), axis=3)
    slopes = 2.0 ** (-8.0 * jnp.arange(1, H + 1, dtype=f32) / H)
    scale = 1.0 / math.sqrt(dh)
    bi = jnp.arange(B_)[:, None, None, None]
    hi = jnp.arange(H)[None, None, :, None]
    blk_ids = jnp.arange(nb)
    in_blk = jnp.arange(MOBA_BLOCK)

    def one_chunk(c):
        start = c * QUERY_CHUNK
        qf = lax.dynamic_slice_in_dim(q, start, QUERY_CHUNK, axis=1).astype(f32)
        t_pos = start + jnp.arange(QUERY_CHUNK)
        own = start // MOBA_BLOCK
        gate = jnp.einsum("bqhd,bhnd->bqhn", qf, k_mean)
        gate = jnp.where((blk_ids < own)[None, None, None, :], gate, -jnp.inf)
        _, sel = lax.top_k(gate, topk)
        sel_valid = sel < own
        k_sel = kb[bi, hi, sel].astype(f32)
        v_sel = vb[bi, hi, sel].astype(f32)
        s_sel = jnp.einsum("bqhd,bqhnkd->bqhnk", qf, k_sel) * scale
        kpos_sel = sel[..., None] * MOBA_BLOCK + in_blk
        dist_sel = (t_pos[None, :, None, None, None] - kpos_sel).astype(f32)
        s_sel = s_sel - slopes[None, None, :, None, None] * dist_sel
        s_sel = jnp.where(sel_valid[..., None], s_sel, -jnp.inf)
        k_own = lax.dynamic_slice_in_dim(kp, own * MOBA_BLOCK, MOBA_BLOCK, axis=1).astype(f32)
        v_own = lax.dynamic_slice_in_dim(vp, own * MOBA_BLOCK, MOBA_BLOCK, axis=1).astype(f32)
        s_own = jnp.einsum("bqhd,bkhd->bqhk", qf, k_own) * scale
        dist_own = t_pos[:, None] - (own * MOBA_BLOCK + in_blk)[None, :]
        s_own = s_own - slopes[None, None, :, None] * dist_own[None, :, None, :].astype(f32)
        s_own = jnp.where((dist_own >= 0)[None, :, None, :], s_own, -jnp.inf)
        n_sel = topk * MOBA_BLOCK
        p = jax.nn.softmax(jnp.concatenate(
            [s_sel.reshape(B_, QUERY_CHUNK, H, n_sel), s_own], axis=-1), axis=-1)
        p_sel = p[..., :n_sel].reshape(B_, QUERY_CHUNK, H, topk, MOBA_BLOCK)
        out = (jnp.einsum("bqhnk,bqhnkd->bqhd", p_sel, v_sel)
               + jnp.einsum("bqhk,bkhd->bqhd", p[..., n_sel:], v_own))
        return out.astype(q.dtype)

    outs = lax.map(one_chunk, jnp.arange(S // QUERY_CHUNK))
    return outs.transpose(1, 0, 2, 3, 4).reshape(B_, S, H, dh)

def gla_attention(q, k, v, log_a):
    B_, S, H, dk = q.shape
    dv = v.shape[-1]
    f32 = jnp.float32
    n = S // GLA_CHUNK

    def chunked(t):
        return t.astype(f32).reshape(B_, n, GLA_CHUNK, H, t.shape[-1]).transpose(0, 3, 1, 2, 4)

    qc = chunked(q) * (dk ** -0.5)
    kc, vc = chunked(k), chunked(v)
    b = jnp.cumsum(chunked(log_a), axis=3)
    b_last = b[..., -1:, :]
    q_in = qc * jnp.exp(b)
    k_in = kc * jnp.exp(-b)
    k_dec = kc * jnp.exp(b_last - b)
    causal = jnp.tril(jnp.ones((GLA_CHUNK, GLA_CHUNK), dtype=bool))
    a_intra = jnp.where(causal, jnp.einsum("bhncd,bhnsd->bhncs", q_in, k_in), 0.0)
    o_intra = jnp.einsum("bhncs,bhnse->bhnce", a_intra, vc)
    kv = jnp.einsum("bhncd,bhnce->bhnde", k_dec, vc)
    decay = jnp.exp(b_last[..., 0, :])

    def step(state, inp):
        kv_n, d_n = inp
        return d_n[..., None] * state + kv_n, state

    _, s_prev = lax.scan(step, jnp.zeros((B_, H, dk, dv), f32),
                         (kv.transpose(2, 0, 1, 3, 4), decay.transpose(2, 0, 1, 3)))
    s_prev = s_prev.transpose(1, 2, 0, 3, 4)
    o = o_intra + jnp.einsum("bhncd,bhnde->bhnce", q_in, s_prev)
    return o.transpose(0, 2, 3, 1, 4).reshape(B_, S, H, dv)

def short_conv(u, w):
    ch = u.shape[-1]
    return lax.conv_general_dilated(
        u, w[:, None, :].astype(u.dtype), window_strides=(1,), padding=[(CONV_K - 1, 0)],
        dimension_numbers=("NWC", "WIO", "NWC"), feature_group_count=ch)

def first_inputs(seed: int = 0) -> dict:
    key = jax.random.key(seed)
    ks = jax.random.split(key, 16)
    L, D = DEPTH, D_MODEL
    nrm = lambda k, shape, s: jax.random.normal(k, shape, jnp.float32) * s
    gain = lambda k, shape: 1.0 + 0.02 * jax.random.normal(k, shape, jnp.float32)
    return {
        "x": nrm(ks[0], (BATCH, SEQ, D), 1.0),
        "norm1_w": gain(ks[1], (L, D)),
        "w_in": nrm(ks[2], (L, D, N_IN_COLS), D ** -0.5),
        "gla_w_up": nrm(ks[3], (L, GLA_GATE_RANK, GLA_KEY_WIDTH), GLA_GATE_RANK ** -0.5),
        "gla_b": nrm(ks[4], (L, GLA_KEY_WIDTH), 0.02),
        "gla_norm_w": gain(ks[5], (L, GLA_VAL_DIM)),
        "conv_w": nrm(ks[6], (L, CONV_K, CONV_WIDTH), CONV_K ** -0.5),
        "w_br_attn": nrm(ks[7], (L, ATTN_WIDTH, D), ATTN_WIDTH ** -0.5),
        "w_br_gla": nrm(ks[8], (L, GLA_VAL_WIDTH, D), GLA_VAL_WIDTH ** -0.5),
        "w_br_conv": nrm(ks[9], (L, CONV_WIDTH, D), CONV_WIDTH ** -0.5),
        "w_out": nrm(ks[10], (L, D, D), D ** -0.5),
        "norm2_w": gain(ks[11], (L, D)),
        "w_ffn_gate": nrm(ks[12], (L, D, D_FF), D ** -0.5),
        "w_ffn_up": nrm(ks[13], (L, D, D_FF), D ** -0.5),
        "w_ffn_down": nrm(ks[14], (L, D_FF, D), D_FF ** -0.5),
        "final_norm_w": gain(ks[15], (D,)),
    }

def first_block(x, norm1_w, w_in, gla_w_up, gla_b, gla_norm_w, conv_w, w_br_attn, w_br_gla,
              w_br_conv, w_out, norm2_w, w_ffn_gate, w_ffn_up, w_ffn_down, final_norm_w):
    B_, S, D = x.shape
    f32 = jnp.float32
    splits = [int(s) for s in np.cumsum(COL_SIZES)[:-1]]
    for l in range(DEPTH):
        h = rms_norm(x, norm1_w[l])
        proj = h @ w_in[l]
        (q_a, k_a, v_a, q_g, k_g, v_g, r_g, a_down,
         b_gate, c_gate, u_conv, merge) = jnp.split(proj, splits, axis=-1)
        hs_a = (B_, S, ATTN_HEADS, ATTN_HEAD_DIM)
        o_a = moba_attention(q_a.reshape(hs_a), k_a.reshape(hs_a), v_a.reshape(hs_a))
        br_a = o_a.reshape(B_, S, ATTN_WIDTH) @ w_br_attn[l]
        z = (a_down @ gla_w_up[l]).astype(f32) + gla_b[l].astype(f32)
        log_a = jax.nn.log_sigmoid(z) / GLA_GATE_TAU
        hs_k = (B_, S, GLA_HEADS, GLA_KEY_DIM)
        o_g = gla_attention(q_g.reshape(hs_k), k_g.reshape(hs_k),
                            v_g.reshape(B_, S, GLA_HEADS, GLA_VAL_DIM), log_a.reshape(hs_k))
        o_g = o_g * lax.rsqrt(jnp.mean(o_g * o_g, axis=-1, keepdims=True) + RMS_EPS)
        o_g = o_g * gla_norm_w[l].astype(f32)
        o_g = o_g.reshape(B_, S, GLA_VAL_WIDTH) * jax.nn.silu(r_g.astype(f32))
        br_b = o_g.astype(x.dtype) @ w_br_gla[l]
        y_c = b_gate * short_conv(c_gate * u_conv, conv_w[l])
        br_c = y_c @ w_br_conv[l]
        g = jax.nn.sigmoid(merge.astype(f32)).reshape(B_, S, N_BRANCH, D)
        mixed = (g[:, :, 0] * br_a.astype(f32) + g[:, :, 1] * br_b.astype(f32)
                 + g[:, :, 2] * br_c.astype(f32)).astype(x.dtype)
        x = x + mixed @ w_out[l]
        h2 = rms_norm(x, norm2_w[l])
        x = x + (jax.nn.silu(h2 @ w_ffn_gate[l]) * (h2 @ w_ffn_up[l])) @ w_ffn_down[l]
    return rms_norm(x, final_norm_w)


N_Q_HEADS = 16
N_KV_HEADS = 2
HEAD_DIM = 64
Q_PER_KV = N_Q_HEADS // N_KV_HEADS
WINDOW = 128
BLOCK = 128
ATTN_WIDTH_2 = N_Q_HEADS * HEAD_DIM
KV_WIDTH = N_KV_HEADS * HEAD_DIM
SSM_GROUP = 16
SSM_GROUPS = 32
SSM_WIDTH = SSM_GROUP * SSM_GROUPS
SSM_STATE = 64
DT_MIN = 0.001
DT_MAX = 0.1
D_FF_2 = 5632
CONV_WIDTH_2 = 3
IN_COLS = ATTN_WIDTH_2 + 2 * KV_WIDTH + SSM_WIDTH + 2 * D_MODEL
SPLIT_POINTS = (ATTN_WIDTH_2, ATTN_WIDTH_2 + KV_WIDTH, ATTN_WIDTH_2 + 2 * KV_WIDTH,
                ATTN_WIDTH_2 + 2 * KV_WIDTH + SSM_WIDTH,
                ATTN_WIDTH_2 + 2 * KV_WIDTH + SSM_WIDTH + D_MODEL)
NEG_BIG = -1e30


def rms_norm_2(x, g):
    xf = x.astype(jnp.float32)
    y = xf * lax.rsqrt(jnp.mean(xf * xf, axis=-1, keepdims=True) + RMS_EPS)
    return (y * g.astype(jnp.float32)).astype(x.dtype)

def sliding_window_attention(q, k, v, sinks):
    b, l = q.shape[0], q.shape[1]
    nb = l // BLOCK
    qb = q.reshape(b, nb, BLOCK, N_KV_HEADS, Q_PER_KV, HEAD_DIM)
    kb = k.reshape(b, nb, BLOCK, N_KV_HEADS, HEAD_DIM)
    vb = v.reshape(b, nb, BLOCK, N_KV_HEADS, HEAD_DIM)

    def with_prev(t):
        prev = jnp.pad(t, ((0, 0), (1, 0), (0, 0), (0, 0), (0, 0)))[:, :-1]
        return jnp.concatenate([prev, t], axis=2)

    kx = with_prev(kb)
    vx = with_prev(vb)
    scores = jnp.einsum('bnqgrd,bnsgd->bngrqs', qb, kx).astype(jnp.float32) * (HEAD_DIM ** -0.5)
    q_idx = jnp.arange(BLOCK)[:, None]
    s_idx = jnp.arange(2 * BLOCK)[None, :]
    dist = q_idx + BLOCK - s_idx
    band = (dist >= 0) & (dist < WINDOW)
    valid = band[None] & ((jnp.arange(nb)[:, None, None] > 0) | (s_idx[None] >= BLOCK))
    slopes = 2.0 ** (-8.0 * jnp.arange(1, N_Q_HEADS + 1, dtype=jnp.float32) / N_Q_HEADS)
    slopes = slopes.reshape(N_KV_HEADS, Q_PER_KV)
    alibi = -slopes[:, :, None, None] * dist.astype(jnp.float32)[None, None]
    scores = scores + alibi[None, None]
    scores = jnp.where(valid[None, :, None, None], scores, NEG_BIG)
    sink = sinks.astype(jnp.float32).reshape(N_KV_HEADS, Q_PER_KV)[None, None, :, :, None, None]
    m = jnp.maximum(jnp.max(scores, axis=-1, keepdims=True), sink)
    p = jnp.exp(scores - m)
    p = p / (jnp.sum(p, axis=-1, keepdims=True) + jnp.exp(sink - m))
    out = jnp.einsum('bngrqs,bnsgd->bnqgrd', p.astype(v.dtype), vx)
    return out.reshape(b, l, ATTN_WIDTH_2)

def s5_ssm(u, a_re, a_im, log_dt, b_re, b_im, c_re, c_im, d_skip):
    bsz, l = u.shape[0], u.shape[1]
    ug = u.reshape(bsz, l, SSM_GROUPS, SSM_GROUP)
    dt = jnp.exp(log_dt)[:, None]
    mag = jnp.exp(a_re * dt)
    ab_re = mag * jnp.cos(a_im * dt)
    ab_im = mag * jnp.sin(a_im * dt)
    nr = ab_re - 1.0
    ni = ab_im
    den = a_re * a_re + a_im * a_im
    z_re = (nr * a_re + ni * a_im) / den
    z_im = (ni * a_re - nr * a_im) / den
    bb_re = z_re[..., None] * b_re - z_im[..., None] * b_im
    bb_im = z_re[..., None] * b_im + z_im[..., None] * b_re
    bu_re = jnp.einsum('gph,blgh->blgp', bb_re, ug)
    bu_im = jnp.einsum('gph,blgh->blgp', bb_im, ug)
    a_re_t = jnp.broadcast_to(ab_re, bu_re.shape)
    a_im_t = jnp.broadcast_to(ab_im, bu_im.shape)

    def combine(left, right):
        a1r, a1i, b1r, b1i = left
        a2r, a2i, b2r, b2i = right
        return (a1r * a2r - a1i * a2i,
                a1r * a2i + a1i * a2r,
                a2r * b1r - a2i * b1i + b2r,
                a2r * b1i + a2i * b1r + b2i)

    _, _, xs_re, xs_im = lax.associative_scan(combine, (a_re_t, a_im_t, bu_re, bu_im), axis=1)
    y = (jnp.einsum('ghp,blgp->blgh', c_re, xs_re)
         - jnp.einsum('ghp,blgp->blgh', c_im, xs_im)
         + d_skip.reshape(SSM_GROUPS, SSM_GROUP) * ug)
    return y.reshape(bsz, l, SSM_WIDTH)

def causal_depthwise_conv(x, w, b):
    l = x.shape[1]
    xp = jnp.pad(x, ((0, 0), (CONV_WIDTH_2 - 1, 0), (0, 0)))
    y = b
    for k in range(CONV_WIDTH_2):
        y = y + w[k] * xp[:, k:k + l]
    return y

def second_inputs(seed: int = 0) -> dict:
    key = jax.random.key(seed)
    ks = jax.random.split(key, 24)
    f32 = jnp.float32
    nrm = lambda k, shape, s: jax.random.normal(k, shape, f32) * s
    x = jax.random.normal(ks[0], (BATCH, SEQ, D_MODEL), f32)
    attn_norm_g = 1.0 + nrm(ks[1], (DEPTH, D_MODEL), 0.02)
    w_in = nrm(ks[2], (DEPTH, D_MODEL, IN_COLS), D_MODEL ** -0.5)
    b_in = nrm(ks[3], (DEPTH, IN_COLS), 0.02)
    attn_sinks = nrm(ks[4], (DEPTH, N_Q_HEADS), 0.5)
    ssm_a_re = -0.5 + nrm(ks[5], (DEPTH, SSM_GROUPS, SSM_STATE), 0.01)
    ssm_a_im = (jnp.pi * jnp.arange(SSM_STATE, dtype=f32))[None, None, :] + nrm(ks[6], (DEPTH, SSM_GROUPS, SSM_STATE), 0.01)
    ssm_log_dt = jax.random.uniform(ks[7], (DEPTH, SSM_GROUPS), f32, minval=math.log(DT_MIN), maxval=math.log(DT_MAX))
    ssm_b_re = nrm(ks[8], (DEPTH, SSM_GROUPS, SSM_STATE, SSM_GROUP), (2 * SSM_GROUP) ** -0.5)
    ssm_b_im = nrm(ks[9], (DEPTH, SSM_GROUPS, SSM_STATE, SSM_GROUP), (2 * SSM_GROUP) ** -0.5)
    ssm_c_re = nrm(ks[10], (DEPTH, SSM_GROUPS, SSM_GROUP, SSM_STATE), (2 * SSM_STATE) ** -0.5)
    ssm_c_im = nrm(ks[11], (DEPTH, SSM_GROUPS, SSM_GROUP, SSM_STATE), (2 * SSM_STATE) ** -0.5)
    ssm_d = nrm(ks[12], (DEPTH, SSM_WIDTH), 1.0)
    w_glu = nrm(ks[13], (DEPTH, SSM_WIDTH, 2 * SSM_WIDTH), SSM_WIDTH ** -0.5)
    b_glu = nrm(ks[14], (DEPTH, 2 * SSM_WIDTH), 0.02)
    w_branch_attn = nrm(ks[15], (DEPTH, ATTN_WIDTH_2, D_MODEL), ATTN_WIDTH_2 ** -0.5)
    w_branch_ssm = nrm(ks[16], (DEPTH, SSM_WIDTH, D_MODEL), SSM_WIDTH ** -0.5)
    w_out = nrm(ks[17], (DEPTH, D_MODEL, D_MODEL), D_MODEL ** -0.5)
    ffn_norm_g = 1.0 + nrm(ks[18], (DEPTH, D_MODEL), 0.02)
    w_up = nrm(ks[19], (DEPTH, D_MODEL, 2 * D_FF_2), D_MODEL ** -0.5)
    conv_w = nrm(ks[20], (DEPTH, CONV_WIDTH_2, D_FF_2), CONV_WIDTH_2 ** -0.5)
    conv_b = nrm(ks[21], (DEPTH, D_FF_2), 0.02)
    w_down = nrm(ks[22], (DEPTH, D_FF_2, D_MODEL), D_FF_2 ** -0.5)
    final_norm_g = 1.0 + nrm(ks[23], (D_MODEL,), 0.02)
    return {"x": x, "attn_norm_g": attn_norm_g, "w_in": w_in, "b_in": b_in, "attn_sinks": attn_sinks,
            "ssm_a_re": ssm_a_re, "ssm_a_im": ssm_a_im, "ssm_log_dt": ssm_log_dt,
            "ssm_b_re": ssm_b_re, "ssm_b_im": ssm_b_im, "ssm_c_re": ssm_c_re, "ssm_c_im": ssm_c_im,
            "ssm_d": ssm_d, "w_glu": w_glu, "b_glu": b_glu, "w_branch_attn": w_branch_attn,
            "w_branch_ssm": w_branch_ssm, "w_out": w_out, "ffn_norm_g": ffn_norm_g, "w_up": w_up,
            "conv_w": conv_w, "conv_b": conv_b, "w_down": w_down, "final_norm_g": final_norm_g}

def second_block(x, attn_norm_g, w_in, b_in, attn_sinks, ssm_a_re, ssm_a_im, ssm_log_dt, ssm_b_re, ssm_b_im,
              ssm_c_re, ssm_c_im, ssm_d, w_glu, b_glu, w_branch_attn, w_branch_ssm, w_out, ffn_norm_g,
              w_up, conv_w, conv_b, w_down, final_norm_g):
    bsz, seq = x.shape[0], x.shape[1]
    for i in range(DEPTH):
        h = rms_norm_2(x, attn_norm_g[i])
        proj = h @ w_in[i] + b_in[i]
        q, k, v, u, gate_attn, gate_ssm = jnp.split(proj, SPLIT_POINTS, axis=-1)
        q = q.reshape(bsz, seq, N_Q_HEADS, HEAD_DIM)
        k = k.reshape(bsz, seq, N_KV_HEADS, HEAD_DIM)
        v = v.reshape(bsz, seq, N_KV_HEADS, HEAD_DIM)
        attn = sliding_window_attention(q, k, v, attn_sinks[i])
        y = s5_ssm(u, ssm_a_re[i], ssm_a_im[i], ssm_log_dt[i], ssm_b_re[i], ssm_b_im[i],
                   ssm_c_re[i], ssm_c_im[i], ssm_d[i])
        y_val, y_gate = jnp.split(jax.nn.gelu(y, approximate=False) @ w_glu[i] + b_glu[i], 2, axis=-1)
        ssm = y_val * jax.nn.sigmoid(y_gate)
        merged = (jax.nn.sigmoid(gate_attn) * (attn @ w_branch_attn[i])
                  + jax.nn.sigmoid(gate_ssm) * (ssm @ w_branch_ssm[i]))
        x = x + merged @ w_out[i]
        h = rms_norm_2(x, ffn_norm_g[i])
        val, gate = jnp.split(h @ w_up[i], 2, axis=-1)
        gate = causal_depthwise_conv(gate, conv_w[i], conv_b[i])
        x = x + (val * jax.nn.gelu(gate, approximate=False)) @ w_down[i]
    return rms_norm_2(x, final_norm_g)


def setup_inputs(seed=0):
    out = dict(first_inputs(seed))
    for name, value in second_inputs(seed + 1).items():
        if name != "x":
            out[name + "_2"] = value
    return out


def reference(
    x, norm1_w, w_in, gla_w_up, gla_b, gla_norm_w, conv_w, w_br_attn, w_br_gla, w_br_conv,
    w_out, norm2_w, w_ffn_gate, w_ffn_up, w_ffn_down, final_norm_w, attn_norm_g_2, w_in_2,
    b_in_2, attn_sinks_2, ssm_a_re_2, ssm_a_im_2, ssm_log_dt_2, ssm_b_re_2, ssm_b_im_2,
    ssm_c_re_2, ssm_c_im_2, ssm_d_2, w_glu_2, b_glu_2, w_branch_attn_2, w_branch_ssm_2, w_out_2,
    ffn_norm_g_2, w_up_2, conv_w_2, conv_b_2, w_down_2, final_norm_g_2,
):
    x = first_block(
        x, norm1_w, w_in, gla_w_up, gla_b, gla_norm_w, conv_w, w_br_attn, w_br_gla, w_br_conv,
        w_out, norm2_w, w_ffn_gate, w_ffn_up, w_ffn_down, final_norm_w,
    )
    return second_block(
        x, attn_norm_g_2, w_in_2, b_in_2, attn_sinks_2, ssm_a_re_2, ssm_a_im_2, ssm_log_dt_2,
        ssm_b_re_2, ssm_b_im_2, ssm_c_re_2, ssm_c_im_2, ssm_d_2, w_glu_2, b_glu_2,
        w_branch_attn_2, w_branch_ssm_2, w_out_2, ffn_norm_g_2, w_up_2, conv_w_2, conv_b_2,
        w_down_2, final_norm_g_2,
    )


_drawn_inputs = setup_inputs


def setup_inputs(seed=0):
    import zlib

    import numpy as np

    out = dict(_drawn_inputs(seed))
    spreads = {}
    factors = {'gla_b': 8.0,
     'gla_norm_w': 7.721,
     'norm2_w': 3.88,
     'attn_norm_g_2': 7.241,
     'b_in_2': 4.37,
     'attn_sinks_2': 21.823,
     'ssm_a_re_2': 64.0,
     'ssm_a_im_2': 35.216,
     'ssm_log_dt_2': 36.624,
     'ssm_b_re_2': 50.728,
     'ssm_b_im_2': 49.648,
     'ssm_c_re_2': 48.592,
     'ssm_c_im_2': 48.968,
     'b_glu_2': 8.0,
     'ffn_norm_g_2': 3.6,
     'conv_b_2': 5.374,
     'final_norm_g_2': 7.742}
    for name, (base, spread) in spreads.items():
        noise = np.random.default_rng([zlib.crc32(name.encode()), seed]).standard_normal(out[name].shape)
        drawn = base * np.exp(spread * noise) if base else spread * noise
        out[name] = __import__('jax').numpy.asarray(drawn.astype(out[name].dtype))
    for name, factor in factors.items():
        out[name] = (out[name] * factor).astype(out[name].dtype)
    return out
```

```python
from contextlib import ExitStack

import numpy as np

import concourse.bass as bass
from concourse import mybir

F32 = mybir.dt.float32
F32R = mybir.dt.float32r
U32 = mybir.dt.uint32
ALU = mybir.AluOpType
ACT = mybir.ActivationFunctionType
AX = mybir.AxisListType.X
ds = bass.ds

P = 128
S = 256
TT = S // P
D = 2048
KD = D // P
EPS = 1e-6
NEVER = 1e30
HEADS, DH = 8, 128
GH, GK, GV, RANK, CHUNK, TAU = 4, 128, 256, 16, 64, 16.0
BW = 1024
FF = 5632
KF = FF // P
COL_QKV, COL_GLA, COL_AD = 0, 3072, 6144
COL_BCU = COL_AD + RANK
COL_MERGE = COL_BCU + 3 * BW
HEADS2, DH2, KVH2, WINDOW2 = 16, 64, 2, 128
NG, GROUP, STATE = 32, 16, 64
ST = NG * STATE // P
SSMW = NG * GROUP
QKVU2 = HEADS2 * DH2 + 2 * KVH2 * DH2 + SSMW
BLK = 16
NB = S // BLK
PANEL = 512
CK = 4
SLOTS = 4
AHEAD = 3
PIECES = 4
TWO_PI = 2.0 * np.pi


class Token:

    def __init__(self, counter, n, loop):
        self.counter, self.n, self.loop = counter, n, loop


class Counter:

    def __init__(self, sem, step=1):
        self.sem, self.step, self.n, self.loop = sem, step, 0, None

    def __call__(self, inst):
        inst.then_inc(self.sem, self.step)
        self.n += self.step
        return Token(self, self.n, self.loop)

    def at(self, n):
        return Token(self, n, self.loop)


class Loop:

    def __init__(self, index, turns, per):
        self.index, self.turns, self.per = index, turns, per


def wait(eng, *tokens):
    for t in tokens:
        if t is None:
            continue
        if t.loop is None:
            value = t.n
        elif t.counter.loop is t.loop:
            value = t.loop.index * t.loop.per[t.counter] + t.n
        else:
            value = (t.loop.turns - 1) * t.loop.per[t.counter] + t.n
        eng.wait_ge(t.counter.sem, value)


class Kernel:
    def __init__(self, nc, ctx, t, out):
        self.nc, self.ctx, self.t, self.out = nc, ctx, t, out
        self.sp, self.pe, self.act, self.dve, self.pool = nc.sync, nc.tensor, nc.scalar, nc.vector, nc.gpsimd
        sem = lambda name: ctx.enter_context(nc.semaphore(name))
        self.tick = sem("loads_started")
        self.loaded = [Counter(sem(f"loaded{i}"), 16) for i in range(4)]
        self.hi = Counter(sem("hi_split"))
        self.lo = Counter(sem("lo_split"))
        self.mm = Counter(sem("chunk_multiplied"))
        self.ev = [Counter(sem(f"evacuated{i}")) for i in range(TT)]
        self.cpe = Counter(sem("tensor_step"))
        self.cact = Counter(sem("scalar_step"))
        self.cdve = Counter(sem("vector_step"))
        self.cpool = Counter(sem("pool_step"))
        self.cdma = [Counter(sem(f"param_load{i}"), 16) for i in range(8)]
        self.ndma = 0
        self.counters = self.loaded + [self.hi, self.lo, self.mm] + self.ev + [
            self.cpe, self.cact, self.cdve, self.cpool]
        self.g = 0
        self.gs = 0
        self.background = []
        self.panel = 0
        self.loop = None
        self.base = (nc.sbuf_base + 63) // 64 * 64
        self.side_free = [[] for _ in range(4)]
        self.memory()

    def sb(self, name, shape, offset, dtype=F32):
        return self.nc.alloc_sbuf_tensor_at(name, shape, dtype, offset=self.base + offset)

    def memory(self):
        K = 1024
        sb = self.sb
        self.RAW = sb("weights", [P, 4, CK * PANEL], 0)
        self.HI = sb("weights_hi", [P, PIECES, 2 * PANEL], 32 * K, F32R)
        self.LO = sb("weights_lo", [P, PIECES, 2 * PANEL], 48 * K, F32R)
        self.X = sb("x", [P, TT, D], 64 * K)
        off = 80 * K

        def small(name, shape, dtype=F32):
            nonlocal off
            t = sb(name, shape, off, dtype)
            off += (int(np.prod(shape[1:])) * 4 + 31) // 32 * 32
            return t

        self.IDENT = small("identity", [P, P])
        self.U = small("cumsum_in_chunk", [P, P])
        self.LS = small("suffix_in_chunk", [P, P])
        self.DIST = small("distance", [P, 3 * P])
        self.DIST2 = small("distance_in_window", [P, 3 * P])
        self.V1 = small("vectors1", [P, 90])
        self.V2 = small("vectors2", [P, 4 * KF])
        self.V3 = small("vectors3", [P, 66])
        self.SS = small("square_sums", [P, 2])
        self.MS = small("mean_squares", [P, 2])
        self.RSTD = small("rstd", [P, 2])
        self.NHALF = small("minus_half", [P, 2])
        self.AD = small("a_down", [P, TT, RANK])
        self.RMAX = small("row_max", [P, 2, 2])
        self.RSUM = small("row_sum", [P, 2, 2])
        self.RINV = small("row_inverse", [P, 2, 2])
        self.SINK = small("sinks", [P, HEADS2])
        self.NM = small("minus_max", [P, 2, 2])
        self.ESINK = small("exp_sink", [P, 2, 2])
        assert off <= 88 * K, off
        self.AA = A = 88 * K
        self.XH = sb("xT_hi", [P, KD, S], A, F32R)
        self.XL = sb("xT_lo", [P, KD, S], A + 16 * K, F32R)
        R = A + 32 * K
        self.H = sb("normed", [P, TT, D], R + 64 * K)
        self.TOK = sb("projected", [P, TT, 3 * BW], R)
        self.QT = sb("qT", [P, HEADS, S], R + 24 * K)
        self.KT = sb("kT", [P, HEADS, S], R + 32 * K)
        self.YH = sb("convT_hi", [P, 8, S], R + 40 * K, F32R)
        self.YL = sb("convT_lo", [P, 8, S], R + 48 * K, F32R)
        self.OH = sb("attnT_hi", [P, 8, S], R + 56 * K, F32R)
        self.OL = sb("attnT_lo", [P, 8, S], R + 64 * K, F32R)
        self.GHI = sb("glaT_hi", [P, 8, S], R + 24 * K, F32R)
        self.GLO = sb("glaT_lo", [P, 8, S], R + 32 * K, F32R)
        self.MIX = sb("mixed", [P, TT, D], R + 72 * K)
        T = R + 72 * K
        self.WAD = sb("w_a_down", [P, KD, RANK], T)
        self.WADH = sb("w_a_down_hi", [P, KD, RANK], T + K, F32R)
        self.WADL = sb("w_a_down_lo", [P, KD, RANK], T + 2 * K, F32R)
        self.BT = sb("b_gateT", [P, 2, S], T)
        self.CUT = sb("cuT", [P, 2, S], T + 2 * K)
        self.CACC = sb("conv_acc", [P, 2, S], T + 4 * K)
        self.PR = sb("probabilities", [P, 2, 3 * P], T)
        self.PT = sb("probabilitiesT", [P, 2, 3 * P], T + 3 * K)
        self.LA = sb("log_a", [P, TT, 512], T)
        self.KDEC = sb("k_decayed", [P, TT, 512], T + 4 * K)
        self.GB = sb("gla_b_rows", [P, 512], T + 8 * K)
        self.ADT = sb("a_downT", [RANK, S], T + 10 * K)
        self.WUP = sb("gla_w_up", [RANK, 512], T + 11 * K)
        self.EB = sb("exp_b", [P, S], T + 8 * K)
        self.EN = sb("exp_minus_b", [P, S], T + 9 * K)
        self.QIN = sb("q_in", [P, S], T + 10 * K)
        self.KIN = sb("k_in", [P, S], T + 11 * K)
        self.AT = sb("aT", [P, TT, P], T + 13 * K)
        self.ST = sb("gla_state", [P, 3, 256], T + 14 * K)
        self.HH = sb("hiddenT_hi", [P, KF, S], R, F32R)
        self.HL = sb("hiddenT_lo", [P, KF, S], R + 44 * K, F32R)
        self.CG = sb("conv_gelu", [P, 2, S], R + 96 * K)
        self.FW = sb("final_norm_rows", [P, D], R)
        self.TOK2 = sb("projected2", [P, TT, QKVU2], R)
        self.QT2 = sb("qT2", [P, 8, S], R + 14 * K)
        self.KT2 = sb("kT2", [P, KVH2, S], R + 22 * K)
        self.KDUP = sb("k_twice", [P, TT, KVH2 * P], R + 24 * K)
        self.VB = sb("v_bias_rows", [P, KVH2 * DH2], R + 26 * K)
        self.PR2 = sb("probabilities2", [P, 2, 3 * P], R + 27 * K)
        self.PT2 = sb("probabilitiesT2", [P, 2, 3 * P], R + 30 * K)
        self.OH2 = sb("attn2T_hi", [P, 8, S], R + 72 * K, F32R)
        self.OL2 = sb("attn2T_lo", [P, 8, S], R + 80 * K, F32R)
        self.UT = sb("uT", [P, 4, S], R + 33 * K)
        self.XS = sb("ssm_states", [P, 2, ST, S], R + 37 * K)
        self.BRE = sb("b_re", [P, ST, GROUP], R + 14 * K)
        self.BIM = sb("b_im", [P, ST, GROUP], R + 15 * K)
        self.BBR = sb("bb_re", [P, ST, 2 * GROUP], R + 16 * K)
        self.BBI = sb("bb_im", [P, ST, 2 * GROUP], R + 18 * K)
        self.BTR = sb("bbT_re", [P, 4, P], R + 20 * K)
        self.BTI = sb("bbT_im", [P, 4, P], R + 22 * K)
        self.CRE = sb("c_twice", [P, 2, 4, P], R + 24 * K)
        self.CTR = sb("cT_re", [P, ST, 2 * GROUP], R + 28 * K)
        self.CTI = sb("cT_im", [P, ST, 2 * GROUP], R + 30 * K)
        self.SV = sb("ssm_vectors", [P, 32, ST], R + 69 * K)
        self.SROW = sb("log_dt_rows", [ST, P], R + 32 * K)
        self.LDT = sb("log_dt", [ST, 2], R + 32 * K + 512)
        self.SCR = sb("ssm_scratch", [P, 3600], R)
        self.POW = sb("a_powers", [P, 2, ST, BLK], R + 16 * K)
        self.STEP = sb("scan_step", [P, 2, ST, NB], R + 20 * K)
        self.GE = sb("ssm_gelu", [P, 4, S], R + 14 * K)
        self.GEH = sb("ssm_geluT_hi", [P, 4, S], R + 18 * K, F32R)
        self.GEL = sb("ssm_geluT_lo", [P, 4, S], R + 22 * K, F32R)
        self.GLU = sb("glu", [P, TT, 2 * SSMW], R)
        self.GBR = sb("b_glu_rows", [P, 2 * SSMW], R + 8 * K)
        self.SH = sb("ssmT_hi", [P, 4, S], R + 26 * K, F32R)
        self.SL = sb("ssmT_lo", [P, 4, S], R + 30 * K, F32R)
        self.MG = sb("merged", [P, TT, D], R + 34 * K)
        self.GROW = sb("gate_bias_rows", [P, 2 * D], R + 50 * K)
        self.SIG = sb("gates", [P, TT, 2, PANEL], R + 88 * K)
        self.FF1 = sb("ffn_gate", [P, TT, PANEL], R + 88 * K)
        self.FF2 = sb("ffn_hidden", [P, TT, PANEL], R + 92 * K)
        psum = lambda n: self.ctx.enter_context(self.nc.psum_tensor(n, [P, 4, PANEL], F32))
        self.ACC, self.SIDE = psum("panels"), psum("side")
        self.R = R

    def repeat(self, turns, body, per):
        per = {c: per.get(c, 0) for c in self.counters}
        start = {c: c.n for c in self.counters}
        nc = self.nc
        with nc.Fori(0, turns, engines=[e.engine for e in (self.act, self.pe, self.dve, self.sp)]) as i:
            loop = self.loop = Loop(i, turns, per)
            for c in self.counters:
                c.loop = loop
            for b in range(4):
                self.side_free[b] = [self.cact.at(self.cact.n), self.cdve.at(self.cdve.n)]
            self.before = [c.at(c.n) for c in (self.cpe, self.cact, self.cdve)]
            body(i)
        self.loop = None
        for c in self.counters:
            grown = c.n - start[c]
            assert grown == per[c], (c.sem, grown, per[c])
            c.loop = None
            c.n = start[c] + turns * grown
        chunks = per[self.mm]
        for b in range(4):
            self.side_free[b] = [self.cact.at(self.cact.n), self.cdve.at(self.cdve.n)]
        self.g += (turns - 1) * chunks
        self.gs += (turns - 1) * chunks
        self.panel += (turns - 1) * per[self.ev[0]]

    def per(self, chunks, panels, **more):
        p = {c: 16 * chunks // 4 for c in self.loaded}
        p.update({self.hi: 2 * chunks, self.lo: 2 * chunks, self.mm: 2 * chunks, self.ev[0]: panels, self.ev[1]: panels})
        p.update({{"cpe": self.cpe, "cact": self.cact, "cdve": self.cdve}[k]: v for k, v in more.items()})
        return p

    def load_chunk(self, w, k0, nk, col, width):
        g = self.g // 2
        slot = g % SLOTS
        wait(self.sp, self.lo.at(2 * g + 2))
        self.sp.sem_inc(self.tick, 1)
        src = w[k0 * P:(k0 + nk) * P, ds(col, width)].rearrange("(k p) n -> p k n", p=P)
        dst = self.RAW[:, slot, :].rearrange("p (k n) -> p k n", n=PANEL)
        dst = dst[:, 0:CK:2, 0:width] if nk == 2 else dst[:, 0:nk, 0:width]
        self.loaded[slot](self.sp.dma_start(dst, src))

    def split_piece(self):
        g = self.gs
        slot, part, ring = g // 2 % SLOTS, g % 2, g % PIECES
        raw = self.RAW[:, slot, part * 2 * PANEL:(part + 1) * 2 * PANEL]
        if part == 0:
            wait(self.act, self.loaded[slot].at(16 * (g // 2 // SLOTS + 1)))
        if g >= PIECES or self.loop:
            wait(self.act, self.mm.at(g + 1))
        self.hi(self.act.activation(self.HI[:, ring, :], raw, ACT.Copy))
        wait(self.dve, self.hi.at(g + 1))
        self.lo(self.dve.tensor_tensor(self.LO[:, ring, :], raw, self.HI[:, ring, :].bitcast(F32), ALU.subtract))
        self.gs += 1

    def product(self, w, col, width, stat, chunks, evacuate, last=False, side=None):
        p = self.panel
        hi, lo = stat
        k0 = 0
        total = sum(chunks)
        for c, nk in enumerate(chunks):
            self.load_chunk(w, k0, nk, col, width)
            for part, np_ in enumerate(((nk + 1) // 2, nk // 2)):
                g, ring = self.g, self.g % PIECES
                self.g += 1
                if not last or 2 * c + part + AHEAD < 2 * len(chunks):
                    self.split_piece()
                wait(self.pe, self.lo.at(g + 1 + 2 * SLOTS))
                for t in range(TT):
                    if k0 == 0:
                        wait(self.pe, self.ev[t].at(p + 1))
                    acc = self.ACC[:, (p % 2) * TT + t, 0:width]
                    for k in range(np_):
                        a, b = (x[:, k0 + k, t * P:(t + 1) * P] for x in (hi, lo))
                        wh, wl = (x[:, ring, k * PANEL:k * PANEL + width] for x in (self.HI, self.LO))
                        first, final = k0 + k == 0, k0 + k == total - 1
                        self.pe.matmul(acc, a, wh, start=first, stop=False)
                        self.pe.matmul(acc, a, wl, start=False, stop=False)
                        inst = self.pe.matmul(acc, b, wh, start=False, stop=final)
                done = self.mm(inst)
                k0 += np_
                if side and 2 * c + part in side:
                    side[2 * c + part]()
                if self.loop is None and self.background:
                    if next(self.background[0], self) is self:
                        self.background.pop(0)
        self.panel += 1
        for t in range(TT):
            evacuate(t, self.ACC[:, (p % 2) * TT + t, 0:width], done)

    def finish_background(self):
        for work in self.background:
            for _ in work:
                pass
        self.background = []

    def bank(self, b):
        wait(self.pe, *self.side_free[b])
        self.side_free[b] = []
        return self.SIDE[:, b, :]

    def release(self, b, *tokens):
        self.side_free[b] = list(tokens)

    def param(self, dst, src):
        c = self.cdma[self.ndma % len(self.cdma)]
        self.ndma += 1
        if c.n:
            wait(self.act, c.at(c.n))
        return c(self.act.dma_start(dst, src))

    def tr(self, out, in_):
        return self.pe.transpose(out, in_, self.IDENT[0:in_.shape[0], 0:in_.shape[0]])

    def feature_major(self, src, nk, hi, lo, ready, weights=None, at=0):
        wait(self.pe, *ready)
        last = None
        for kp in range(nk // 2):
            b = kp % 4
            ps = self.bank(b)
            for k in range(2):
                for t in range(TT):
                    inst = self.tr(ps[:, k * S + t * P:k * S + (t + 1) * P], src(2 * kp + k, t))
            done = self.cpe(inst)
            wait(self.act, done)
            if weights is None:
                a = self.cact(self.act.activation(hi[:, ds(at + 2 * kp, 2), :], ps[:, :], ACT.Copy))
                wait(self.dve, a)
                last = self.cdve(self.dve.tensor_tensor(lo[:, ds(at + 2 * kp, 2), :], ps[:, :],
                                                        hi[:, ds(at + 2 * kp, 2), :].bitcast(F32), ALU.subtract))
            else:
                for k in range(2):
                    w = weights(2 * kp + k)
                    a = self.cact(self.act.activation(hi[:, 2 * kp + k, :], ps[:, k * S:(k + 1) * S],
                                                      ACT.Copy, scale=w))
                for k in range(2):
                    w = weights(2 * kp + k)
                    wait(self.dve, a)
                    last = self.cdve(self.dve.scalar_tensor_tensor(
                        out=lo[:, 2 * kp + k, :], in0=ps[:, k * S:(k + 1) * S], scalar=w,
                        in1=hi[:, 2 * kp + k, :].bitcast(F32), op0=ALU.mult, op1=ALU.subtract))
            self.release(b, last)
        return last

    def constants(self):
        pool = self.pool

        def c(inst):
            tok = self.cpool(inst)
            wait(pool, tok)
            return tok

        c(pool.memset(self.IDENT[:, :], 0.0))
        c(pool.memset(self.U[:, :], 1.0 / TAU))
        c(pool.memset(self.LS[:, :], 1.0 / TAU))
        c(pool.memset(self.NHALF[:, :], -0.5))
        c(pool.iota(self.DIST[:, 0:P], [[-1, P]], base=0, channel_multiplier=1, allow_small_or_imprecise_dtypes=True))
        c(pool.iota(self.DIST[:, P:3 * P], [[-1, S]], base=P, channel_multiplier=1,
                    allow_small_or_imprecise_dtypes=True))

        def select(m, pattern, base, cm, op, fill, like=None):
            return c(pool.affine_select(out=m, in_=m if like is None else like, compare_op=op, fill=fill,
                                        base=base, pattern=pattern, channel_multiplier=cm))

        select(self.IDENT[:, :], [[-1, P]], 0, 1, ALU.not_equal, 1.0)
        select(self.U[:, :], [[1, P]], 0, -1, ALU.is_ge, 0.0)
        select(self.LS[:, :], [[-1, P]], 0, 1, ALU.is_gt, 0.0)
        select(self.DIST[:, 0:P], [[-1, P]], 0, 1, ALU.is_ge, NEVER)
        select(self.DIST[:, P:3 * P], [[-1, S]], P, 1, ALU.is_ge, NEVER)
        select(self.U[0:64, 64:P], [[0, 64]], -1, 0, ALU.is_ge, 0.0)
        select(self.LS[64:P, 0:64], [[0, 64]], -1, 0, ALU.is_ge, 0.0)
        c(pool.tensor_copy(self.DIST2[:, 0:P], self.DIST[:, 0:P]))
        return select(self.DIST2[:, P:3 * P], [[1, S]], WINDOW2 - 1 - P, -1, ALU.is_ge, NEVER,
                      like=self.DIST[:, P:3 * P])

    def vectors(self):
        t = self.t
        R = self.R
        rows = [self.sb(f"rows{i}", [P, P], R + 512 * i) for i in range(4)]
        loads = [[], [], [], []]
        put = lambda i, at, n, src: loads[i].append(self.param(rows[i][at:at + n, :], src))
        vec = lambda x: x.rearrange("(k p) -> k p", p=P)
        at = 0
        for n in ("norm1_w", "norm2_w", "attn_norm_g_2", "ffn_norm_g_2"):
            put(0, at, KD, vec(t[n][0]))
            at += KD
        put(0, at, 2, vec(t["gla_norm_w"][0]))
        put(0, at + 2, 24, t["conv_w"][0].rearrange("j (k p) -> (j k) p", p=P))
        cw = t["conv_w_2"][0].rearrange("j (k p) -> (j k) p", p=P)
        put(1, 0, 88, cw[0:88, :])
        put(2, 0, 44, cw[88:132, :])
        put(2, 44, 44, vec(t["conv_b_2"][0]))
        put(3, 0, 14, t["b_in_2"][0, 0:QKVU2].rearrange("(k p) -> k p", p=P))
        put(3, 14, 4, vec(t["ssm_d_2"][0]))
        put(3, 18, ST, t["ssm_a_re_2"][0].rearrange("(s q) p -> s (q p)", q=2))
        put(3, 34, ST, t["ssm_a_im_2"][0].rearrange("(s q) p -> s (q p)", q=2))
        for i, (dst, n) in enumerate(((self.V1[:, :], 90), (self.V2[:, 0:88], 88), (self.V2[:, 88:176], 88),
                                      (self.V3[:, 0:50], 50))):
            wait(self.pe, *loads[i], self.const_ready)
            ps = self.bank(i)
            done = self.cpe(self.tr(ps[:, 0:n], rows[i][0:n, :]))
            wait(self.act, done)
            self.vec_ready = self.cact(self.act.activation(dst, ps[:, 0:n], ACT.Copy))
            self.release(i, self.vec_ready)
        wait(self.dve, self.vec_ready)

    def rstd(self, x_ready, out):
        junk = self.H
        wait(self.act, *x_ready)
        for t in range(TT):
            a = self.cact(self.act.activation(junk[:, t, :], self.X[:, t, :], ACT.Square,
                                              accum_out=self.SS[:, t:t + 1]))
        return self.power(a, self.SS[:, 0:2], 1.0 / D, out)

    def power(self, ready, sums, scale, out):
        wait(self.dve, ready)
        d = self.cdve(self.dve.tensor_scalar(self.MS[:, 0:2], sums, scale, EPS, ALU.mult, ALU.add))
        wait(self.pool, d)
        return self.cpool(self.pool.tensor_tensor(out, self.MS[:, 0:2], self.NHALF[:, 0:2], ALU.pow))

    def norm_to_T(self, x_ready, w0):
        r = self.rstd(x_ready, self.RSTD[:, 0:2])
        wait(self.dve, r)
        for t in range(TT):
            h = self.cdve(self.dve.tensor_scalar(self.H[:, t, :], self.X[:, t, :], self.RSTD[:, t:t + 1], None,
                                                 ALU.mult))
        last = self.feature_major(lambda k, t: self.H[:, t, k * P:(k + 1) * P], KD, self.XH, self.XL, [h],
                                  weights=lambda k: self.V1[:, w0 + k:w0 + k + 1])
        wait(self.pe, last)

    def project(self, w, col0, width, panels, dst):

        def body(i):
            for p in range(2):
                def evacuate(t, acc, done, p=p):
                    o = dst[:, t, ds(i * 2 * width + p * width, width)]
                    if t == 0:
                        wait(self.act, done)
                        self.ev[0](self.act.activation(o, acc, ACT.Copy))
                    else:
                        wait(self.dve, done)
                        self.ev[1](self.dve.tensor_copy(o, acc))
                self.product(w, i * 2 * width + (col0 + p * width), width, (self.XH, self.XL), [CK] * 4, evacuate)
        self.repeat(panels // 2, body, self.per(8, 2))
        return self.ev[0].at(self.ev[0].n), self.ev[1].at(self.ev[1].n)

    def a_down(self):
        w = self.t["w_in"][0][:, COL_AD:COL_AD + RANK].rearrange("(k p) n -> p k n", p=P)
        d = self.param(self.WAD[:, :, :], w)
        wait(self.act, d)
        a = self.cact(self.act.activation(self.WADH[:, :, :], self.WAD[:, :, :], ACT.Copy))
        wait(self.dve, a)
        v = self.cdve(self.dve.tensor_tensor(self.WADL[:, :, :], self.WAD[:, :, :],
                                             self.WADH[:, :, :].bitcast(F32), ALU.subtract))
        wait(self.pe, v)
        for t in range(TT):
            ps = self.bank(t)[:, 0:RANK]
            for k in range(KD):
                a_, b_ = (x[:, k, t * P:(t + 1) * P] for x in (self.XH, self.XL))
                self.pe.matmul(ps, a_, self.WADH[:, k, :], start=k == 0, stop=False)
                self.pe.matmul(ps, a_, self.WADL[:, k, :], start=False, stop=False)
                inst = self.pe.matmul(ps, b_, self.WADH[:, k, :], start=False, stop=k == KD - 1)
            done = self.cpe(inst)
            wait(self.act, done)
            self.release(t, self.cact(self.act.activation(self.AD[:, t, :], ps, ACT.Copy)))

    def conv_branch(self, ready):
        TOK, dve = self.TOK, self.dve
        wait(dve, *ready)
        for t in range(TT):
            cu = self.cdve(dve.tensor_tensor(TOK[:, t, BW:2 * BW], TOK[:, t, BW:2 * BW],
                                             TOK[:, t, 2 * BW:3 * BW], ALU.mult))
        wait(self.pe, *ready, cu)
        free = None
        for kp in range(4):
            b0, b1 = self.bank((2 * kp) % 4), self.bank((2 * kp + 1) % 4)
            for k in range(2):
                for t in range(TT):
                    o = slice(k * S + t * P, k * S + (t + 1) * P)
                    f = (2 * kp + k) * P
                    self.tr(b0[:, o], TOK[:, t, BW + f:BW + f + P])
                    inst = self.tr(b1[:, o], TOK[:, t, f:f + P])
            done = self.cpe(inst)
            wait(self.act, done, free)
            bt = self.cact(self.act.activation(self.BT[:, :, :], b1, ACT.Copy))
            wait(dve, done)
            tap = lambda j, k: self.V1[:, 66 + j * 8 + 2 * kp + k:67 + j * 8 + 2 * kp + k]
            acc = self.CACC
            for k in range(2):
                v = self.cdve(dve.tensor_scalar(acc[:, k, :], b0[:, k * S:(k + 1) * S], tap(2, k), None, ALU.mult))
            for j in (1, 0):
                s = 2 - j
                wait(dve, v)
                for k in range(2):
                    v = self.cdve(dve.scalar_tensor_tensor(
                        out=acc[:, k, s:S], in0=b0[:, k * S:(k + 1) * S - s], scalar=tap(j, k),
                        in1=acc[:, k, s:S], op0=ALU.mult, op1=ALU.add))
            wait(dve, v, bt)
            y = self.cdve(dve.tensor_tensor(self.CUT[:, :, :], acc[:, :, :], self.BT[:, :, :], ALU.mult))
            self.release((2 * kp) % 4, y)
            self.release((2 * kp + 1) % 4, bt)
            wait(self.act, y)
            a = self.cact(self.act.activation(self.YH[:, 2 * kp:2 * kp + 2, :], self.CUT[:, :, :], ACT.Copy))
            wait(dve, a)
            free = self.cdve(dve.tensor_tensor(self.YL[:, 2 * kp:2 * kp + 2, :], self.CUT[:, :, :],
                                               self.YH[:, 2 * kp:2 * kp + 2, :].bitcast(F32), ALU.subtract))
        return free

    def attention(self, heads, scores, values, out, dist, slope, scale, sink=None, dh=P, ptile=None, ptT=None):
        pe, act, dve = self.pe, self.act, self.dve
        state = {}
        regions = ((slice(0, P), 0), (slice(P, 3 * P), 1))

        def head_scores(h):
            b = h % 2
            ps = self.bank(b)
            q, k = scores(h)
            self.pe.matmul(ps[:, 0:P], q[:, 0:P], k[:, 0:P], start=True, stop=True)
            done = self.cpe(pe.matmul(ps[:, P:3 * P], q[:, P:S], k[:, 0:S], start=True, stop=True))
            pr = ptile[:, b, :]
            wait(dve, done)
            if h >= 2:
                wait(dve, state[h - 2]["transposed"])
            v = self.cdve(dve.scalar_tensor_tensor(out=pr, in0=dist[:, :], scalar=-slope(h) / scale,
                                                   in1=ps[:, 0:3 * P], op0=ALU.mult, op1=ALU.add))
            self.release(b, v)
            wait(dve, v)
            for cols, t in regions:
                m = self.cdve(dve.tensor_reduce(self.RMAX[:, b, t:t + 1], pr[:, cols], AX, ALU.max))
            wait(dve, m)
            if sink is None:
                nm = self.cdve(dve.tensor_scalar(self.NM[:, b, :], self.RMAX[:, b, :], -scale, None, ALU.mult))
            else:
                s = sink[:, h:h + 1]
                mx = self.cdve(dve.tensor_scalar(self.RMAX[:, b, :], self.RMAX[:, b, :], scale, s, ALU.mult, ALU.max))
                wait(dve, mx)
                nm = self.cdve(dve.tensor_scalar(self.NM[:, b, :], self.RMAX[:, b, :], -1.0, None, ALU.mult))
                wait(act, nm)
                es = None
                for t in range(TT):
                    es = self.cact(act.activation(self.ESINK[:, b, t:t + 1], s, ACT.Exp, bias=self.NM[:, b, t:t + 1]))
            wait(act, nm)
            for cols, t in regions:
                e = self.cact(act.activation(pr[:, cols], pr[:, cols], ACT.Exp, bias=self.NM[:, b, t:t + 1],
                                             scale=scale, accum_out=self.RSUM[:, b, t:t + 1]))
            wait(dve, e)
            if sink is not None:
                r = self.cdve(dve.tensor_tensor(self.RSUM[:, b, :], self.RSUM[:, b, :], self.ESINK[:, b, :], ALU.add))
                wait(dve, r)
            r = self.cdve(dve.reciprocal(self.RINV[:, b, :], self.RSUM[:, b, :]))
            wait(dve, r)
            for cols, t in regions:
                n = self.cdve(dve.tensor_scalar(pr[:, cols], pr[:, cols], self.RINV[:, b, t:t + 1], None, ALU.mult))
            state[h] = {"normed": n}

        def head_values(h):
            b = h % 2
            pr, pt = ptile[:, b, :], ptT[:, b, :]
            ps = self.bank(2)
            wait(pe, state[h]["normed"])
            self.tr(ps[:, 0:P], pr[:, 0:P])
            self.tr(ps[:, P:2 * P], pr[:, P:2 * P])
            tr = self.cpe(self.tr(ps[:, 2 * P:3 * P], pr[:, 2 * P:3 * P]))
            state[h]["transposed"] = tr
            wait(act, tr)
            if h >= 2:
                wait(act, state[h - 2]["multiplied"])
            c = self.cact(act.activation(pt, ps[:, 0:3 * P], ACT.Copy))
            self.release(2, c)
            state[h]["copied"] = c

        def head_out(h):
            b = h % 2
            pt = ptT[:, b, :]
            lo_part = slice(0, P) if dh == P else slice(dh * (h % 2), dh * (h % 2) + dh)
            if dh == P or h % 2 == 0:
                self.bank(3)
            o = self.SIDE[lo_part, 3, 0:S]
            wait(pe, state[h]["copied"])
            v0, v1 = values(h)
            self.pe.matmul(o, v0, pt[:, 0:2 * P], start=True, stop=True)
            mu = self.cpe(self.pe.matmul(o[:, P:S], v1, pt[:, 2 * P:3 * P], start=False, stop=True,
                                         skip_group_check=True))
            state[h]["multiplied"] = mu
            if dh != P and h % 2 == 0:
                return None
            tile = h if dh == P else h // 2
            wait(act, mu)
            a = self.cact(act.activation(out[0][:, tile, :], self.SIDE[:, 3, 0:S], ACT.Copy))
            wait(dve, a)
            d = self.cdve(dve.tensor_tensor(out[1][:, tile, :], self.SIDE[:, 3, 0:S],
                                            out[0][:, tile, :].bitcast(F32), ALU.subtract))
            self.release(3, d)
            return d

        head_scores(0)
        for h in range(heads):
            if h + 1 < heads:
                head_scores(h + 1)
            head_values(h)
            last = head_out(h)
        return last

    def transposed(self, src, n, dst, ready, bias=None):
        wait(self.pe, *ready)
        for kp in range(n // 2):
            b = kp % 4
            ps = self.bank(b)
            for k in range(2):
                for t in range(TT):
                    inst = self.tr(ps[:, k * S + t * P:k * S + (t + 1) * P], src(2 * kp + k, t))
            done = self.cpe(inst)
            if bias is None:
                if kp % 2:
                    wait(self.dve, done)
                    last = self.cdve(self.dve.tensor_copy(dst[:, 2 * kp:2 * kp + 2, :], ps))
                else:
                    wait(self.act, done)
                    last = self.cact(self.act.activation(dst[:, 2 * kp:2 * kp + 2, :], ps, ACT.Copy))
            else:
                wait(self.dve, done)
                for k in range(2):
                    last = self.cdve(self.dve.tensor_scalar(dst[:, 2 * kp + k, :], ps[:, k * S:(k + 1) * S],
                                                            bias(2 * kp + k), None, ALU.add))
            self.release(b, last)
        return [self.cact.at(self.cact.n), self.cdve.at(self.cdve.n)]

    def gla(self, ready):
        pe, act, dve, pool, TOK = self.pe, self.act, self.dve, self.pool, self.TOK
        gb = self.param(self.GB[:, :], self.t["gla_b"][0].partition_broadcast(P))
        wu = self.param(self.WUP[:, :], self.t["gla_w_up"][0])
        ps = self.bank(0)
        for t in range(TT):
            inst = self.tr(ps[0:RANK, t * P:(t + 1) * P], self.AD[:, t, :])
        done = self.cpe(inst)
        wait(act, done)
        ad = self.cact(act.activation(self.ADT[:, :], ps[0:RANK, 0:S], ACT.Copy))
        self.release(0, ad)
        wait(pe, ad, wu)
        wait(dve, gb)
        la = []
        for t in range(TT):
            ps = self.bank(1 + t)
            done = self.cpe(pe.matmul(ps, self.ADT[:, t * P:(t + 1) * P], self.WUP[:, :], start=True, stop=True))
            wait(dve, done)
            z = self.cdve(dve.tensor_tensor(self.LA[:, t, :], ps, self.GB[:, :], ALU.add))
            self.release(1 + t, z)
            wait(dve, z)
            a = self.cdve(dve.scalar_tensor_tensor(out=self.KDEC[:, t, :], in0=self.LA[:, t, :], scalar=-1.0,
                                                       in1=self.LA[:, t, :], op0=ALU.mult, op1=ALU.max))
            wait(act, a)
            e = self.cact(act.activation(self.KDEC[:, t, :], self.KDEC[:, t, :], ACT.Exp, scale=-1.0))
            wait(act, e)
            l = self.cact(act.activation(self.KDEC[:, t, :], self.KDEC[:, t, :], ACT.Ln, bias=1.0))
            wait(dve, l)
            la.append(self.cdve(dve.scalar_tensor_tensor(out=self.LA[:, t, :], in0=self.LA[:, t, :], scalar=0.0,
                                                         in1=self.KDEC[:, t, :], op0=ALU.min, op1=ALU.subtract)))
        wait(pe, *la)
        for t in range(TT):
            ps = self.bank(1 + t)
            done = self.cpe(pe.matmul(ps, self.LS[:, :], self.LA[:, t, :], start=True, stop=True))
            wait(act, done, la[t])
            e = self.cact(act.activation(self.KDEC[:, t, :], ps, ACT.Exp))
            self.release(1 + t, e)
            wait(dve, e, *ready)
            kd = self.cdve(dve.tensor_tensor(self.KDEC[:, t, :], self.KDEC[:, t, :], TOK[:, t, 512:1024], ALU.mult))
        wait(act, *ready)
        for t in range(TT):
            sr = self.cact(act.activation(TOK[:, t, 2048:3072], TOK[:, t, 2048:3072], ACT.Silu))
        wait(pe, kd, *ready)
        m0 = self.cdve(dve.memset(self.AT[:, :, :], 0.0))
        wait(dve, m0)
        mask = self.U[:, :].bitcast(U32)
        og = None
        for h in range(GH):
            hk, hv = slice(h * GK, (h + 1) * GK), slice(1024 + h * GV, 1024 + (h + 1) * GV)
            b0, b1 = self.bank(0), self.bank(1)
            for t in range(TT):
                pe.matmul(b0[:, t * P:(t + 1) * P], self.LA[:, t, hk], self.U[:, :], start=True, stop=True)
            bt = self.cpe(self.tr(b1[:, 0:P], TOK[:, 0, hk]))
            self.tr(b1[:, P:S], TOK[:, 1, hk])
            for t in range(TT):
                inst = self.tr(b1[:, S + t * P:S + (t + 1) * P], TOK[:, t, 512 + h * GK:512 + (h + 1) * GK])
            qk = self.cpe(inst)
            wait(act, bt)
            if og is not None:
                wait(act, og)
            eb = self.cact(act.activation(self.EB[:, :], b0[:, 0:S], ACT.Exp))
            en = self.cact(act.activation(self.EN[:, :], b0[:, 0:S], ACT.Exp, scale=-1.0))
            self.release(0, en)
            wait(dve, qk, en)
            if og is not None:
                wait(dve, og)
            qi = self.cdve(dve.scalar_tensor_tensor(out=self.QIN[:, :], in0=b1[:, 0:S], scalar=GK ** -0.5,
                                                    in1=self.EB[:, :], op0=ALU.mult, op1=ALU.mult))
            ki = self.cdve(dve.tensor_tensor(self.KIN[:, :], b1[:, S:2 * S], self.EN[:, :], ALU.mult))
            self.release(1, ki)
            b2 = self.bank(2)
            wait(pe, ki)
            for t in range(TT):
                inst = pe.matmul(b2[:, t * P:(t + 1) * P], self.KIN[:, t * P:(t + 1) * P],
                                 self.QIN[:, t * P:(t + 1) * P], start=True, stop=True)
            sc = self.cpe(inst)
            b0, b1 = self.bank(0), self.bank(1)
            kv = []
            for n in range(3):
                o = (b0[:, 0:256], b1[:, 0:256], b0[:, 256:512])[n]
                r = slice(64 * (n % 2), 64 * (n % 2) + 64)
                kv.append(self.cpe(pe.matmul(o, self.KDEC[r, n // 2, hk], TOK[r, n // 2, hv], start=True, stop=True)))
            wait(dve, sc)
            for t in range(TT):
                at = self.cdve(dve.copy_predicated(self.AT[:, t, :], mask, b2[:, t * P:(t + 1) * P]))
            self.release(2, at)
            wait(dve, kv[2])
            s = self.cdve(dve.tensor_copy(self.ST[:, 0, :], b0[:, 0:256]))
            for n, o in ((1, b1[:, 0:256]), (2, b0[:, 256:512])):
                wait(dve, s, kv[n])
                s = self.cdve(dve.scalar_tensor_tensor(
                    out=self.ST[:, n, :], in0=self.ST[:, n - 1, :], scalar=self.EB[:, 64 * n + 63:64 * n + 64],
                    in1=o, op0=ALU.mult, op1=ALU.add))
            self.release(0, s)
            self.release(1, s)
            b3 = self.bank(3)
            wait(pe, at, s)
            for t in range(TT):
                o = b3[:, t * 256:(t + 1) * 256]
                pe.matmul(o, self.AT[:, t, :], TOK[:, t, hv], start=True, stop=True)
                for n in (2 * t, 2 * t + 1):
                    if n:
                        r = slice(64 * (n % 2), 64 * (n % 2) + 64)
                        inst = pe.matmul(o[r, :], self.QIN[:, 64 * n:64 * n + 64], self.ST[:, n - 1, :],
                                         start=False, stop=True, skip_group_check=True)
            done = self.cpe(inst)
            wait(act, done)
            for t in range(TT):
                q = self.cact(act.activation(self.ST[:, t, :], b3[:, t * 256:(t + 1) * 256], ACT.Square,
                                             accum_out=self.SS[:, t:t + 1]))
            r = self.power(q, self.SS[:, 0:2], 1.0 / GV, self.RSTD[:, 0:2])
            wait(dve, r, sr)
            for t in range(TT):
                og = self.cdve(dve.scalar_tensor_tensor(
                    out=TOK[:, t, hv], in0=b3[:, t * 256:(t + 1) * 256], scalar=self.RSTD[:, t:t + 1],
                    in1=TOK[:, t, 2048 + h * GV:2048 + (h + 1) * GV], op0=ALU.mult, op1=ALU.mult))
            self.release(3, og)
        return self.feature_major(lambda k, t: TOK[:, t, 1024 + k * P:1024 + (k + 1) * P], 8, self.GHI, self.GLO, [og],
                                  weights=lambda k: self.V1[:, 64 + k % 2:65 + k % 2])

    def merge_branch(self, w_gate, gate_col, w_branch, stat, nk, mix, first, rows=None):
        act, dve, SIG = self.act, self.dve, self.SIG
        half = nk // 2

        def body(i):
            base = {}
            for p in range(2):
                col = i * 2 * PANEL + p * PANEL

                def gate(t, acc, done, p=p, col=col):
                    sig = SIG[:, t, p, :]
                    if rows is None:
                        wait(act, done, self.ev[t].at(self.ev[t].n), self.before[2])
                        base[t] = self.ev[t](act.activation(sig, acc, ACT.Sigmoid))
                    else:
                        wait(dve, done)
                        s = self.ev[t](dve.tensor_tensor(sig, acc, rows(col), ALU.add))
                        wait(act, s)
                        base[t] = self.cact(act.activation(sig, sig, ACT.Sigmoid))

                def branch(t, acc, done, p=p, col=col):
                    sig, m = SIG[:, t, p, :], mix[:, t, ds(col, PANEL)]
                    wait(dve, done, base[t])
                    if first:
                        self.ev[t](dve.tensor_tensor(m, acc, sig, ALU.mult))
                    else:
                        v = self.ev[t](dve.tensor_tensor(sig, acc, sig, ALU.mult))
                        wait(dve, v)
                        self.cdve(dve.tensor_tensor(m, m, sig, ALU.add))

                self.product(w_gate, i * 2 * PANEL + (gate_col + p * PANEL), PANEL, (self.XH, self.XL), [CK] * 4, gate)
                self.product(w_branch, col, PANEL, stat, [half] * 2, branch)

        self.repeat(D // PANEL // 2, body, self.per(12, 4, cact=0 if rows is None else 4, cdve=0 if first else 4))

    def residual(self, w, stat, groups, last=False):

        def evacuate(col):
            def f(t, acc, done):
                x = self.X[:, t, ds(col, PANEL)]
                wait(self.dve, done)
                self.ev[t](self.dve.tensor_tensor(x, x, acc, ALU.add))
            return f

        def body(i):
            for p in range(2):
                col = i * 2 * PANEL + p * PANEL
                self.product(w, col, PANEL, stat, groups, evacuate(col))

        n = D // PANEL // 2
        self.repeat(n - 1 if last else n, body, self.per(2 * len(groups), 2)) if not last or n > 1 else None
        if last:
            for p in range(2):
                col = (n - 1) * 2 * PANEL + p * PANEL
                self.product(w, col, PANEL, stat, groups, evacuate(col), last=p == 1)
        return [e.at(e.n) for e in self.ev]

    def ffn(self, w_gate, gate_col, w_up, up_col, second):
        act, dve, FF1, FF2 = self.act, self.dve, self.FF1, self.FF2
        n = FF // PANEL

        def products(i, side, turned):
            evacuated = {}

            def gate(t, acc, done):
                wait(act, done, self.ev[t].at(self.ev[t].n), *turned())
                evacuated[t] = self.ev[t](act.activation(FF1[:, t, :], acc, ACT.Copy if second else ACT.Silu))

            def up(t, acc, done):
                wait(dve, done, evacuated[t], *turned())
                if second:
                    self.ev[t](dve.tensor_copy(FF2[:, t, :], acc))
                else:
                    self.ev[t](dve.tensor_tensor(FF2[:, t, :], acc, FF1[:, t, :], ALU.mult))

            self.product(w_gate, i * PANEL + gate_col, PANEL, (self.XH, self.XL), [CK] * 4, gate, side=side)
            self.product(w_up, i * PANEL + up_col, PANEL, (self.XH, self.XL), [CK] * 4, up)

        def turn(i):
            at = i * (PANEL // P)
            ready = [e.at(e.n) for e in self.ev]
            return [lambda kp=kp: (self.turn_conv if second else self.turn_plain)(at, kp, ready) for kp in range(2)]

        def body(i):
            steps = turn(i)
            products(i + 1, {1: steps[0], 4: steps[1]}, lambda: [self.turned])

        products(0, None, lambda: [])
        steps = dict(cpe=2, cact=2, cdve=2) if not second else dict(cpe=2, cact=4, cdve=16)
        self.repeat(n - 1, body, self.per(8, 2, **steps))
        for step in turn(n - 1):
            step()
        return self.cdve.at(self.cdve.n)

    def turn_plain(self, at, kp, ready):
        b = kp
        ps = self.bank(b)
        wait(self.pe, *ready)
        for k in range(2):
            for t in range(TT):
                f = (2 * kp + k) * P
                inst = self.tr(ps[:, k * S + t * P:k * S + (t + 1) * P], self.FF2[:, t, f:f + P])
        self.turned = self.cpe(inst)
        wait(self.act, self.turned)
        hh, hl = (x[:, ds(at + 2 * kp, 2), :] for x in (self.HH, self.HL))
        a = self.cact(self.act.activation(hh, ps[:, :], ACT.Copy))
        wait(self.dve, a)
        self.release(b, self.cdve(self.dve.tensor_tensor(hl, ps[:, :], hh.bitcast(F32), ALU.subtract)))

    def turn_conv(self, at, kp, ready):
        act, dve, G = self.act, self.dve, self.CG
        wait(self.pe, *ready)
        b0, b1 = self.bank(2 * kp), self.bank(2 * kp + 1)
        for k in range(2):
            for t in range(TT):
                f = (2 * kp + k) * P
                o = slice(k * S + t * P, k * S + (t + 1) * P)
                self.tr(b0[:, o], self.FF1[:, t, f:f + P])
                inst = self.tr(b1[:, o], self.FF2[:, t, f:f + P])
        self.turned = self.cpe(inst)
        wait(dve, self.turned, self.cdve.at(self.cdve.n), self.cact.at(self.cact.n))
        vec = lambda j, k: self.V2[:, ds(at + (j * KF + 2 * kp + k), 1)]
        for k in range(2):
            v = self.cdve(dve.tensor_scalar(G[:, k, :], b0[:, k * S:(k + 1) * S], vec(2, k), vec(3, k),
                                            ALU.mult, ALU.add))
        for j in (1, 0):
            s = 2 - j
            wait(dve, v)
            for k in range(2):
                v = self.cdve(dve.scalar_tensor_tensor(
                    out=G[:, k, s:S], in0=b0[:, k * S:(k + 1) * S - s], scalar=vec(j, k), in1=G[:, k, s:S],
                    op0=ALU.mult, op1=ALU.add))
        wait(act, v)
        ge = self.cact(act.activation(G[:, :, :], G[:, :, :], ACT.Gelu))
        wait(dve, ge)
        v = self.cdve(dve.tensor_tensor(G[:, :, :], b1.rearrange("p (k s) -> p k s", k=2), G[:, :, :], ALU.mult))
        self.release(2 * kp, v)
        self.release(2 * kp + 1, v)
        wait(act, v)
        hh, hl = (x[:, ds(at + 2 * kp, 2), :] for x in (self.HH, self.HL))
        a = self.cact(act.activation(hh, G[:, :, :], ACT.Copy))
        wait(dve, a)
        self.cdve(dve.tensor_tensor(hl, G[:, :, :], hh.bitcast(F32), ALU.subtract))

    def ssm_setup(self):
        pe, act, dve, t = self.pe, self.act, self.dve, self.t
        V = lambda n: self.SV[:, n, :]
        (DT, TH, MAG, KK, R1, R2, SIN, COS, ABR, ABI, NR, DEN, RD, Z1, Z2, ZR, ZI, T1, T2) = range(19)
        are, aim = self.V3[:, 18:18 + ST], self.V3[:, 34:34 + ST]
        ld = self.param(self.LDT[:, :], t["ssm_log_dt_2"][0].rearrange("(s q) -> s q", q=2))
        lb = [self.param(self.BRE[:, :, :], t["ssm_b_re_2"][0].rearrange("(s q) p h -> (q p) s h", q=2)),
              self.param(self.BIM[:, :, :], t["ssm_b_im_2"][0].rearrange("(s q) p h -> (q p) s h", q=2))]
        lc = []
        for i, n in enumerate(("ssm_c_re_2", "ssm_c_im_2")):
            for half in range(2):
                lc.append(self.param(self.CRE[:, i, :, 64 * half:64 * half + 64],
                                     t[n][0].rearrange("(u r) h p -> (r h) u p", r=8)))
        wait(dve, ld)
        v = self.cdve(dve.tensor_copy(self.SROW[:, :].rearrange("s (q p) -> s q p", q=2),
                                      self.LDT[:, :].unsqueeze(2).to_broadcast([ST, 2, STATE])))
        wait(pe, v)
        ps = self.bank(0)
        done = self.cpe(self.tr(ps[:, 0:ST], self.SROW[:, :]))
        wait(act, done)
        a = self.cact(act.activation(V(DT), ps[:, 0:ST], ACT.Exp))
        self.release(0, a)

        def step(inst):
            tok = self.cdve(inst)
            wait(dve, tok)
            return tok

        tt = lambda o, x, y, op: step(dve.tensor_tensor(V(o), x, y, op))
        ts = lambda o, x, s1, s2, op0, op1: step(dve.tensor_scalar(V(o), x, s1, s2, op0, op1))
        wait(dve, a)
        tt(TH, V(DT), aim, ALU.mult)
        x = tt(T1, V(DT), are, ALU.mult)
        wait(act, x)
        mag = self.cact(act.activation(V(MAG), V(T1), ACT.Exp))
        big = 1.5 * 2.0 ** 23
        c1, c2 = 6.28125, 0.0019350051879882812
        c3 = TWO_PI - c1 - c2
        for out, shift in ((R1, 0.0), (R2, 0.25)):
            ts(KK, V(TH), 1.0 / TWO_PI, shift, ALU.mult, ALU.add)
            ts(KK, V(KK), big, None, ALU.add, ALU.bypass)
            ts(KK, V(KK), -big, None, ALU.add, ALU.bypass)
            step(dve.scalar_tensor_tensor(out=V(out), in0=V(KK), scalar=-c1, in1=V(TH), op0=ALU.mult, op1=ALU.add))
            step(dve.scalar_tensor_tensor(out=V(out), in0=V(KK), scalar=-c2, in1=V(out), op0=ALU.mult, op1=ALU.add))
            step(dve.scalar_tensor_tensor(out=V(out), in0=V(KK), scalar=-c3, in1=V(out), op0=ALU.mult, op1=ALU.add))
            if shift:
                ts(out, V(out), float(np.pi / 2), None, ALU.add, ALU.bypass)
            r = ts(out, V(out), 3.1415925, -3.1415925, ALU.min, ALU.max)
        wait(act, r)
        self.cact(act.activation(V(SIN), V(R1), ACT.Sin))
        sc = self.cact(act.activation(V(COS), V(R2), ACT.Sin))
        wait(dve, mag, sc)
        tt(ABR, V(MAG), V(COS), ALU.mult)
        tt(ABI, V(MAG), V(SIN), ALU.mult)
        ts(NR, V(ABR), -1.0, None, ALU.add, ALU.bypass)
        tt(T1, are, are, ALU.mult)
        tt(T2, aim, aim, ALU.mult)
        tt(DEN, V(T1), V(T2), ALU.add)
        step(dve.reciprocal(V(RD), V(DEN)))
        tt(T1, V(NR), are, ALU.mult)
        tt(T2, V(ABI), aim, ALU.mult)
        tt(T1, V(T1), V(T2), ALU.add)
        tt(ZR, V(T1), V(RD), ALU.mult)
        tt(T1, V(ABI), are, ALU.mult)
        tt(T2, V(NR), aim, ALU.mult)
        tt(T1, V(T1), V(T2), ALU.subtract)
        tt(ZI, V(T1), V(RD), ALU.mult)
        step(dve.memset(self.BBR[:, :, :], 0.0))
        step(dve.memset(self.BBI[:, :, :], 0.0))
        wait(dve, *lb)
        sc1 = self.SCR[:, 0:256].rearrange("p (s h) -> p s h", h=GROUP)
        sc2 = self.SCR[:, 256:512].rearrange("p (s h) -> p s h", h=GROUP)
        zr, zi = (V(z).unsqueeze(2).to_broadcast([P, ST, GROUP]) for z in (ZR, ZI))
        for dst, x, y, op in ((self.BBR, zr, zi, ALU.subtract), (self.BBI, zi, zr, ALU.add)):
            step(dve.tensor_tensor(sc1, self.BRE[:, :, :], x, ALU.mult))
            step(dve.tensor_tensor(sc2, self.BIM[:, :, :], y, ALU.mult))
            for q in range(2):
                r = slice(64 * q, 64 * q + 64)
                v = step(dve.tensor_tensor(dst[r, :, GROUP * q:GROUP * (q + 1)], sc1[r], sc2[r], op))
        wait(pe, v)
        b = 0
        for src, dst in ((self.BBR, self.BTR), (self.BBI, self.BTI)):
            ps = self.bank(b)
            for u in range(4):
                inst = self.tr(ps[:, u * P:(u + 1) * P], src[:, 4 * u:4 * u + 4, :])
            done = self.cpe(inst)
            wait(act, done)
            bt = self.cact(act.activation(dst[:, :, :], ps.rearrange("p (u s) -> p u s", u=4), ACT.Copy))
            self.release(b, bt)
            b += 1
        step(dve.memset(self.CTR[:, :, :], 0.0))
        z = step(dve.memset(self.CTI[:, :, :], 0.0))
        wait(pe, *lc)
        wait(act, z)
        for i, (dst, sign) in enumerate(((self.CTR, 1.0), (self.CTI, -1.0))):
            ps = self.bank(2 + i)
            for u in range(4):
                inst = self.tr(ps[:, u * P:(u + 1) * P], self.CRE[:, i, u, :])
            done = self.cpe(inst)
            wait(act, done)
            for q in range(2):
                r = slice(64 * q, 64 * q + 64)
                src = ps.rearrange("p (s q h) -> p s q h", q=2, h=GROUP)[r, :, q, :]
                ct = self.cact(act.activation(dst[r, :, GROUP * q:GROUP * (q + 1)], src, ACT.Copy, scale=sign))
            self.release(2 + i, ct)
        self.a_bar = V(ABR), V(ABI)
        return [bt, ct]

    def ssm_powers(self):
        dve = self.dve

        def step(inst):
            tok = self.cdve(inst)
            wait(dve, tok)
            return tok

        pw = self.POW
        step(dve.tensor_copy(pw[:, 0, :, 0], self.a_bar[0]))
        step(dve.tensor_copy(pw[:, 1, :, 0], self.a_bar[1]))
        n = 1
        while n < BLK:
            lo = lambda ri: pw[:, ri, :, 0:n]
            top = lambda ri: pw[:, ri, :, n - 1:n].to_broadcast([P, ST, n])
            new = lambda ri: pw[:, ri, :, n:2 * n]
            tmp = self.SCR[:, 0:ST * n].rearrange("p (s j) -> p s j", s=ST)
            for ri, x, y, op in ((0, 0, 1, ALU.subtract), (1, 1, 0, ALU.add)):
                step(dve.tensor_tensor(new(ri), lo(0), top(x), ALU.mult))
                step(dve.tensor_tensor(tmp, lo(1), top(y), ALU.mult))
                step(dve.tensor_tensor(new(ri), new(ri), tmp, op))
            n *= 2
        sv = self.SV
        step(dve.tensor_copy(sv[:, 20, :], self.a_bar[0]))
        step(dve.tensor_copy(sv[:, 21, :], self.a_bar[0]))
        step(dve.tensor_scalar(sv[:, 22, :], self.a_bar[1], -1.0, None, ALU.mult))
        step(dve.tensor_copy(sv[:, 23, :], self.a_bar[1]))
        step(dve.tensor_copy(sv[:, 24, :], pw[:, 0, :, BLK - 1]))
        step(dve.tensor_copy(sv[:, 25, :], pw[:, 0, :, BLK - 1]))
        step(dve.tensor_scalar(sv[:, 26, :], pw[:, 1, :, BLK - 1], -1.0, None, ALU.mult))
        step(dve.tensor_copy(sv[:, 27, :], pw[:, 1, :, BLK - 1]))

    def ssm(self, u_ready):
        pe, act, dve, XS = self.pe, self.act, self.dve, self.XS
        wait(pe, *u_ready)
        for s in range(ST):
            b = s % 4
            ps = self.bank(b)
            r = slice(32 * (s % 4), 32 * (s % 4) + 32)
            pe.matmul(ps[:, 0:S], self.BTR[r, s // 4, :], self.UT[r, s // 4, :], start=True, stop=True)
            done = self.cpe(pe.matmul(ps[:, S:2 * S], self.BTI[r, s // 4, :], self.UT[r, s // 4, :], start=True, stop=True))
            wait(act, done)
            a = self.cact(act.activation(XS[:, :, s, :], ps.rearrange("p (c t) -> p c t", c=2), ACT.Copy))
            self.release(b, a)
        wait(dve, *u_ready, a)
        self.ssm_powers()
        X5 = XS[:, :, :, :].rearrange("p c s (b j) -> p c s b j", j=BLK)
        STEP = self.STEP

        def advance(prev, cur, coef, n, tmp):
            row = lambda k: self.SV[:, coef + k, :].unsqueeze(2).to_broadcast([P, ST, n])
            wide = lambda x: x
            for c in range(2):
                self.cdve(dve.tensor_tensor(tmp(c), prev(c), row(c), ALU.mult))
            t = self.cdve.at(self.cdve.n)
            wait(dve, t)
            for c in range(2):
                t = self.cdve(dve.tensor_tensor(cur(c), cur(c), tmp(c), ALU.add))
            wait(dve, t)
            for c in range(2):
                t = self.cdve(dve.tensor_tensor(tmp(c), prev(1 - c), row(2 + c), ALU.mult))
            wait(dve, t)
            for c in range(2):
                t = self.cdve(dve.tensor_tensor(cur(c), cur(c), tmp(c), ALU.add))
            wait(dve, t)

        at = lambda j: (lambda c: XS[:, c, :, :].rearrange("p s (b j) -> p s b j", j=BLK)[:, :, :, j])

        def inner(i):
            sl = lambda off: (lambda c: XS[:, c, :, ds(i + off, NB, step=BLK)])
            advance(sl(0), sl(1), 20, NB, lambda c: STEP[:, c, :, :])

        self.repeat_dve(BLK - 1, inner, 8)

        def carry(i):
            sl = lambda off: (lambda c: XS[:, c, :, ds(i * BLK + off, 1)])
            advance(sl(BLK - 1), sl(2 * BLK - 1), 24, 1, lambda c: STEP[:, c, :, 0:1])

        self.repeat_dve(NB - 1, carry, 8)
        nb, nj = NB - 1, BLK - 1
        tmp = self.SCR[:, 0:ST * nb * nj].rearrange("p (s b j) -> p s b j", b=nb, j=nj)
        for ci, x in ((0, 0), (1, 1)):
            cur = X5[:, ci, :, 1:NB, 0:nj]
            for y in range(2):
                pr = self.POW[:, (ci + y) % 2, :, 0:nj].unsqueeze(2).to_broadcast([P, ST, nb, nj])
                last = X5[:, y, :, 0:nb, BLK - 1:BLK].to_broadcast([P, ST, nb, nj])
                t = self.cdve(dve.tensor_tensor(tmp, pr, last, ALU.mult))
                wait(dve, t)
                t = self.cdve(dve.tensor_tensor(cur, cur, tmp, ALU.subtract if (ci, y) == (0, 1) else ALU.add))
                wait(dve, t)
        wait(pe, t)
        for u in range(4):
            ps = self.bank(u)
            for j in range(4):
                s = 4 * u + j
                o = ps[32 * j:32 * j + 32, 0:S]
                pe.matmul(o, self.CTR[:, s, :], XS[:, 0, s, :], start=True, stop=False)
                inst = pe.matmul(o, self.CTI[:, s, :], XS[:, 1, s, :], start=False, stop=True)
            done = self.cpe(inst)
            wait(dve, done)
            y = self.cdve(dve.scalar_tensor_tensor(out=self.GE[:, u, :], in0=self.UT[:, u, :],
                                                   scalar=self.V3[:, 14 + u:15 + u], in1=ps[:, 0:S],
                                                   op0=ALU.mult, op1=ALU.add))
            self.release(u, y)
        wait(act, y)
        g = self.cact(act.activation(self.GE[:, :, :], self.GE[:, :, :], ACT.Gelu))
        wait(act, g)
        a = self.cact(act.activation(self.GEH[:, :, :], self.GE[:, :, :], ACT.Copy))
        wait(dve, a)
        return self.cdve(dve.tensor_tensor(self.GEL[:, :, :], self.GE[:, :, :], self.GEH[:, :, :].bitcast(F32),
                                           ALU.subtract))

    def repeat_dve(self, turns, body, steps):
        start = self.cdve.n
        with self.dve.Fori(0, turns) as i:
            self.loop = Loop(i, turns, {self.cdve: steps})
            self.cdve.loop = self.loop
            body(i)
        assert self.cdve.n - start == steps, self.cdve.n - start
        self.loop = self.cdve.loop = None
        self.cdve.n = start + turns * steps

    def glu(self):
        act, dve, w = self.act, self.dve, self.t["w_glu_2"][0]
        gb = self.param(self.GBR[:, :], self.t["b_glu_2"][0].partition_broadcast(P))
        wait(dve, gb)
        for p in range(2):
            cols = slice(p * SSMW, (p + 1) * SSMW)

            def evacuate(t, acc, done, cols=cols):
                wait(dve, done)
                self.ev[t](dve.tensor_tensor(self.GLU[:, t, cols], acc, self.GBR[:, cols], ALU.add))
            self.product(w, p * SSMW, SSMW, (self.GEH, self.GEL), [2, 2], evacuate)
        wait(act, *[e.at(e.n) for e in self.ev])
        for t in range(TT):
            a = self.cact(act.activation(self.GLU[:, t, SSMW:], self.GLU[:, t, SSMW:], ACT.Sigmoid))
        wait(dve, a)
        for t in range(TT):
            v = self.cdve(dve.tensor_tensor(self.GLU[:, t, 0:SSMW], self.GLU[:, t, 0:SSMW], self.GLU[:, t, SSMW:],
                                            ALU.mult))
        return self.feature_major(lambda k, t: self.GLU[:, t, k * P:(k + 1) * P], 4, self.SH, self.SL, [v])

    def norm_between(self, x_ready):
        row = self.param(self.FW[:, :], self.t["final_norm_w"].partition_broadcast(P))
        r = self.rstd(x_ready, self.RSTD[:, 0:2])
        wait(self.dve, r, row)
        out = []
        for t in range(TT):
            out.append(self.cdve(self.dve.scalar_tensor_tensor(
                out=self.X[:, t, :], in0=self.X[:, t, :], scalar=self.RSTD[:, t:t + 1], in1=self.FW[:, :],
                op0=ALU.mult, op1=ALU.mult)))
        return out

    def build(self):
        act, dve, pe, t = self.act, self.dve, self.pe, self.t
        dve.sem_inc(self.lo.sem, 2 * SLOTS)
        pe.sem_inc(self.mm.sem, PIECES)
        for e in self.ev:
            dve.sem_inc(e.sem, 2)
        self.lo.n, self.mm.n, self.ev[0].n, self.ev[1].n = 2 * SLOTS, PIECES, 2, 2
        xl = [self.param(self.X[:, i, :], t["x"][0, i * P:(i + 1) * P, :]) for i in range(TT)]
        self.const_ready = self.constants()
        for _ in range(AHEAD):
            self.split_piece()
        self.vectors()
        self.norm_to_T(xl, 0)
        w_in = t["w_in"][0]
        r = self.project(w_in, COL_BCU, PANEL, 6, self.TOK)
        self.conv_branch(r)
        self.settle()
        self.a_down()
        self.settle()
        r = self.project(w_in, COL_QKV, PANEL, 6, self.TOK)
        q = self.transposed(lambda k, t: self.TOK[:, t, k * P:(k + 1) * P], 8, self.QT, r)
        k = self.transposed(lambda k, t: self.TOK[:, t, BW + k * P:BW + (k + 1) * P], 8, self.KT, r)
        wait(pe, *q, *k)
        self.attention(
            HEADS, lambda h: (self.QT[:, h, :], self.KT[:, h, :]),
            lambda h: [self.TOK[:, t, 2 * BW + h * DH:2 * BW + (h + 1) * DH] for t in range(TT)],
            (self.OH, self.OL), self.DIST, lambda h: 2.0 ** (-8.0 * (h + 1) / HEADS), DH ** -0.5,
            ptile=self.PR, ptT=self.PT)
        self.settle()
        r = self.project(w_in, COL_GLA, PANEL, 6, self.TOK)
        self.gla(r)
        self.settle()
        self.merge_branch(w_in, COL_MERGE, t["w_br_attn"][0], (self.OH, self.OL), 8, self.MIX, True)
        self.merge_branch(w_in, COL_MERGE + D, t["w_br_gla"][0], (self.GHI, self.GLO), 8, self.MIX, False)
        self.merge_branch(w_in, COL_MERGE + 2 * D, t["w_br_conv"][0], (self.YH, self.YL), 8, self.MIX, False)
        self.out_and_ffn(self.MIX, t["w_out"][0], KD, t["w_ffn_gate"][0], 0, t["w_ffn_up"][0], 0,
                         t["w_ffn_down"][0], False, False)
        r = self.norm_between([e.at(e.n) for e in self.ev])
        self.settle()
        self.norm_to_T(r, 2 * KD)
        w_in = t["w_in_2"][0]
        r = self.project(w_in, 0, QKVU2 // 4, 4, self.TOK2)
        self.block2_branches(r)
        self.settle()
        gr = self.param(self.GROW[:, :], t["b_in_2"][0, QKVU2:].partition_broadcast(P))
        wait(dve, gr)
        self.merge_branch(w_in, QKVU2, t["w_branch_attn_2"][0], (self.OH2, self.OL2), 8, self.MG, True,
                          rows=lambda c: self.GROW[:, ds(c, PANEL)])
        self.merge_branch(w_in, QKVU2 + D, t["w_branch_ssm_2"][0], (self.SH, self.SL), 4, self.MG, False,
                          rows=lambda c: self.GROW[:, ds(c + D, PANEL)])
        self.out_and_ffn(self.MG, t["w_out_2"][0], 3 * KD, t["w_up_2"][0], FF, t["w_up_2"][0], 0,
                         t["w_down_2"][0], True, True)
        row = self.param(self.FW[:, :], t["final_norm_g_2"].partition_broadcast(P))
        x = self.rstd([e.at(e.n) for e in self.ev], self.RSTD[:, 0:2])
        wait(dve, x, row)
        for i in range(TT):
            v = self.cdve(dve.scalar_tensor_tensor(out=self.X[:, i, :], in0=self.X[:, i, :],
                                                   scalar=self.RSTD[:, i:i + 1], in1=self.FW[:, :],
                                                   op0=ALU.mult, op1=ALU.mult))
            wait(self.sp, v)
            stored = self.cdma[i](self.sp.dma_start(self.out[0, i * P:(i + 1) * P, :], self.X[:, i, :]))
            wait(self.sp, stored)

    def settle(self):
        steps = [c.at(c.n) for c in (self.cpe, self.cact, self.cdve, self.cpool, *self.ev)] + [self.mm.at(self.mm.n)]
        for e in (self.pe, self.act, self.dve):
            wait(e, *steps)

    def out_and_ffn(self, mixed, w_out, w_norm, w_gate, gate_col, w_up, up_col, w_down, second, last):
        ready = [e.at(e.n) for e in self.ev] + [self.cdve.at(self.cdve.n)]
        self.settle()
        m = self.feature_major(lambda k, t: mixed[:, t, k * P:(k + 1) * P], KD, self.XH, self.XL, ready)
        wait(self.pe, m)
        r = self.residual(w_out, (self.XH, self.XL), [CK] * 4)
        self.settle()
        self.norm_to_T(r, KD if not second else 3 * KD)
        self.settle()
        h = self.ffn(w_gate, gate_col, w_up, up_col, second)
        wait(self.pe, h)
        self.residual(w_down, (self.HH, self.HL), [4] * 8 + [3] * 4, last=last)
        self.settle()

    def block2_branches(self, r):
        act, dve, pe, t = self.act, self.dve, self.pe, self.t
        TOK = self.TOK2
        kcol, vcol, ucol = 1024, 1152, 1280
        vb = self.param(self.VB[:, :], t["b_in_2"][0, vcol:ucol].partition_broadcast(P))
        sk = self.param(self.SINK[:, :], t["attn_sinks_2"][0].partition_broadcast(P))
        bias = lambda k: self.V3[:, k:k + 1]
        q = self.transposed(lambda k, t: TOK[:, t, k * P:(k + 1) * P], 8, self.QT2, r, bias=bias)
        wait(dve, *r, vb, sk)
        for g in range(KVH2):
            src = TOK[:, :, kcol + g * DH2:kcol + (g + 1) * DH2]
            for half in range(2):
                v = self.cdve(dve.tensor_copy(self.KDUP[:, :, g * P + half * DH2:g * P + (half + 1) * DH2], src))
        vv = self.cdve(dve.tensor_tensor(TOK[:, 0, vcol:ucol], TOK[:, 0, vcol:ucol], self.VB[:, :], ALU.add))
        vv = self.cdve(dve.tensor_tensor(TOK[:, 1, vcol:ucol], TOK[:, 1, vcol:ucol], self.VB[:, :], ALU.add))
        kb = self.SV[:, 28:29, 0:2]
        self.KB = kb
        wait(pe, v)
        ps = self.bank(0)
        for g in range(KVH2):
            for i in range(TT):
                inst = self.tr(ps[:, g * S + i * P:g * S + (i + 1) * P], self.KDUP[:, i, g * P:(g + 1) * P])
        done = self.cpe(inst)
        for g in range(KVH2):
            for half in range(2):
                rows = slice(half * DH2, (half + 1) * DH2)
                c = self.cact(act.activation(self.SV[rows, 28, g:g + 1], self.V3[g * DH2:(g + 1) * DH2, 8:9], ACT.Copy))
        wait(dve, done, c)
        for g in range(KVH2):
            k = self.cdve(dve.tensor_scalar(self.KT2[:, g, :], ps[:, g * S:(g + 1) * S], self.SV[:, 28, g:g + 1], None,
                                            ALU.add))
        self.release(0, k)
        u = self.transposed(lambda k, t: TOK[:, t, ucol + k * P:ucol + (k + 1) * P], 4, self.UT, r,
                            bias=lambda k: self.V3[:, 10 + k:11 + k])
        wait(pe, *q, k, vv)

        def scores(h):
            r = slice(DH2 * (h % 2), DH2 * (h % 2) + DH2)
            return self.QT2[r, h // 2, :], self.KT2[r, h // (HEADS2 // KVH2), :]

        def values(h):
            c = vcol + DH2 * (h // (HEADS2 // KVH2))
            return [TOK[:, i, c:c + DH2] for i in range(TT)]

        self.attention(HEADS2, scores, values, (self.OH2, self.OL2), self.DIST2,
                       lambda h: 2.0 ** (-8.0 * (h + 1) / HEADS2), DH2 ** -0.5, sink=self.SINK, dh=DH2,
                       ptile=self.PR2, ptT=self.PT2)
        self.settle()
        s = self.ssm_setup()
        g = self.ssm([*s, *u])
        wait(pe, g)
        self.glu()


def block_program(nc, tensors, out):
    with ExitStack() as ctx:
        Kernel(nc, ctx, tensors, out).build()


def kernel(**inputs):
    import concourse.bacc as bacc
    from concourse.bass_utils import run_bass_kernel_spmd

    nc = bacc.Bacc("TRN2", target_bir_lowering=False, num_devices=1, dynamic_dma_scratch_size=1024)
    arrays = {f"in_{n}": np.ascontiguousarray(a) for n, a in inputs.items()}
    tensors = {n: nc.dram_tensor(f"in_{n}", a.shape, mybir.dt.from_np(arrays[f"in_{n}"].dtype),
                                 kind="ExternalInput").ap() for n, a in inputs.items()}
    out = nc.dram_tensor("out", (1, S, D), F32, kind="ExternalOutput").ap()
    block_program(nc, tensors, out)
    r = run_bass_kernel_spmd(nc, [arrays], core_ids=[0])
    return r.results[0]["out"]
```

```python
from contextlib import ExitStack

import numpy as np

import concourse.bass as bass
from concourse import mybir

F32 = mybir.dt.float32
F32R = mybir.dt.float32r
U32 = mybir.dt.uint32
ALU = mybir.AluOpType
ACT = mybir.ActivationFunctionType
AX = mybir.AxisListType.X
ds = bass.ds

P = 128
S = 256
TT = S // P
D = 2048
KD = D // P
EPS = 1e-6
NEVER = 1e30
HEADS, DH = 8, 128
GH, GK, GV, RANK, CHUNK, TAU = 4, 128, 256, 16, 64, 16.0
BW = 1024
FF = 5632
KF = FF // P
COL_QKV, COL_GLA, COL_AD = 0, 3072, 6144
COL_BCU = COL_AD + RANK
COL_MERGE = COL_BCU + 3 * BW
HEADS2, DH2, KVH2, WINDOW2 = 16, 64, 2, 128
NG, GROUP, STATE = 32, 16, 64
ST = NG * STATE // P
SSMW = NG * GROUP
QKVU2 = HEADS2 * DH2 + 2 * KVH2 * DH2 + SSMW
BLK = 16
NB = S // BLK
PANEL = 512
CK = 4
SLOTS = 4
AHEAD = 3
PIECES = 4
TWO_PI = 2.0 * np.pi


class Token:

    def __init__(self, counter, n, loop):
        self.counter, self.n, self.loop = counter, n, loop


class Counter:

    def __init__(self, sem, step=1):
        self.sem, self.step, self.n, self.loop = sem, step, 0, None

    def __call__(self, inst):
        inst.then_inc(self.sem, self.step)
        self.n += self.step
        return Token(self, self.n, self.loop)

    def at(self, n):
        return Token(self, n, self.loop)


class Loop:

    def __init__(self, index, turns, per):
        self.index, self.turns, self.per = index, turns, per


def wait(eng, *tokens):
    for t in tokens:
        if t is None:
            continue
        if t.loop is None:
            value = t.n
        elif t.counter.loop is t.loop:
            value = t.loop.index * t.loop.per[t.counter] + t.n
        else:
            value = (t.loop.turns - 1) * t.loop.per[t.counter] + t.n
        eng.wait_ge(t.counter.sem, value)


class Kernel:
    def __init__(self, nc, ctx, t, out):
        self.nc, self.ctx, self.t, self.out = nc, ctx, t, out
        self.sp, self.pe, self.act, self.dve, self.pool = nc.sync, nc.tensor, nc.scalar, nc.vector, nc.gpsimd
        sem = lambda name: ctx.enter_context(nc.semaphore(name))
        self.tick = sem("loads_started")
        self.loaded = [Counter(sem(f"loaded{i}"), 16) for i in range(4)]
        self.hi = Counter(sem("hi_split"))
        self.lo = Counter(sem("lo_split"))
        self.mm = Counter(sem("chunk_multiplied"))
        self.ev = [Counter(sem(f"evacuated{i}")) for i in range(TT)]
        self.cpe = Counter(sem("tensor_step"))
        self.cact = Counter(sem("scalar_step"))
        self.cdve = Counter(sem("vector_step"))
        self.cpool = Counter(sem("pool_step"))
        self.cdma = [Counter(sem(f"param_load{i}"), 16) for i in range(8)]
        self.ndma = 0
        self.counters = self.loaded + [self.hi, self.lo, self.mm] + self.ev + [
            self.cpe, self.cact, self.cdve, self.cpool]
        self.g = 0
        self.gs = 0
        self.background = []
        self.panel = 0
        self.loop = None
        self.base = (nc.sbuf_base + 63) // 64 * 64
        self.side_free = [[] for _ in range(4)]
        self.memory()

    def sb(self, name, shape, offset, dtype=F32):
        return self.nc.alloc_sbuf_tensor_at(name, shape, dtype, offset=self.base + offset)

    def memory(self):
        K = 1024
        sb = self.sb
        self.RAW = sb("weights", [P, 4, CK * PANEL], 0)
        self.HI = sb("weights_hi", [P, PIECES, 2 * PANEL], 32 * K, F32R)
        self.LO = sb("weights_lo", [P, PIECES, 2 * PANEL], 48 * K, F32R)
        self.X = sb("x", [P, TT, D], 64 * K)
        off = 80 * K

        def small(name, shape, dtype=F32):
            nonlocal off
            t = sb(name, shape, off, dtype)
            off += (int(np.prod(shape[1:])) * 4 + 31) // 32 * 32
            return t

        self.IDENT = small("identity", [P, P])
        self.U = small("cumsum_in_chunk", [P, P])
        self.LS = small("suffix_in_chunk", [P, P])
        self.DIST = small("distance", [P, 3 * P])
        self.DIST2 = small("distance_in_window", [P, 3 * P])
        self.V1 = small("vectors1", [P, 90])
        self.V2 = small("vectors2", [P, 4 * KF])
        self.V3 = small("vectors3", [P, 66])
        self.SS = small("square_sums", [P, 2])
        self.MS = small("mean_squares", [P, 2])
        self.RSTD = small("rstd", [P, 2])
        self.NHALF = small("minus_half", [P, 2])
        self.AD = small("a_down", [P, TT, RANK])
        self.RMAX = small("row_max", [P, 2, 2])
        self.RSUM = small("row_sum", [P, 2, 2])
        self.RINV = small("row_inverse", [P, 2, 2])
        self.SINK = small("sinks", [P, HEADS2])
        self.NM = small("minus_max", [P, 2, 2])
        self.ESINK = small("exp_sink", [P, 2, 2])
        assert off <= 88 * K, off
        self.AA = A = 88 * K
        self.XH = sb("xT_hi", [P, KD, S], A, F32R)
        self.XL = sb("xT_lo", [P, KD, S], A + 16 * K, F32R)
        R = A + 32 * K
        self.H = sb("normed", [P, TT, D], R + 80 * K)
        self.TA = sb("projected_a", [P, TT, 3 * BW], R)
        self.TB = sb("projected_b", [P, TT, 3 * BW], R + 24 * K)
        self.YH = sb("convT_hi", [P, 8, S], R + 48 * K, F32R)
        self.YL = sb("convT_lo", [P, 8, S], R + 56 * K, F32R)
        self.QT = sb("qT", [P, HEADS, S], R + 64 * K)
        self.KT = sb("kT", [P, HEADS, S], R + 72 * K)
        self.OH = sb("attnT_hi", [P, 8, S], R + 80 * K, F32R)
        self.OL = sb("attnT_lo", [P, 8, S], R + 88 * K, F32R)
        self.MIX = sb("mixed", [P, TT, D], R + 24 * K)
        self.SIG = sb("gates", [P, TT, 2, PANEL], R + 40 * K)
        self.GHI = sb("glaT_hi", [P, 8, S], R + 64 * K, F32R)
        self.GLO = sb("glaT_lo", [P, 8, S], R + 72 * K, F32R)
        self.WAD = sb("w_a_down", [P, KD, RANK], R + 64 * K)
        self.WADH = sb("w_a_down_hi", [P, KD, RANK], R + 65 * K, F32R)
        self.WADL = sb("w_a_down_lo", [P, KD, RANK], R + 66 * K, F32R)
        T = R + 96 * K
        self.BT = sb("b_gateT", [P, 2, S], T)
        self.CUT = sb("cuT", [P, 2, S], T + 2 * K)
        self.CACC = sb("conv_acc", [P, 2, S], T + 4 * K)
        self.PR = sb("probabilities", [P, 2, 3 * P], T)
        self.PT = sb("probabilitiesT", [P, 2, 3 * P], T + 3 * K)
        self.LA = sb("log_a", [P, TT, 512], R + 64 * K)
        self.KDEC = sb("k_decayed", [P, TT, 512], R + 68 * K)
        self.GB = sb("gla_b_rows", [P, 512], R + 72 * K)
        self.ADT = sb("a_downT", [RANK, S], R + 74 * K)
        self.WUP = sb("gla_w_up", [RANK, 512], R + 75 * K)
        self.ST = sb("gla_state", [P, 3, 256], R + 77 * K)
        self.EB = sb("exp_b", [P, S], T)
        self.EN = sb("exp_minus_b", [P, S], T + K)
        self.QIN = sb("q_in", [P, S], T + 2 * K)
        self.KIN = sb("k_in", [P, S], T + 3 * K)
        self.AT = sb("aT", [P, TT, P], T + 4 * K)
        self.HH = sb("hiddenT_hi", [P, KF, S], R, F32R)
        self.HL = sb("hiddenT_lo", [P, KF, S], R + 44 * K, F32R)
        self.CG = sb("conv_gelu", [P, 2, S], R + 96 * K)
        self.FW = sb("final_norm_rows", [P, D], R)
        self.TOK2 = sb("projected2", [P, TT, QKVU2], R)
        self.QT2 = sb("qT2", [P, 8, S], R + 14 * K)
        self.OH2 = sb("attn2T_hi", [P, 8, S], R + 14 * K, F32R)
        self.OL2 = sb("attn2T_lo", [P, 8, S], R + 22 * K, F32R)
        self.KT2 = sb("kT2", [P, KVH2, S], R + 30 * K)
        self.KDUP = sb("k_twice", [P, TT, KVH2 * P], R + 32 * K)
        self.VB = sb("v_bias_rows", [P, KVH2 * DH2], R + 34 * K)
        self.PR2 = sb("probabilities2", [P, 2, 3 * P], R + 35 * K)
        self.PT2 = sb("probabilitiesT2", [P, 2, 3 * P], R + 38 * K)
        self.UT = sb("uT", [P, 4, S], R + 41 * K)
        self.GEL = sb("ssm_geluT_lo", [P, 4, S], R + 41 * K, F32R)
        self.GEH = sb("ssm_geluT_hi", [P, 4, S], R + 30 * K, F32R)
        self.XS = sb("ssm_states", [P, 2, ST // 2, S], R + 45 * K)
        self.STEP = sb("scan_step", [P, 4, ST // 2, NB], R + 61 * K)
        self.SCR = sb("ssm_scratch", [P, 1024], R + 63 * K)
        self.POW = sb("a_powers", [P, 2, ST, BLK], R + 67 * K)
        self.BTR = sb("bbT_re", [P, 4, P], R + 69 * K)
        self.BTI = sb("bbT_im", [P, 4, P], R + 71 * K)
        self.CTR = sb("cT_re", [P, ST, 2 * GROUP], R + 73 * K)
        self.CTI = sb("cT_im", [P, ST, 2 * GROUP], R + 75 * K)
        self.SV = sb("ssm_vectors", [P, 32, ST], R + 77 * K)
        self.MG = sb("merged", [P, TT, D], R + 79 * K)
        self.GROW = sb("gate_bias_rows", [P, 2, PANEL], R + 95 * K)
        self.BRE = sb("b_re", [P, ST, GROUP], R + 14 * K)
        self.BIM = sb("b_im", [P, ST, GROUP], R + 15 * K)
        self.BBR = sb("bb_re", [P, ST, 2 * GROUP], R + 16 * K)
        self.BBI = sb("bb_im", [P, ST, 2 * GROUP], R + 18 * K)
        self.CRE = sb("c_twice", [P, 2, 4, P], R + 20 * K)
        self.SROW = sb("log_dt_rows", [ST, P], R + 24 * K)
        self.LDT = sb("log_dt", [ST, 2], R + 24 * K + 512)
        self.GS = sb("ssm_gates", [P, TT, D], R)
        self.GLU = sb("glu", [P, TT, 2 * SSMW], R + 16 * K)
        self.GBR = sb("b_glu_rows", [P, 2 * SSMW], R + 24 * K)
        self.SH = sb("ssmT_hi", [P, 4, S], R + 45 * K, F32R)
        self.SL = sb("ssmT_lo", [P, 4, S], R + 49 * K, F32R)
        self.FF1 = sb("ffn_gate", [P, TT, PANEL], R + 88 * K)
        self.FF2 = sb("ffn_hidden", [P, TT, PANEL], R + 92 * K)
        psum = lambda n: self.ctx.enter_context(self.nc.psum_tensor(n, [P, 4, PANEL], F32))
        self.ACC, self.SIDE = psum("panels"), psum("side")
        self.R = R

    def repeat(self, turns, body, per):
        per = {c: per.get(c, 0) for c in self.counters}
        start = {c: c.n for c in self.counters}
        nc = self.nc
        with nc.Fori(0, turns, engines=[e.engine for e in (self.act, self.pe, self.dve, self.sp)]) as i:
            loop = self.loop = Loop(i, turns, per)
            for c in self.counters:
                c.loop = loop
            for b in range(4):
                self.side_free[b] = [self.cact.at(self.cact.n), self.cdve.at(self.cdve.n)]
            self.before = [c.at(c.n) for c in (self.cpe, self.cact, self.cdve)]
            body(i)
        self.loop = None
        for c in self.counters:
            grown = c.n - start[c]
            assert grown == per[c], (c.sem, grown, per[c])
            c.loop = None
            c.n = start[c] + turns * grown
        chunks = per[self.mm]
        for b in range(4):
            self.side_free[b] = [self.cact.at(self.cact.n), self.cdve.at(self.cdve.n)]
        self.g += (turns - 1) * chunks
        self.gs += (turns - 1) * chunks
        self.panel += (turns - 1) * per[self.ev[0]]

    def per(self, chunks, panels, **more):
        p = {c: 16 * chunks // 4 for c in self.loaded}
        p.update({self.hi: 2 * chunks, self.lo: 2 * chunks, self.mm: 2 * chunks, self.ev[0]: panels, self.ev[1]: panels})
        p.update({{"cpe": self.cpe, "cact": self.cact, "cdve": self.cdve}[k]: v for k, v in more.items()})
        return p

    def load_chunk(self, w, k0, nk, col, width):
        g = self.g // 2
        slot = g % SLOTS
        wait(self.sp, self.lo.at(2 * g + 2))
        self.sp.sem_inc(self.tick, 1)
        src = w[k0 * P:(k0 + nk) * P, ds(col, width)].rearrange("(k p) n -> p k n", p=P)
        dst = self.RAW[:, slot, :].rearrange("p (k n) -> p k n", n=PANEL)
        dst = dst[:, 0:CK:2, 0:width] if nk == 2 else dst[:, 0:nk, 0:width]
        self.loaded[slot](self.sp.dma_start(dst, src))

    def split_piece(self):
        g = self.gs
        slot, part, ring = g // 2 % SLOTS, g % 2, g % PIECES
        raw = self.RAW[:, slot, part * 2 * PANEL:(part + 1) * 2 * PANEL]
        if part == 0:
            wait(self.act, self.loaded[slot].at(16 * (g // 2 // SLOTS + 1)))
        if g >= PIECES or self.loop:
            wait(self.act, self.mm.at(g + 1))
        self.hi(self.act.activation(self.HI[:, ring, :], raw, ACT.Copy))
        wait(self.dve, self.hi.at(g + 1))
        self.lo(self.dve.tensor_tensor(self.LO[:, ring, :], raw, self.HI[:, ring, :].bitcast(F32), ALU.subtract))
        self.gs += 1

    def product(self, w, col, width, stat, chunks, evacuate, last=False, side=None):
        p = self.panel
        hi, lo = stat
        k0 = 0
        total = sum(chunks)
        for c, nk in enumerate(chunks):
            self.load_chunk(w, k0, nk, col, width)
            for part, np_ in enumerate(((nk + 1) // 2, nk // 2)):
                g, ring = self.g, self.g % PIECES
                self.g += 1
                if not last or 2 * c + part + AHEAD < 2 * len(chunks):
                    self.split_piece()
                wait(self.pe, self.lo.at(g + 1 + 2 * SLOTS))
                for t in range(TT):
                    if k0 == 0:
                        wait(self.pe, self.ev[t].at(p + 1))
                    acc = self.ACC[:, (p % 2) * TT + t, 0:width]
                    for k in range(np_):
                        a, b = (x[:, k0 + k, t * P:(t + 1) * P] for x in (hi, lo))
                        wh, wl = (x[:, ring, k * PANEL:k * PANEL + width] for x in (self.HI, self.LO))
                        first, final = k0 + k == 0, k0 + k == total - 1
                        self.pe.matmul(acc, a, wh, start=first, stop=False)
                        self.pe.matmul(acc, a, wl, start=False, stop=False)
                        inst = self.pe.matmul(acc, b, wh, start=False, stop=final)
                done = self.mm(inst)
                k0 += np_
                if side and 2 * c + part in side:
                    side[2 * c + part]()
                if self.loop is None and self.background:
                    if next(self.background[0], self) is self:
                        self.background.pop(0)
        self.panel += 1
        for t in range(TT):
            evacuate(t, self.ACC[:, (p % 2) * TT + t, 0:width], done)

    def run(self, work):
        while True:
            try:
                next(work)
            except StopIteration as end:
                return end.value

    def finish_background(self):
        for work in self.background:
            self.run(work)
        self.background = []

    def unrolled(self, turns, body):
        for i in range(turns):
            self.before = [c.at(c.n) for c in (self.cpe, self.cact, self.cdve)]
            body(i)

    def bank(self, b):
        wait(self.pe, *self.side_free[b])
        self.side_free[b] = []
        return self.SIDE[:, b, :]

    def release(self, b, *tokens):
        self.side_free[b] = list(tokens)

    def param(self, dst, src):
        c = self.cdma[self.ndma % len(self.cdma)]
        self.ndma += 1
        if c.n:
            wait(self.act, c.at(c.n))
        return c(self.act.dma_start(dst, src))

    def tr(self, out, in_):
        return self.pe.transpose(out, in_, self.IDENT[0:in_.shape[0], 0:in_.shape[0]])

    def feature_major_steps(self, src, nk, hi, lo, ready, weights=None, at=0):
        wait(self.pe, *ready)
        last = None
        for kp in range(nk // 2):
            b = kp % 4
            ps = self.bank(b)
            for k in range(2):
                for t in range(TT):
                    inst = self.tr(ps[:, k * S + t * P:k * S + (t + 1) * P], src(2 * kp + k, t))
            done = self.cpe(inst)
            wait(self.act, done)
            if weights is None:
                a = self.cact(self.act.activation(hi[:, ds(at + 2 * kp, 2), :], ps[:, :], ACT.Copy))
                wait(self.dve, a)
                last = self.cdve(self.dve.tensor_tensor(lo[:, ds(at + 2 * kp, 2), :], ps[:, :],
                                                        hi[:, ds(at + 2 * kp, 2), :].bitcast(F32), ALU.subtract))
            else:
                for k in range(2):
                    w = weights(2 * kp + k)
                    a = self.cact(self.act.activation(hi[:, 2 * kp + k, :], ps[:, k * S:(k + 1) * S],
                                                      ACT.Copy, scale=w))
                for k in range(2):
                    w = weights(2 * kp + k)
                    wait(self.dve, a)
                    last = self.cdve(self.dve.scalar_tensor_tensor(
                        out=lo[:, 2 * kp + k, :], in0=ps[:, k * S:(k + 1) * S], scalar=w,
                        in1=hi[:, 2 * kp + k, :].bitcast(F32), op0=ALU.mult, op1=ALU.subtract))
            self.release(b, last)
            yield
        return last

    def feature_major(self, *args, **more):
        return self.run(self.feature_major_steps(*args, **more))

    def constants(self):
        pool = self.pool

        def c(inst):
            tok = self.cpool(inst)
            wait(pool, tok)
            return tok

        c(pool.memset(self.IDENT[:, :], 0.0))
        c(pool.memset(self.U[:, :], 1.0 / TAU))
        c(pool.memset(self.LS[:, :], 1.0 / TAU))
        c(pool.memset(self.NHALF[:, :], -0.5))
        c(pool.iota(self.DIST[:, 0:P], [[-1, P]], base=0, channel_multiplier=1, allow_small_or_imprecise_dtypes=True))
        c(pool.iota(self.DIST[:, P:3 * P], [[-1, S]], base=P, channel_multiplier=1,
                    allow_small_or_imprecise_dtypes=True))

        def select(m, pattern, base, cm, op, fill, like=None):
            return c(pool.affine_select(out=m, in_=m if like is None else like, compare_op=op, fill=fill,
                                        base=base, pattern=pattern, channel_multiplier=cm))

        select(self.IDENT[:, :], [[-1, P]], 0, 1, ALU.not_equal, 1.0)
        select(self.U[:, :], [[1, P]], 0, -1, ALU.is_ge, 0.0)
        select(self.LS[:, :], [[-1, P]], 0, 1, ALU.is_gt, 0.0)
        select(self.DIST[:, 0:P], [[-1, P]], 0, 1, ALU.is_ge, NEVER)
        select(self.DIST[:, P:3 * P], [[-1, S]], P, 1, ALU.is_ge, NEVER)
        select(self.U[0:64, 64:P], [[0, 64]], -1, 0, ALU.is_ge, 0.0)
        select(self.LS[64:P, 0:64], [[0, 64]], -1, 0, ALU.is_ge, 0.0)
        c(pool.tensor_copy(self.DIST2[:, 0:P], self.DIST[:, 0:P]))
        return select(self.DIST2[:, P:3 * P], [[1, S]], WINDOW2 - 1 - P, -1, ALU.is_ge, NEVER,
                      like=self.DIST[:, P:3 * P])

    def vectors(self):
        t = self.t
        R = self.R
        rows = [self.sb(f"rows{i}", [P, P], R + 512 * i) for i in range(4)]
        loads = [[], [], [], []]
        put = lambda i, at, n, src: loads[i].append(self.param(rows[i][at:at + n, :], src))
        vec = lambda x: x.rearrange("(k p) -> k p", p=P)
        at = 0
        for n in ("norm1_w", "norm2_w", "attn_norm_g_2", "ffn_norm_g_2"):
            put(0, at, KD, vec(t[n][0]))
            at += KD
        put(0, at, 2, vec(t["gla_norm_w"][0]))
        put(0, at + 2, 24, t["conv_w"][0].rearrange("j (k p) -> (j k) p", p=P))
        cw = t["conv_w_2"][0].rearrange("j (k p) -> (j k) p", p=P)
        put(1, 0, 88, cw[0:88, :])
        put(2, 0, 44, cw[88:132, :])
        put(2, 44, 44, vec(t["conv_b_2"][0]))
        put(3, 0, 14, t["b_in_2"][0, 0:QKVU2].rearrange("(k p) -> k p", p=P))
        put(3, 14, 4, vec(t["ssm_d_2"][0]))
        put(3, 18, ST, t["ssm_a_re_2"][0].rearrange("(s q) p -> s (q p)", q=2))
        put(3, 34, ST, t["ssm_a_im_2"][0].rearrange("(s q) p -> s (q p)", q=2))
        for i, (dst, n) in enumerate(((self.V1[:, :], 90), (self.V2[:, 0:88], 88), (self.V2[:, 88:176], 88),
                                      (self.V3[:, 0:50], 50))):
            wait(self.pe, *loads[i], self.const_ready)
            ps = self.bank(i)
            done = self.cpe(self.tr(ps[:, 0:n], rows[i][0:n, :]))
            wait(self.act, done)
            self.vec_ready = self.cact(self.act.activation(dst, ps[:, 0:n], ACT.Copy))
            self.release(i, self.vec_ready)
        wait(self.dve, self.vec_ready)

    def rstd(self, x_ready, out):
        junk = self.H
        wait(self.act, *x_ready)
        for t in range(TT):
            a = self.cact(self.act.activation(junk[:, t, :], self.X[:, t, :], ACT.Square,
                                              accum_out=self.SS[:, t:t + 1]))
        return self.power(a, self.SS[:, 0:2], 1.0 / D, out)

    def power(self, ready, sums, scale, out):
        wait(self.dve, ready)
        d = self.cdve(self.dve.tensor_scalar(self.MS[:, 0:2], sums, scale, EPS, ALU.mult, ALU.add))
        wait(self.pool, d)
        return self.cpool(self.pool.tensor_tensor(out, self.MS[:, 0:2], self.NHALF[:, 0:2], ALU.pow))

    def norm_to_T(self, x_ready, w0):
        r = self.rstd(x_ready, self.RSTD[:, 0:2])
        wait(self.dve, r)
        for t in range(TT):
            h = self.cdve(self.dve.tensor_scalar(self.H[:, t, :], self.X[:, t, :], self.RSTD[:, t:t + 1], None,
                                                 ALU.mult))
        last = self.feature_major(lambda k, t: self.H[:, t, k * P:(k + 1) * P], KD, self.XH, self.XL, [h],
                                  weights=lambda k: self.V1[:, w0 + k:w0 + k + 1])
        wait(self.pe, last)

    def project(self, w, col0, width, panels, dst, unroll=False):

        def body(i):
            for p in range(2):
                def evacuate(t, acc, done, p=p):
                    o = dst[:, t, ds(i * 2 * width + p * width, width)]
                    if t == 0:
                        wait(self.act, done)
                        self.ev[0](self.act.activation(o, acc, ACT.Copy))
                    else:
                        wait(self.dve, done)
                        self.ev[1](self.dve.tensor_copy(o, acc))
                self.product(w, i * 2 * width + (col0 + p * width), width, (self.XH, self.XL), [CK] * 4, evacuate)
        if unroll:
            self.unrolled(panels // 2, body)
        else:
            self.repeat(panels // 2, body, self.per(8, 2))
        return self.ev[0].at(self.ev[0].n), self.ev[1].at(self.ev[1].n)

    def a_down(self):
        w = self.t["w_in"][0][:, COL_AD:COL_AD + RANK].rearrange("(k p) n -> p k n", p=P)
        d = self.param(self.WAD[:, :, :], w)
        yield
        yield
        wait(self.act, d)
        a = self.cact(self.act.activation(self.WADH[:, :, :], self.WAD[:, :, :], ACT.Copy))
        wait(self.dve, a)
        v = self.cdve(self.dve.tensor_tensor(self.WADL[:, :, :], self.WAD[:, :, :],
                                             self.WADH[:, :, :].bitcast(F32), ALU.subtract))
        yield
        wait(self.pe, v)
        for t in range(TT):
            ps = self.bank(t)[:, 0:RANK]
            for k in range(KD):
                a_, b_ = (x[:, k, t * P:(t + 1) * P] for x in (self.XH, self.XL))
                self.pe.matmul(ps, a_, self.WADH[:, k, :], start=k == 0, stop=False)
                self.pe.matmul(ps, a_, self.WADL[:, k, :], start=False, stop=False)
                inst = self.pe.matmul(ps, b_, self.WADH[:, k, :], start=False, stop=k == KD - 1)
            done = self.cpe(inst)
            wait(self.act, done)
            self.release(t, self.cact(self.act.activation(self.AD[:, t, :], ps, ACT.Copy)))
            yield

    def conv_branch(self, ready):
        TOK, dve = self.TA, self.dve
        wait(dve, *ready)
        for t in range(TT):
            cu = self.cdve(dve.tensor_tensor(TOK[:, t, BW:2 * BW], TOK[:, t, BW:2 * BW],
                                             TOK[:, t, 2 * BW:3 * BW], ALU.mult))
        yield
        wait(self.pe, *ready, cu)
        free = None
        for kp in range(4):
            b0, b1 = self.bank((2 * kp) % 4), self.bank((2 * kp + 1) % 4)
            for k in range(2):
                for t in range(TT):
                    o = slice(k * S + t * P, k * S + (t + 1) * P)
                    f = (2 * kp + k) * P
                    self.tr(b0[:, o], TOK[:, t, BW + f:BW + f + P])
                    inst = self.tr(b1[:, o], TOK[:, t, f:f + P])
            done = self.cpe(inst)
            wait(self.act, done, free)
            bt = self.cact(self.act.activation(self.BT[:, :, :], b1, ACT.Copy))
            wait(dve, done)
            tap = lambda j, k: self.V1[:, 66 + j * 8 + 2 * kp + k:67 + j * 8 + 2 * kp + k]
            acc = self.CACC
            for k in range(2):
                v = self.cdve(dve.tensor_scalar(acc[:, k, :], b0[:, k * S:(k + 1) * S], tap(2, k), None, ALU.mult))
            for j in (1, 0):
                s = 2 - j
                wait(dve, v)
                for k in range(2):
                    v = self.cdve(dve.scalar_tensor_tensor(
                        out=acc[:, k, s:S], in0=b0[:, k * S:(k + 1) * S - s], scalar=tap(j, k),
                        in1=acc[:, k, s:S], op0=ALU.mult, op1=ALU.add))
            wait(dve, v, bt)
            y = self.cdve(dve.tensor_tensor(self.CUT[:, :, :], acc[:, :, :], self.BT[:, :, :], ALU.mult))
            self.release((2 * kp) % 4, y)
            self.release((2 * kp + 1) % 4, bt)
            wait(self.act, y)
            a = self.cact(self.act.activation(self.YH[:, 2 * kp:2 * kp + 2, :], self.CUT[:, :, :], ACT.Copy))
            wait(dve, a)
            free = self.cdve(dve.tensor_tensor(self.YL[:, 2 * kp:2 * kp + 2, :], self.CUT[:, :, :],
                                               self.YH[:, 2 * kp:2 * kp + 2, :].bitcast(F32), ALU.subtract))
            yield
            yield

    def attention(self, heads, scores, values, out, dist, slope, scale, sink=None, dh=P, ptile=None, ptT=None, pace=3):
        pe, act, dve = self.pe, self.act, self.dve
        state = {}
        regions = ((slice(0, P), 0), (slice(P, 3 * P), 1))

        def head_scores(h):
            b = h % 2
            ps = self.bank(b)
            q, k = scores(h)
            self.pe.matmul(ps[:, 0:P], q[:, 0:P], k[:, 0:P], start=True, stop=True)
            done = self.cpe(pe.matmul(ps[:, P:3 * P], q[:, P:S], k[:, 0:S], start=True, stop=True))
            pr = ptile[:, b, :]
            wait(dve, done)
            if h >= 2:
                wait(dve, state[h - 2]["transposed"])
            v = self.cdve(dve.scalar_tensor_tensor(out=pr, in0=dist[:, :], scalar=-slope(h) / scale,
                                                   in1=ps[:, 0:3 * P], op0=ALU.mult, op1=ALU.add))
            self.release(b, v)
            wait(dve, v)
            for cols, t in regions:
                m = self.cdve(dve.tensor_reduce(self.RMAX[:, b, t:t + 1], pr[:, cols], AX, ALU.max))
            wait(dve, m)
            if sink is None:
                nm = self.cdve(dve.tensor_scalar(self.NM[:, b, :], self.RMAX[:, b, :], -scale, None, ALU.mult))
            else:
                s = sink[:, h:h + 1]
                mx = self.cdve(dve.tensor_scalar(self.RMAX[:, b, :], self.RMAX[:, b, :], scale, s, ALU.mult, ALU.max))
                wait(dve, mx)
                nm = self.cdve(dve.tensor_scalar(self.NM[:, b, :], self.RMAX[:, b, :], -1.0, None, ALU.mult))
                wait(act, nm)
                es = None
                for t in range(TT):
                    es = self.cact(act.activation(self.ESINK[:, b, t:t + 1], s, ACT.Exp, bias=self.NM[:, b, t:t + 1]))
            wait(act, nm)
            for cols, t in regions:
                e = self.cact(act.activation(pr[:, cols], pr[:, cols], ACT.Exp, bias=self.NM[:, b, t:t + 1],
                                             scale=scale, accum_out=self.RSUM[:, b, t:t + 1]))
            wait(dve, e)
            if sink is not None:
                r = self.cdve(dve.tensor_tensor(self.RSUM[:, b, :], self.RSUM[:, b, :], self.ESINK[:, b, :], ALU.add))
                wait(dve, r)
            r = self.cdve(dve.reciprocal(self.RINV[:, b, :], self.RSUM[:, b, :]))
            wait(dve, r)
            for cols, t in regions:
                n = self.cdve(dve.tensor_scalar(pr[:, cols], pr[:, cols], self.RINV[:, b, t:t + 1], None, ALU.mult))
            state[h] = {"normed": n}

        def head_values(h):
            b = h % 2
            pr, pt = ptile[:, b, :], ptT[:, b, :]
            ps = self.bank(2)
            wait(pe, state[h]["normed"])
            self.tr(ps[:, 0:P], pr[:, 0:P])
            self.tr(ps[:, P:2 * P], pr[:, P:2 * P])
            tr = self.cpe(self.tr(ps[:, 2 * P:3 * P], pr[:, 2 * P:3 * P]))
            state[h]["transposed"] = tr
            wait(act, tr)
            if h >= 2:
                wait(act, state[h - 2]["multiplied"])
            c = self.cact(act.activation(pt, ps[:, 0:3 * P], ACT.Copy))
            self.release(2, c)
            state[h]["copied"] = c

        def head_out(h):
            b = h % 2
            pt = ptT[:, b, :]
            lo_part = slice(0, P) if dh == P else slice(dh * (h % 2), dh * (h % 2) + dh)
            if dh == P or h % 2 == 0:
                self.bank(3)
            o = self.SIDE[lo_part, 3, 0:S]
            wait(pe, state[h]["copied"])
            v0, v1 = values(h)
            self.pe.matmul(o, v0, pt[:, 0:2 * P], start=True, stop=True)
            mu = self.cpe(self.pe.matmul(o[:, P:S], v1, pt[:, 2 * P:3 * P], start=False, stop=True,
                                         skip_group_check=True))
            state[h]["multiplied"] = mu
            if dh != P and h % 2 == 0:
                return None
            tile = h if dh == P else h // 2
            wait(act, mu)
            a = self.cact(act.activation(out[0][:, tile, :], self.SIDE[:, 3, 0:S], ACT.Copy))
            wait(dve, a)
            d = self.cdve(dve.tensor_tensor(out[1][:, tile, :], self.SIDE[:, 3, 0:S],
                                            out[0][:, tile, :].bitcast(F32), ALU.subtract))
            self.release(3, d)
            return d

        head_scores(0)
        yield
        for h in range(heads):
            if h + 1 < heads:
                head_scores(h + 1)
                yield
            head_values(h)
            if pace > 2:
                yield
            head_out(h)
            yield

    def attention1(self, ready):
        TOK = self.TB
        q = yield from self.transposed(lambda k, t: TOK[:, t, k * P:(k + 1) * P], 8, self.QT, ready)
        k = yield from self.transposed(lambda k, t: TOK[:, t, BW + k * P:BW + (k + 1) * P], 8, self.KT, ready)
        wait(self.pe, *q, *k)
        yield from self.attention(
            HEADS, lambda h: (self.QT[:, h, :], self.KT[:, h, :]),
            lambda h: [TOK[:, t, 2 * BW + h * DH:2 * BW + (h + 1) * DH] for t in range(TT)],
            (self.OH, self.OL), self.DIST, lambda h: 2.0 ** (-8.0 * (h + 1) / HEADS), DH ** -0.5,
            ptile=self.PR, ptT=self.PT)

    def transposed(self, src, n, dst, ready, bias=None):
        wait(self.pe, *ready)
        for kp in range(n // 2):
            b = kp % 4
            ps = self.bank(b)
            for k in range(2):
                for t in range(TT):
                    inst = self.tr(ps[:, k * S + t * P:k * S + (t + 1) * P], src(2 * kp + k, t))
            done = self.cpe(inst)
            if bias is None:
                if kp % 2:
                    wait(self.dve, done)
                    last = self.cdve(self.dve.tensor_copy(dst[:, 2 * kp:2 * kp + 2, :], ps))
                else:
                    wait(self.act, done)
                    last = self.cact(self.act.activation(dst[:, 2 * kp:2 * kp + 2, :], ps, ACT.Copy))
            else:
                wait(self.dve, done)
                for k in range(2):
                    last = self.cdve(self.dve.tensor_scalar(dst[:, 2 * kp + k, :], ps[:, k * S:(k + 1) * S],
                                                            bias(2 * kp + k), None, ALU.add))
            self.release(b, last)
            yield
        return [self.cact.at(self.cact.n), self.cdve.at(self.cdve.n)]

    def gla(self, ready):
        pe, act, dve, pool, TOK = self.pe, self.act, self.dve, self.pool, self.TA
        gb = self.param(self.GB[:, :], self.t["gla_b"][0].partition_broadcast(P))
        wu = self.param(self.WUP[:, :], self.t["gla_w_up"][0])
        ps = self.bank(0)
        for t in range(TT):
            inst = self.tr(ps[0:RANK, t * P:(t + 1) * P], self.AD[:, t, :])
        done = self.cpe(inst)
        wait(act, done)
        ad = self.cact(act.activation(self.ADT[:, :], ps[0:RANK, 0:S], ACT.Copy))
        self.release(0, ad)
        yield
        wait(pe, ad, wu)
        wait(dve, gb)
        la = []
        for t in range(TT):
            ps = self.bank(1 + t)
            done = self.cpe(pe.matmul(ps, self.ADT[:, t * P:(t + 1) * P], self.WUP[:, :], start=True, stop=True))
            wait(dve, done)
            z = self.cdve(dve.tensor_tensor(self.LA[:, t, :], ps, self.GB[:, :], ALU.add))
            self.release(1 + t, z)
            wait(dve, z)
            a = self.cdve(dve.scalar_tensor_tensor(out=self.KDEC[:, t, :], in0=self.LA[:, t, :], scalar=-1.0,
                                                       in1=self.LA[:, t, :], op0=ALU.mult, op1=ALU.max))
            wait(act, a)
            e = self.cact(act.activation(self.KDEC[:, t, :], self.KDEC[:, t, :], ACT.Exp, scale=-1.0))
            wait(act, e)
            l = self.cact(act.activation(self.KDEC[:, t, :], self.KDEC[:, t, :], ACT.Ln, bias=1.0))
            wait(dve, l)
            la.append(self.cdve(dve.scalar_tensor_tensor(out=self.LA[:, t, :], in0=self.LA[:, t, :], scalar=0.0,
                                                         in1=self.KDEC[:, t, :], op0=ALU.min, op1=ALU.subtract)))
            yield
        wait(pe, *la)
        for t in range(TT):
            ps = self.bank(1 + t)
            done = self.cpe(pe.matmul(ps, self.LS[:, :], self.LA[:, t, :], start=True, stop=True))
            wait(act, done, la[t])
            e = self.cact(act.activation(self.KDEC[:, t, :], ps, ACT.Exp))
            self.release(1 + t, e)
            wait(dve, e, *ready)
            kd = self.cdve(dve.tensor_tensor(self.KDEC[:, t, :], self.KDEC[:, t, :], TOK[:, t, 512:1024], ALU.mult))
        yield
        wait(act, *ready)
        for t in range(TT):
            sr = self.cact(act.activation(TOK[:, t, 2048:3072], TOK[:, t, 2048:3072], ACT.Silu))
        wait(pe, kd, *ready)
        m0 = self.cdve(dve.memset(self.AT[:, :, :], 0.0))
        wait(dve, m0)
        mask = self.U[:, :].bitcast(U32)
        og = None
        for h in range(GH):
            hk, hv = slice(h * GK, (h + 1) * GK), slice(1024 + h * GV, 1024 + (h + 1) * GV)
            b0, b1 = self.bank(0), self.bank(1)
            for t in range(TT):
                pe.matmul(b0[:, t * P:(t + 1) * P], self.LA[:, t, hk], self.U[:, :], start=True, stop=True)
            bt = self.cpe(self.tr(b1[:, 0:P], TOK[:, 0, hk]))
            self.tr(b1[:, P:S], TOK[:, 1, hk])
            for t in range(TT):
                inst = self.tr(b1[:, S + t * P:S + (t + 1) * P], TOK[:, t, 512 + h * GK:512 + (h + 1) * GK])
            qk = self.cpe(inst)
            wait(act, bt)
            if og is not None:
                wait(act, og)
            eb = self.cact(act.activation(self.EB[:, :], b0[:, 0:S], ACT.Exp))
            en = self.cact(act.activation(self.EN[:, :], b0[:, 0:S], ACT.Exp, scale=-1.0))
            self.release(0, en)
            wait(dve, qk, en)
            if og is not None:
                wait(dve, og)
            qi = self.cdve(dve.scalar_tensor_tensor(out=self.QIN[:, :], in0=b1[:, 0:S], scalar=GK ** -0.5,
                                                    in1=self.EB[:, :], op0=ALU.mult, op1=ALU.mult))
            ki = self.cdve(dve.tensor_tensor(self.KIN[:, :], b1[:, S:2 * S], self.EN[:, :], ALU.mult))
            self.release(1, ki)
            yield
            b2 = self.bank(2)
            wait(pe, ki)
            for t in range(TT):
                inst = pe.matmul(b2[:, t * P:(t + 1) * P], self.KIN[:, t * P:(t + 1) * P],
                                 self.QIN[:, t * P:(t + 1) * P], start=True, stop=True)
            sc = self.cpe(inst)
            b0, b1 = self.bank(0), self.bank(1)
            kv = []
            for n in range(3):
                o = (b0[:, 0:256], b1[:, 0:256], b0[:, 256:512])[n]
                r = slice(64 * (n % 2), 64 * (n % 2) + 64)
                kv.append(self.cpe(pe.matmul(o, self.KDEC[r, n // 2, hk], TOK[r, n // 2, hv], start=True, stop=True)))
            yield
            wait(dve, sc)
            for t in range(TT):
                at = self.cdve(dve.copy_predicated(self.AT[:, t, :], mask, b2[:, t * P:(t + 1) * P]))
            self.release(2, at)
            wait(dve, kv[2])
            s = self.cdve(dve.tensor_copy(self.ST[:, 0, :], b0[:, 0:256]))
            for n, o in ((1, b1[:, 0:256]), (2, b0[:, 256:512])):
                wait(dve, s, kv[n])
                s = self.cdve(dve.scalar_tensor_tensor(
                    out=self.ST[:, n, :], in0=self.ST[:, n - 1, :], scalar=self.EB[:, 64 * n + 63:64 * n + 64],
                    in1=o, op0=ALU.mult, op1=ALU.add))
            self.release(0, s)
            self.release(1, s)
            yield
            b3 = self.bank(3)
            wait(pe, at, s)
            for t in range(TT):
                o = b3[:, t * 256:(t + 1) * 256]
                pe.matmul(o, self.AT[:, t, :], TOK[:, t, hv], start=True, stop=True)
                for n in (2 * t, 2 * t + 1):
                    if n:
                        r = slice(64 * (n % 2), 64 * (n % 2) + 64)
                        inst = pe.matmul(o[r, :], self.QIN[:, 64 * n:64 * n + 64], self.ST[:, n - 1, :],
                                         start=False, stop=True, skip_group_check=True)
            done = self.cpe(inst)
            wait(act, done)
            for t in range(TT):
                q = self.cact(act.activation(self.ST[:, t, :], b3[:, t * 256:(t + 1) * 256], ACT.Square,
                                             accum_out=self.SS[:, t:t + 1]))
            r = self.power(q, self.SS[:, 0:2], 1.0 / GV, self.RSTD[:, 0:2])
            wait(dve, r, sr)
            for t in range(TT):
                og = self.cdve(dve.scalar_tensor_tensor(
                    out=TOK[:, t, hv], in0=b3[:, t * 256:(t + 1) * 256], scalar=self.RSTD[:, t:t + 1],
                    in1=TOK[:, t, 2048 + h * GV:2048 + (h + 1) * GV], op0=ALU.mult, op1=ALU.mult))
            self.release(3, og)
            yield
        yield from self.feature_major_steps(lambda k, t: TOK[:, t, 1024 + k * P:1024 + (k + 1) * P], 8, self.GHI, self.GLO, [og],
                                  weights=lambda k: self.V1[:, 64 + k % 2:65 + k % 2])

    def merge_branch(self, w_gate, gate_col, w_branch, stat, nk, mix, first, rows=None, unroll=False):
        act, dve = self.act, self.dve
        SIG = self.SIG
        half = nk // 2

        def body(i):
            base = {}
            for p in range(2):
                col = i * 2 * PANEL + p * PANEL

                def gate(t, acc, done, p=p, col=col):
                    sig = SIG[:, t, p, :]
                    if rows is None:
                        wait(act, done, self.ev[t].at(self.ev[t].n), self.before[2])
                        base[t] = self.ev[t](act.activation(sig, acc, ACT.Sigmoid))
                    else:
                        wait(dve, done)
                        s = self.ev[t](dve.tensor_tensor(sig, acc, rows(col), ALU.add))
                        wait(act, s)
                        base[t] = self.cact(act.activation(sig, sig, ACT.Sigmoid))

                def branch(t, acc, done, p=p, col=col):
                    sig, m = SIG[:, t, p, :], mix[:, t, ds(col, PANEL)]
                    wait(dve, done, base[t])
                    if first:
                        self.ev[t](dve.tensor_tensor(m, acc, sig, ALU.mult))
                    else:
                        v = self.ev[t](dve.tensor_tensor(sig, acc, sig, ALU.mult))
                        wait(dve, v)
                        self.cdve(dve.tensor_tensor(m, m, sig, ALU.add))

                self.product(w_gate, i * 2 * PANEL + (gate_col + p * PANEL), PANEL, (self.XH, self.XL), [CK] * 4, gate)
                self.product(w_branch, col, PANEL, stat, [half] * 2, branch)

        if unroll:
            self.unrolled(D // PANEL // 2, body)
            return
        self.repeat(D // PANEL // 2, body, self.per(12, 4, cact=0 if rows is None else 4, cdve=0 if first else 4))

    def residual(self, w, stat, groups, last=False):

        def evacuate(col):
            def f(t, acc, done):
                x = self.X[:, t, ds(col, PANEL)]
                wait(self.dve, done)
                self.ev[t](self.dve.tensor_tensor(x, x, acc, ALU.add))
            return f

        def body(i):
            for p in range(2):
                col = i * 2 * PANEL + p * PANEL
                self.product(w, col, PANEL, stat, groups, evacuate(col))

        n = D // PANEL // 2
        self.repeat(n - 1 if last else n, body, self.per(2 * len(groups), 2)) if not last or n > 1 else None
        if last:
            for p in range(2):
                col = (n - 1) * 2 * PANEL + p * PANEL
                self.product(w, col, PANEL, stat, groups, evacuate(col), last=p == 1)
        return [e.at(e.n) for e in self.ev]

    def ffn(self, w_gate, gate_col, w_up, up_col, second):
        act, dve, FF1, FF2 = self.act, self.dve, self.FF1, self.FF2
        n = FF // PANEL

        def products(i, side, turned):
            evacuated = {}

            def gate(t, acc, done):
                wait(act, done, self.ev[t].at(self.ev[t].n), *turned())
                evacuated[t] = self.ev[t](act.activation(FF1[:, t, :], acc, ACT.Copy if second else ACT.Silu))

            def up(t, acc, done):
                wait(dve, done, evacuated[t], *turned())
                if second:
                    self.ev[t](dve.tensor_copy(FF2[:, t, :], acc))
                else:
                    self.ev[t](dve.tensor_tensor(FF2[:, t, :], acc, FF1[:, t, :], ALU.mult))

            self.product(w_gate, i * PANEL + gate_col, PANEL, (self.XH, self.XL), [CK] * 4, gate, side=side)
            self.product(w_up, i * PANEL + up_col, PANEL, (self.XH, self.XL), [CK] * 4, up)

        def turn(i):
            at = i * (PANEL // P)
            ready = [e.at(e.n) for e in self.ev]
            return [lambda kp=kp: (self.turn_conv if second else self.turn_plain)(at, kp, ready) for kp in range(2)]

        def body(i):
            steps = turn(i)
            products(i + 1, {1: steps[0], 4: steps[1]}, lambda: [self.turned])

        products(0, None, lambda: [])
        steps = dict(cpe=2, cact=2, cdve=2) if not second else dict(cpe=2, cact=4, cdve=16)
        self.repeat(n - 1, body, self.per(8, 2, **steps))
        for step in turn(n - 1):
            step()
        return self.cdve.at(self.cdve.n)

    def turn_plain(self, at, kp, ready):
        b = kp
        ps = self.bank(b)
        wait(self.pe, *ready)
        for k in range(2):
            for t in range(TT):
                f = (2 * kp + k) * P
                inst = self.tr(ps[:, k * S + t * P:k * S + (t + 1) * P], self.FF2[:, t, f:f + P])
        self.turned = self.cpe(inst)
        wait(self.act, self.turned)
        hh, hl = (x[:, ds(at + 2 * kp, 2), :] for x in (self.HH, self.HL))
        a = self.cact(self.act.activation(hh, ps[:, :], ACT.Copy))
        wait(self.dve, a)
        self.release(b, self.cdve(self.dve.tensor_tensor(hl, ps[:, :], hh.bitcast(F32), ALU.subtract)))

    def turn_conv(self, at, kp, ready):
        act, dve, G = self.act, self.dve, self.CG
        wait(self.pe, *ready)
        b0, b1 = self.bank(2 * kp), self.bank(2 * kp + 1)
        for k in range(2):
            for t in range(TT):
                f = (2 * kp + k) * P
                o = slice(k * S + t * P, k * S + (t + 1) * P)
                self.tr(b0[:, o], self.FF1[:, t, f:f + P])
                inst = self.tr(b1[:, o], self.FF2[:, t, f:f + P])
        self.turned = self.cpe(inst)
        wait(dve, self.turned, self.cdve.at(self.cdve.n), self.cact.at(self.cact.n))
        vec = lambda j, k: self.V2[:, ds(at + (j * KF + 2 * kp + k), 1)]
        for k in range(2):
            v = self.cdve(dve.tensor_scalar(G[:, k, :], b0[:, k * S:(k + 1) * S], vec(2, k), vec(3, k),
                                            ALU.mult, ALU.add))
        for j in (1, 0):
            s = 2 - j
            wait(dve, v)
            for k in range(2):
                v = self.cdve(dve.scalar_tensor_tensor(
                    out=G[:, k, s:S], in0=b0[:, k * S:(k + 1) * S - s], scalar=vec(j, k), in1=G[:, k, s:S],
                    op0=ALU.mult, op1=ALU.add))
        wait(act, v)
        ge = self.cact(act.activation(G[:, :, :], G[:, :, :], ACT.Gelu))
        wait(dve, ge)
        v = self.cdve(dve.tensor_tensor(G[:, :, :], b1.rearrange("p (k s) -> p k s", k=2), G[:, :, :], ALU.mult))
        self.release(2 * kp, v)
        self.release(2 * kp + 1, v)
        wait(act, v)
        hh, hl = (x[:, ds(at + 2 * kp, 2), :] for x in (self.HH, self.HL))
        a = self.cact(act.activation(hh, G[:, :, :], ACT.Copy))
        wait(dve, a)
        self.cdve(dve.tensor_tensor(hl, G[:, :, :], hh.bitcast(F32), ALU.subtract))

    def ssm_setup(self):
        pe, act, dve, t = self.pe, self.act, self.dve, self.t
        V = lambda n: self.SV[:, n, :]
        (DT, TH, MAG, KK, R1, R2, SIN, COS, ABR, ABI, NR, DEN, RD, Z1, Z2, ZR, ZI, T1, T2) = range(19)
        are, aim = self.V3[:, 18:18 + ST], self.V3[:, 34:34 + ST]
        ld = self.param(self.LDT[:, :], t["ssm_log_dt_2"][0].rearrange("(s q) -> s q", q=2))
        lb = [self.param(self.BRE[:, :, :], t["ssm_b_re_2"][0].rearrange("(s q) p h -> (q p) s h", q=2)),
              self.param(self.BIM[:, :, :], t["ssm_b_im_2"][0].rearrange("(s q) p h -> (q p) s h", q=2))]
        lc = []
        for i, n in enumerate(("ssm_c_re_2", "ssm_c_im_2")):
            for half in range(2):
                lc.append(self.param(self.CRE[:, i, :, 64 * half:64 * half + 64],
                                     t[n][0].rearrange("(u r) h p -> (r h) u p", r=8)))
        yield
        yield
        wait(dve, ld)
        v = self.cdve(dve.tensor_copy(self.SROW[:, :].rearrange("s (q p) -> s q p", q=2),
                                      self.LDT[:, :].unsqueeze(2).to_broadcast([ST, 2, STATE])))
        wait(pe, v)
        ps = self.bank(0)
        done = self.cpe(self.tr(ps[:, 0:ST], self.SROW[:, :]))
        wait(act, done)
        a = self.cact(act.activation(V(DT), ps[:, 0:ST], ACT.Exp))
        self.release(0, a)

        def step(inst):
            tok = self.cdve(inst)
            wait(dve, tok)
            return tok

        tt = lambda o, x, y, op: step(dve.tensor_tensor(V(o), x, y, op))
        ts = lambda o, x, s1, s2, op0, op1: step(dve.tensor_scalar(V(o), x, s1, s2, op0, op1))
        yield
        wait(dve, a)
        tt(TH, V(DT), aim, ALU.mult)
        x = tt(T1, V(DT), are, ALU.mult)
        wait(act, x)
        mag = self.cact(act.activation(V(MAG), V(T1), ACT.Exp))
        big = 1.5 * 2.0 ** 23
        c1, c2 = 6.28125, 0.0019350051879882812
        c3 = TWO_PI - c1 - c2
        for out, shift in ((R1, 0.0), (R2, 0.25)):
            ts(KK, V(TH), 1.0 / TWO_PI, shift, ALU.mult, ALU.add)
            ts(KK, V(KK), big, None, ALU.add, ALU.bypass)
            ts(KK, V(KK), -big, None, ALU.add, ALU.bypass)
            step(dve.scalar_tensor_tensor(out=V(out), in0=V(KK), scalar=-c1, in1=V(TH), op0=ALU.mult, op1=ALU.add))
            step(dve.scalar_tensor_tensor(out=V(out), in0=V(KK), scalar=-c2, in1=V(out), op0=ALU.mult, op1=ALU.add))
            step(dve.scalar_tensor_tensor(out=V(out), in0=V(KK), scalar=-c3, in1=V(out), op0=ALU.mult, op1=ALU.add))
            if shift:
                ts(out, V(out), float(np.pi / 2), None, ALU.add, ALU.bypass)
            r = ts(out, V(out), 3.1415925, -3.1415925, ALU.min, ALU.max)
            yield
        wait(act, r)
        self.cact(act.activation(V(SIN), V(R1), ACT.Sin))
        sc = self.cact(act.activation(V(COS), V(R2), ACT.Sin))
        wait(dve, mag, sc)
        tt(ABR, V(MAG), V(COS), ALU.mult)
        tt(ABI, V(MAG), V(SIN), ALU.mult)
        ts(NR, V(ABR), -1.0, None, ALU.add, ALU.bypass)
        yield
        tt(T1, are, are, ALU.mult)
        tt(T2, aim, aim, ALU.mult)
        tt(DEN, V(T1), V(T2), ALU.add)
        step(dve.reciprocal(V(RD), V(DEN)))
        tt(T1, V(NR), are, ALU.mult)
        tt(T2, V(ABI), aim, ALU.mult)
        tt(T1, V(T1), V(T2), ALU.add)
        tt(ZR, V(T1), V(RD), ALU.mult)
        tt(T1, V(ABI), are, ALU.mult)
        tt(T2, V(NR), aim, ALU.mult)
        tt(T1, V(T1), V(T2), ALU.subtract)
        tt(ZI, V(T1), V(RD), ALU.mult)
        yield
        step(dve.memset(self.BBR[:, :, :], 0.0))
        step(dve.memset(self.BBI[:, :, :], 0.0))
        wait(dve, *lb)
        sc1 = self.SCR[:, 0:256].rearrange("p (s h) -> p s h", h=GROUP)
        sc2 = self.SCR[:, 256:512].rearrange("p (s h) -> p s h", h=GROUP)
        zr, zi = (V(z).unsqueeze(2).to_broadcast([P, ST, GROUP]) for z in (ZR, ZI))
        for dst, x, y, op in ((self.BBR, zr, zi, ALU.subtract), (self.BBI, zi, zr, ALU.add)):
            step(dve.tensor_tensor(sc1, self.BRE[:, :, :], x, ALU.mult))
            step(dve.tensor_tensor(sc2, self.BIM[:, :, :], y, ALU.mult))
            for q in range(2):
                r = slice(64 * q, 64 * q + 64)
                v = step(dve.tensor_tensor(dst[r, :, GROUP * q:GROUP * (q + 1)], sc1[r], sc2[r], op))
            yield
        wait(pe, v)
        b = 0
        for src, dst in ((self.BBR, self.BTR), (self.BBI, self.BTI)):
            ps = self.bank(b)
            for u in range(4):
                inst = self.tr(ps[:, u * P:(u + 1) * P], src[:, 4 * u:4 * u + 4, :])
            done = self.cpe(inst)
            wait(act, done)
            bt = self.cact(act.activation(dst[:, :, :], ps.rearrange("p (u s) -> p u s", u=4), ACT.Copy))
            self.release(b, bt)
            b += 1
            yield
        step(dve.memset(self.CTR[:, :, :], 0.0))
        z = step(dve.memset(self.CTI[:, :, :], 0.0))
        wait(pe, *lc)
        wait(act, z)
        for i, (dst, sign) in enumerate(((self.CTR, 1.0), (self.CTI, -1.0))):
            ps = self.bank(2 + i)
            for u in range(4):
                inst = self.tr(ps[:, u * P:(u + 1) * P], self.CRE[:, i, u, :])
            done = self.cpe(inst)
            wait(act, done)
            for q in range(2):
                r = slice(64 * q, 64 * q + 64)
                src = ps.rearrange("p (s q h) -> p s q h", q=2, h=GROUP)[r, :, q, :]
                ct = self.cact(act.activation(dst[r, :, GROUP * q:GROUP * (q + 1)], src, ACT.Copy, scale=sign))
            self.release(2 + i, ct)
            yield
        self.a_bar = V(ABR), V(ABI)
        yield from self.ssm_powers()

    def ssm_powers(self):
        dve = self.dve

        def step(inst):
            tok = self.cdve(inst)
            wait(dve, tok)
            return tok

        pw = self.POW
        step(dve.tensor_copy(pw[:, 0, :, 0], self.a_bar[0]))
        step(dve.tensor_copy(pw[:, 1, :, 0], self.a_bar[1]))
        n = 1
        while n < BLK:
            lo = lambda ri: pw[:, ri, :, 0:n]
            top = lambda ri: pw[:, ri, :, n - 1:n].to_broadcast([P, ST, n])
            new = lambda ri: pw[:, ri, :, n:2 * n]
            tmp = self.SCR[:, 0:ST * n].rearrange("p (s j) -> p s j", s=ST)
            for ri, x, y, op in ((0, 0, 1, ALU.subtract), (1, 1, 0, ALU.add)):
                step(dve.tensor_tensor(new(ri), lo(0), top(x), ALU.mult))
                step(dve.tensor_tensor(tmp, lo(1), top(y), ALU.mult))
                step(dve.tensor_tensor(new(ri), new(ri), tmp, op))
            n *= 2
            yield
        sv = self.SV
        step(dve.tensor_copy(sv[:, 20, :], self.a_bar[0]))
        step(dve.tensor_copy(sv[:, 21, :], self.a_bar[0]))
        step(dve.tensor_scalar(sv[:, 22, :], self.a_bar[1], -1.0, None, ALU.mult))
        step(dve.tensor_copy(sv[:, 23, :], self.a_bar[1]))
        step(dve.tensor_copy(sv[:, 24, :], pw[:, 0, :, BLK - 1]))
        step(dve.tensor_copy(sv[:, 25, :], pw[:, 0, :, BLK - 1]))
        step(dve.tensor_scalar(sv[:, 26, :], pw[:, 1, :, BLK - 1], -1.0, None, ALU.mult))
        step(dve.tensor_copy(sv[:, 27, :], pw[:, 1, :, BLK - 1]))

    def ssm_half(self, half, u_ready):
        pe, act, dve, XS = self.pe, self.act, self.dve, self.XS
        nt = ST // 2
        s0 = half * nt
        wait(pe, *u_ready)
        for s in range(nt):
            b = s % 4
            ps = self.bank(b)
            u, r = (s0 + s) // 4, slice(32 * (s % 4), 32 * (s % 4) + 32)
            pe.matmul(ps[:, 0:S], self.BTR[r, u, :], self.UT[r, u, :], start=True, stop=True)
            done = self.cpe(pe.matmul(ps[:, S:2 * S], self.BTI[r, u, :], self.UT[r, u, :], start=True, stop=True))
            wait(act, done)
            a = self.cact(act.activation(XS[:, :, s, :], ps.rearrange("p (c t) -> p c t", c=2), ACT.Copy))
            self.release(b, a)
            if s % 2:
                yield
        wait(dve, a)
        X5 = XS[:, :, :, :].rearrange("p c s (b j) -> p c s b j", j=BLK)

        def advance(prev, cur, coef, n):
            row = lambda k, m: self.SV[:, coef + k:coef + k + m, s0:s0 + nt].unsqueeze(3).to_broadcast([P, m, nt, n])
            same, cross = self.STEP[:, 0:2, :, 0:n], self.STEP[:, 2:4, :, 0:n]
            v = self.cdve(dve.tensor_tensor(same, prev, row(0, 2), ALU.mult))
            for c in range(2):
                w = self.cdve(dve.tensor_tensor(cross[:, c:c + 1], prev[:, 1 - c:2 - c], row(2 + c, 1), ALU.mult))
            wait(dve, v)
            v = self.cdve(dve.tensor_tensor(cur, cur, same, ALU.add))
            wait(dve, v)
            v = self.cdve(dve.tensor_tensor(cur, cur, cross, ALU.add))
            wait(dve, v)

        for j in range(BLK - 1):
            advance(X5[:, :, :, :, j], X5[:, :, :, :, j + 1], 20, NB)
            yield
        for b in range(NB - 1):
            advance(X5[:, :, :, b:b + 1, BLK - 1], X5[:, :, :, b + 1:b + 2, BLK - 1], 24, 1)
            if b % 3 == 2:
                yield
        nb, nj, ns = NB - 1, BLK - 1, 4
        tmp = self.SCR[:, 0:ns * nb * nj].rearrange("p (s b j) -> p s b j", b=nb, j=nj)
        for q in range(0, nt, ns):
            for ci in range(2):
                cur = X5[:, ci, q:q + ns, 1:NB, 0:nj]
                for y in range(2):
                    pr = self.POW[:, (ci + y) % 2, s0 + q:s0 + q + ns, 0:nj].unsqueeze(2).to_broadcast([P, ns, nb, nj])
                    last = X5[:, y, q:q + ns, 0:nb, BLK - 1:BLK].to_broadcast([P, ns, nb, nj])
                    t = self.cdve(dve.tensor_tensor(tmp, pr, last, ALU.mult))
                    wait(dve, t)
                    t = self.cdve(dve.tensor_tensor(cur, cur, tmp, ALU.subtract if (ci, y) == (0, 1) else ALU.add))
                    wait(dve, t)
                    yield
            u = (s0 + q) // 4
            wait(pe, t)
            ps = self.bank(u)
            for j in range(4):
                o = ps[32 * j:32 * j + 32, 0:S]
                pe.matmul(o, self.CTR[:, s0 + q + j, :], XS[:, 0, q + j, :], start=True, stop=False)
                inst = pe.matmul(o, self.CTI[:, s0 + q + j, :], XS[:, 1, q + j, :], start=False, stop=True)
            done = self.cpe(inst)
            wait(dve, done)
            y = self.cdve(dve.scalar_tensor_tensor(out=self.UT[:, u, :], in0=self.UT[:, u, :],
                                                   scalar=self.V3[:, 14 + u:15 + u], in1=ps[:, 0:S],
                                                   op0=ALU.mult, op1=ALU.add))
            self.release(u, y)
            self.y_ready = y
            yield

    def ssm_second_half(self):
        act, dve = self.act, self.dve
        yield from self.ssm_half(1, [self.cpe.at(self.cpe.n)])
        wait(act, self.y_ready)
        g = self.cact(act.activation(self.UT[:, :, :], self.UT[:, :, :], ACT.Gelu))
        wait(act, g)
        a = self.cact(act.activation(self.GEH[:, :, :], self.UT[:, :, :], ACT.Copy))
        wait(dve, a)
        g = self.cdve(dve.tensor_tensor(self.GEL[:, :, :], self.UT[:, :, :], self.GEH[:, :, :].bitcast(F32),
                                        ALU.subtract))
        wait(self.pe, g)

    def glu(self):
        act, dve, w = self.act, self.dve, self.t["w_glu_2"][0]
        gb = self.param(self.GBR[:, :], self.t["b_glu_2"][0].partition_broadcast(P))
        wait(dve, gb)
        for p in range(2):
            cols = slice(p * SSMW, (p + 1) * SSMW)

            def evacuate(t, acc, done, cols=cols):
                wait(dve, done)
                self.ev[t](dve.tensor_tensor(self.GLU[:, t, cols], acc, self.GBR[:, cols], ALU.add))
            self.product(w, p * SSMW, SSMW, (self.GEH, self.GEL), [2, 2], evacuate)
        self.glu_ready = [e.at(e.n) for e in self.ev]

    def glu_turned(self):
        act, dve = self.act, self.dve
        wait(act, *self.glu_ready)
        for t in range(TT):
            a = self.cact(act.activation(self.GLU[:, t, SSMW:], self.GLU[:, t, SSMW:], ACT.Sigmoid))
        wait(dve, a)
        for t in range(TT):
            v = self.cdve(dve.tensor_tensor(self.GLU[:, t, 0:SSMW], self.GLU[:, t, 0:SSMW], self.GLU[:, t, SSMW:],
                                            ALU.mult))
        yield
        yield from self.feature_major_steps(lambda k, t: self.GLU[:, t, k * P:(k + 1) * P], 4, self.SH, self.SL, [v])

    def norm_between(self, x_ready):
        row = self.param(self.FW[:, :], self.t["final_norm_w"].partition_broadcast(P))
        r = self.rstd(x_ready, self.RSTD[:, 0:2])
        wait(self.dve, r, row)
        out = []
        for t in range(TT):
            out.append(self.cdve(self.dve.scalar_tensor_tensor(
                out=self.X[:, t, :], in0=self.X[:, t, :], scalar=self.RSTD[:, t:t + 1], in1=self.FW[:, :],
                op0=ALU.mult, op1=ALU.mult)))
        return out

    def build(self):
        act, dve, pe, t = self.act, self.dve, self.pe, self.t
        dve.sem_inc(self.lo.sem, 2 * SLOTS)
        pe.sem_inc(self.mm.sem, PIECES)
        for e in self.ev:
            dve.sem_inc(e.sem, 2)
        self.lo.n, self.mm.n, self.ev[0].n, self.ev[1].n = 2 * SLOTS, PIECES, 2, 2
        xl = [self.param(self.X[:, i, :], t["x"][0, i * P:(i + 1) * P, :]) for i in range(TT)]
        self.const_ready = self.constants()
        for _ in range(AHEAD):
            self.split_piece()
        self.vectors()
        self.norm_to_T(xl, 0)
        w_in = t["w_in"][0]
        r = self.project(w_in, COL_BCU, PANEL, 6, self.TA)
        self.background = [self.conv_branch(r), self.a_down()]
        r = self.project(w_in, COL_QKV, PANEL, 6, self.TB, unroll=True)
        self.finish_background()
        self.settle()
        self.background = [self.attention1(r)]
        r = self.project(w_in, COL_GLA, PANEL, 6, self.TA, unroll=True)
        self.finish_background()
        self.settle()
        self.background = [self.gla(r)]
        self.merge_branch(w_in, COL_MERGE, t["w_br_attn"][0], (self.OH, self.OL), 8, self.MIX, True, unroll=True)
        self.finish_background()
        self.settle()
        self.merge_branch(w_in, COL_MERGE + D, t["w_br_gla"][0], (self.GHI, self.GLO), 8, self.MIX, False)
        self.merge_branch(w_in, COL_MERGE + 2 * D, t["w_br_conv"][0], (self.YH, self.YL), 8, self.MIX, False)
        self.out_and_ffn(self.MIX, t["w_out"][0], KD, t["w_ffn_gate"][0], 0, t["w_ffn_up"][0], 0,
                         t["w_ffn_down"][0], False, False)
        r = self.norm_between([e.at(e.n) for e in self.ev])
        self.settle()
        self.norm_to_T(r, 2 * KD)
        w_in = t["w_in_2"][0]
        self.block2_branches(w_in)
        self.out_and_ffn(self.MG, t["w_out_2"][0], 3 * KD, t["w_up_2"][0], FF, t["w_up_2"][0], 0,
                         t["w_down_2"][0], True, True)
        row = self.param(self.FW[:, :], t["final_norm_g_2"].partition_broadcast(P))
        x = self.rstd([e.at(e.n) for e in self.ev], self.RSTD[:, 0:2])
        wait(dve, x, row)
        for i in range(TT):
            v = self.cdve(dve.scalar_tensor_tensor(out=self.X[:, i, :], in0=self.X[:, i, :],
                                                   scalar=self.RSTD[:, i:i + 1], in1=self.FW[:, :],
                                                   op0=ALU.mult, op1=ALU.mult))
            wait(self.sp, v)
            stored = self.cdma[i](self.sp.dma_start(self.out[0, i * P:(i + 1) * P, :], self.X[:, i, :]))
            wait(self.sp, stored)

    def settle(self):
        steps = [c.at(c.n) for c in (self.cpe, self.cact, self.cdve, self.cpool, *self.ev)] + [self.mm.at(self.mm.n)]
        for e in (self.pe, self.act, self.dve):
            wait(e, *steps)

    def out_and_ffn(self, mixed, w_out, w_norm, w_gate, gate_col, w_up, up_col, w_down, second, last):
        ready = [e.at(e.n) for e in self.ev] + [self.cdve.at(self.cdve.n)]
        self.settle()
        m = self.feature_major(lambda k, t: mixed[:, t, k * P:(k + 1) * P], KD, self.XH, self.XL, ready)
        wait(self.pe, m)
        r = self.residual(w_out, (self.XH, self.XL), [CK] * 4)
        self.settle()
        self.norm_to_T(r, KD if not second else 3 * KD)
        self.settle()
        h = self.ffn(w_gate, gate_col, w_up, up_col, second)
        wait(self.pe, h)
        self.residual(w_down, (self.HH, self.HL), [4] * 8 + [3] * 4, last=last)
        self.settle()

    def columns2(self, w, col, width, wait_act=()):
        def evacuate(t, acc, done):
            wait(self.act, done)
            self.ev[t](self.act.activation(self.TOK2[:, t, col:col + width], acc, ACT.Copy))
        self.product(w, col, width, (self.XH, self.XL), [CK] * 4, evacuate)
        return [e.at(e.n) for e in self.ev]

    def gates2(self, w, first, panel, dst):
        act, dve = self.act, self.dve
        cols = slice(panel * PANEL, (panel + 1) * PANEL)
        col = QKVU2 + first + panel * PANEL
        rows = self.GROW[:, panel % 2, :]
        wait(act, *[e.at(e.n) for e in self.ev])
        gr = self.param(rows, self.t["b_in_2"][0, col:col + PANEL].partition_broadcast(P))

        def evacuate(t, acc, done):
            wait(dve, done, gr)
            s = self.ev[t](dve.tensor_tensor(dst[:, t, cols], acc, rows, ALU.add))
            wait(act, s)
            self.gated = self.cact(act.activation(dst[:, t, cols], dst[:, t, cols], ACT.Sigmoid))
        self.product(w, col, PANEL, (self.XH, self.XL), [CK] * 4, evacuate)

    def branch2(self, w, panel, stat, chunks, gates, add):
        dve = self.dve
        cols = slice(panel * PANEL, (panel + 1) * PANEL)

        def evacuate(t, acc, done):
            g = gates[:, t, cols]
            wait(dve, done, self.gated)
            v = self.ev[t](dve.tensor_tensor(g, acc, g, ALU.mult))
            if add:
                wait(dve, v)
                self.cdve(dve.tensor_tensor(self.MG[:, t, cols], self.MG[:, t, cols], g, ALU.add))
        self.product(w, panel * PANEL, PANEL, stat, chunks, evacuate)

    def block2_branches(self, w):
        t, pe = self.t, self.pe
        self.background = [self.ssm_setup()]
        r = self.columns2(w, 1280, SSMW)
        self.background.append(self.ssm_first_half(r))
        self.columns2(w, 0, PANEL)
        self.columns2(w, PANEL, PANEL)
        r = self.columns2(w, 1024, 256)
        self.background.append(self.attention2(r))
        for p in range(4):
            self.gates2(w, 0, p, self.MG)
        self.finish_background()
        wait(pe, self.cact.at(self.cact.n), self.cdve.at(self.cdve.n))
        self.background = [self.ssm_second_half()]
        for p in range(4):
            self.branch2(t["w_branch_attn_2"][0], p, (self.OH2, self.OL2), [4, 4], self.MG, False)
        self.free_act_dve()
        for p in range(3):
            self.gates2(w, D, p, self.GS)
        self.finish_background()
        self.glu()
        self.background = [self.glu_turned()]
        self.gates2(w, D, 3, self.GS)
        self.finish_background()
        wait(pe, self.cact.at(self.cact.n), self.cdve.at(self.cdve.n))
        for p in range(4):
            self.branch2(t["w_branch_ssm_2"][0], p, (self.SH, self.SL), [2, 2], self.GS, True)

    def free_act_dve(self):
        for e in (self.act, self.dve):
            wait(e, self.cpe.at(self.cpe.n), self.cact.at(self.cact.n), self.cdve.at(self.cdve.n))

    def ssm_first_half(self, ready):
        ucol = 1280
        u = yield from self.transposed(lambda k, t: self.TOK2[:, t, ucol + k * P:ucol + (k + 1) * P], 4, self.UT,
                                       ready, bias=lambda k: self.V3[:, 10 + k:11 + k])
        yield from self.ssm_half(0, [*u])

    def attention2(self, r):
        act, dve, pe, t = self.act, self.dve, self.pe, self.t
        TOK = self.TOK2
        kcol, vcol, ucol = 1024, 1152, 1280
        self.free_act_dve()
        vb = self.param(self.VB[:, :], t["b_in_2"][0, vcol:ucol].partition_broadcast(P))
        sk = self.param(self.SINK[:, :], t["attn_sinks_2"][0].partition_broadcast(P))
        bias = lambda k: self.V3[:, k:k + 1]
        q = yield from self.transposed(lambda k, t: TOK[:, t, k * P:(k + 1) * P], 8, self.QT2, r, bias=bias)
        wait(dve, *r, vb, sk)
        for g in range(KVH2):
            src = TOK[:, :, kcol + g * DH2:kcol + (g + 1) * DH2]
            for half in range(2):
                v = self.cdve(dve.tensor_copy(self.KDUP[:, :, g * P + half * DH2:g * P + (half + 1) * DH2], src))
        vv = self.cdve(dve.tensor_tensor(TOK[:, 0, vcol:ucol], TOK[:, 0, vcol:ucol], self.VB[:, :], ALU.add))
        vv = self.cdve(dve.tensor_tensor(TOK[:, 1, vcol:ucol], TOK[:, 1, vcol:ucol], self.VB[:, :], ALU.add))
        kb = self.SV[:, 28:29, 0:2]
        self.KB = kb
        yield
        wait(pe, v)
        ps = self.bank(0)
        for g in range(KVH2):
            for i in range(TT):
                inst = self.tr(ps[:, g * S + i * P:g * S + (i + 1) * P], self.KDUP[:, i, g * P:(g + 1) * P])
        done = self.cpe(inst)
        for g in range(KVH2):
            for half in range(2):
                rows = slice(half * DH2, (half + 1) * DH2)
                c = self.cact(act.activation(self.SV[rows, 28, g:g + 1], self.V3[g * DH2:(g + 1) * DH2, 8:9], ACT.Copy))
        wait(dve, done, c)
        for g in range(KVH2):
            k = self.cdve(dve.tensor_scalar(self.KT2[:, g, :], ps[:, g * S:(g + 1) * S], self.SV[:, 28, g:g + 1], None,
                                            ALU.add))
        self.release(0, k)
        yield
        wait(pe, *q, k, vv)

        def scores(h):
            r = slice(DH2 * (h % 2), DH2 * (h % 2) + DH2)
            return self.QT2[r, h // 2, :], self.KT2[r, h // (HEADS2 // KVH2), :]

        def values(h):
            c = vcol + DH2 * (h // (HEADS2 // KVH2))
            return [TOK[:, i, c:c + DH2] for i in range(TT)]

        yield from self.attention(HEADS2, scores, values, (self.OH2, self.OL2), self.DIST2,
                                  lambda h: 2.0 ** (-8.0 * (h + 1) / HEADS2), DH2 ** -0.5, sink=self.SINK, dh=DH2,
                                  ptile=self.PR2, ptT=self.PT2, pace=2)


def block_program(nc, tensors, out):
    with ExitStack() as ctx:
        Kernel(nc, ctx, tensors, out).build()


def kernel(**inputs):
    import concourse.bacc as bacc
    from concourse.bass_utils import run_bass_kernel_spmd

    nc = bacc.Bacc("TRN2", target_bir_lowering=False, num_devices=1, dynamic_dma_scratch_size=1024)
    arrays = {f"in_{n}": np.ascontiguousarray(a) for n, a in inputs.items()}
    tensors = {n: nc.dram_tensor(f"in_{n}", a.shape, mybir.dt.from_np(arrays[f"in_{n}"].dtype),
                                 kind="ExternalInput").ap() for n, a in inputs.items()}
    out = nc.dram_tensor("out", (1, S, D), F32, kind="ExternalOutput").ap()
    block_program(nc, tensors, out)
    r = run_bass_kernel_spmd(nc, [arrays], core_ids=[0])
    return r.results[0]["out"]
```

```python
from contextlib import ExitStack

import numpy as np

import concourse.bass as bass
from concourse import mybir

F32 = mybir.dt.float32
F32R = mybir.dt.float32r
U32 = mybir.dt.uint32
ALU = mybir.AluOpType
ACT = mybir.ActivationFunctionType
AX = mybir.AxisListType.X
ds = bass.ds

P = 128
S = 256
TT = S // P
D = 2048
KD = D // P
EPS = 1e-6
NEVER = 1e30
HEADS, DH = 8, 128
GH, GK, GV, RANK, CHUNK, TAU = 4, 128, 256, 16, 64, 16.0
BW = 1024
FF = 5632
KF = FF // P
COL_QKV, COL_GLA, COL_AD = 0, 3072, 6144
COL_BCU = COL_AD + RANK
COL_MERGE = COL_BCU + 3 * BW
HEADS2, DH2, KVH2, WINDOW2 = 16, 64, 2, 128
NG, GROUP, STATE = 32, 16, 64
ST = NG * STATE // P
SSMW = NG * GROUP
QKVU2 = HEADS2 * DH2 + 2 * KVH2 * DH2 + SSMW
BLK = 16
NB = S // BLK
PANEL = 512
CK = 4
SLOTS = 4
AHEAD = 3
PIECES = 4
MIDWAY = 12
TWO_PI = 2.0 * np.pi


class Token:

    def __init__(self, counter, n, loop):
        self.counter, self.n, self.loop = counter, n, loop


class Counter:

    def __init__(self, sem, step=1):
        self.sem, self.step, self.n, self.loop = sem, step, 0, None

    def __call__(self, inst):
        inst.then_inc(self.sem, self.step)
        self.n += self.step
        return Token(self, self.n, self.loop)

    def at(self, n):
        return Token(self, n, self.loop)


class Loop:

    def __init__(self, index, turns, per):
        self.index, self.turns, self.per = index, turns, per


def wait(eng, *tokens):
    for t in tokens:
        if t is None:
            continue
        if t.loop is None:
            value = t.n
        elif t.counter.loop is t.loop:
            value = t.loop.index * t.loop.per[t.counter] + t.n
        else:
            value = (t.loop.turns - 1) * t.loop.per[t.counter] + t.n
        eng.wait_ge(t.counter.sem, value)


class Kernel:
    def __init__(self, nc, ctx, t, out):
        self.nc, self.ctx, self.t, self.out = nc, ctx, t, out
        self.sp, self.pe, self.act, self.dve, self.pool = nc.sync, nc.tensor, nc.scalar, nc.vector, nc.gpsimd
        sem = lambda name: ctx.enter_context(nc.semaphore(name))
        self.tick = sem("loads_started")
        self.loaded = [Counter(sem(f"loaded{i}"), 16) for i in range(4)]
        self.hi = Counter(sem("hi_split"))
        self.lo = Counter(sem("lo_split"))
        self.mm = Counter(sem("chunk_multiplied"))
        self.ev = [Counter(sem(f"evacuated{i}")) for i in range(TT)]
        self.cpe = Counter(sem("tensor_step"))
        self.cact = Counter(sem("scalar_step"))
        self.cdve = Counter(sem("vector_step"))
        self.cpool = Counter(sem("pool_step"))
        self.cdma = [Counter(sem(f"param_load{i}"), 16) for i in range(16)]
        self.ndma = 0
        self.counters = self.loaded + [self.hi, self.lo, self.mm] + self.ev + [
            self.cpe, self.cact, self.cdve, self.cpool]
        self.g = 0
        self.gs = 0
        self.background = []
        self.dense = False
        self.panel = 0
        self.loop = None
        self.base = (nc.sbuf_base + 63) // 64 * 64
        self.side_free = [[] for _ in range(4)]
        self.memory()

    def sb(self, name, shape, offset, dtype=F32):
        return self.nc.alloc_sbuf_tensor_at(name, shape, dtype, offset=self.base + offset)

    def memory(self):
        K = 1024
        sb = self.sb
        self.RAW = sb("weights", [P, 4, CK * PANEL], 0)
        self.HI = sb("weights_hi", [P, PIECES, 2 * PANEL], 32 * K, F32R)
        self.LO = sb("weights_lo", [P, PIECES, 2 * PANEL], 48 * K, F32R)
        self.X = sb("x", [P, TT, D], 64 * K)
        off = 80 * K

        def small(name, shape, dtype=F32):
            nonlocal off
            t = sb(name, shape, off, dtype)
            off += (int(np.prod(shape[1:])) * 4 + 31) // 32 * 32
            return t

        self.IDENT = small("identity", [P, P])
        self.U = small("cumsum_in_chunk", [P, P])
        self.LS = small("suffix_in_chunk", [P, P])
        self.DIST = small("distance", [P, 3 * P])
        self.DIST2 = small("distance_in_window", [P, 3 * P])
        self.V1 = small("vectors1", [P, 90])
        self.V2 = small("vectors2", [P, 4 * KF])
        self.V3 = small("vectors3", [P, 66])
        self.SS = small("square_sums", [P, 2])
        self.MS = small("mean_squares", [P, 2])
        self.SQ = small("square_sums_by_panel", [P, 2, TT, D // PANEL])
        self.RSTD = small("rstd", [P, 2])
        self.RX = small("rstd_first", [P, 2])
        self.GR = small("rstd_gla", [P, 2])
        self.NHALF = small("minus_half", [P, 2])
        self.ADT = small("a_downT", [RANK, S])
        self.RMAX = small("row_max", [P, 2, 2])
        self.RSUM = small("row_sum", [P, 2, 2])
        self.RINV = small("row_inverse", [P, 2, 2])
        self.SINK = small("sinks", [P, HEADS2])
        self.NM = small("minus_max", [P, 2, 2])
        self.ESINK = small("exp_sink", [P, 2, 2])
        assert off <= 88 * K, off
        A = 88 * K
        self.XH = sb("xT_hi", [P, KD, S], A, F32R)
        self.XL = sb("xT_lo", [P, KD, S], A + 16 * K, F32R)
        R = A + 32 * K
        self.JUNK = sb("squares", [P, PANEL], R + 100 * K)
        self.MH = sb("mixedT_hi", [P, KD, S], R + 64 * K, F32R)
        self.ML = sb("mixedT_lo", [P, KD, S], R + 80 * K, F32R)
        self.TA = sb("projected_a", [P, TT, 3 * BW], R)
        self.TB = sb("projected_b", [P, TT, 3 * BW], R + 24 * K)
        self.YH = sb("convT_hi", [P, 8, S], R + 48 * K, F32R)
        self.YL = sb("convT_lo", [P, 8, S], R + 56 * K, F32R)
        self.QT = sb("qT", [P, HEADS, S], R + 64 * K)
        self.KT = sb("kT", [P, HEADS, S], R + 72 * K)
        self.OH = sb("attnT_hi", [P, 8, S], R + 80 * K, F32R)
        self.OL = sb("attnT_lo", [P, 8, S], R + 88 * K, F32R)
        self.MIX = sb("mixed", [P, TT, D], R + 24 * K)
        self.SIG = sb("gates", [P, TT, 2, PANEL], R + 40 * K)
        self.GHI = sb("glaT_hi", [P, 8, S], R + 64 * K, F32R)
        self.GLO = sb("glaT_lo", [P, 8, S], R + 72 * K, F32R)
        self.WAD = sb("w_a_down", [P, KD, RANK], R + 64 * K)
        self.WADH = sb("w_a_down_hi", [P, KD, RANK], R + 65 * K, F32R)
        self.WADL = sb("w_a_down_lo", [P, KD, RANK], R + 66 * K, F32R)
        T = R + 96 * K
        self.BT = sb("b_gateT", [P, 2, S], T)
        self.CUT = sb("cuT", [P, 2, S], T + 2 * K)
        self.CACC = sb("conv_acc", [P, 2, S], T + 4 * K)
        self.PR = sb("probabilities", [P, 2, 3 * P], T)
        self.PT = sb("probabilitiesT", [P, 2, 3 * P], T + 3 * K)
        self.LA = sb("log_a", [P, TT, 512], R + 64 * K)
        self.KDEC = sb("k_decayed", [P, TT, 512], R + 68 * K)
        self.GB = sb("gla_b_rows", [P, 512], R + 72 * K)
        self.WUP = sb("gla_w_up", [RANK, 512], R + 75 * K)
        self.ST = sb("gla_state", [P, 3, 256], R + 77 * K)
        self.EB = sb("exp_b", [P, S], T)
        self.EN = sb("exp_minus_b", [P, S], T + K)
        self.QIN = sb("q_in", [P, S], T + 2 * K)
        self.KIN = sb("k_in", [P, S], T + 3 * K)
        self.AT = sb("aT", [P, TT, P], T + 4 * K)
        self.HH = sb("hiddenT_hi", [P, KF, S], R, F32R)
        self.HL = sb("hiddenT_lo", [P, KF, S], R + 44 * K, F32R)
        self.CG = sb("conv_gelu", [P, 2, S], R + 96 * K)
        self.FW = sb("norm_rows", [P, D], R + 88 * K)
        self.TOK2 = sb("projected2", [P, TT, QKVU2], R)
        self.QT2 = sb("qT2", [P, 8, S], R + 14 * K)
        self.OH2 = sb("attn2T_hi", [P, 8, S], R + 14 * K, F32R)
        self.OL2 = sb("attn2T_lo", [P, 8, S], R + 22 * K, F32R)
        self.KT2 = sb("kT2", [P, KVH2, S], R + 30 * K)
        self.KDUP = sb("k_twice", [P, TT, KVH2 * P], R + 32 * K)
        self.VB = sb("v_bias_rows", [P, KVH2 * DH2], R + 34 * K)
        self.PR2 = sb("probabilities2", [P, 2, 3 * P], R + 35 * K)
        self.PT2 = sb("probabilitiesT2", [P, 2, 3 * P], R + 38 * K)
        self.UT = sb("uT", [P, 4, S], R + 41 * K)
        self.GEL = sb("ssm_geluT_lo", [P, 4, S], R + 41 * K, F32R)
        self.GEH = sb("ssm_geluT_hi", [P, 4, S], R + 30 * K, F32R)
        self.XS = sb("ssm_states", [P, 2, ST // 2, S], R + 45 * K)
        self.STEP = sb("scan_step", [P, 4, ST // 2, NB], R + 61 * K)
        self.SCR = sb("ssm_scratch", [P, 1024], R + 63 * K)
        self.POW = sb("a_powers", [P, 2, ST, BLK], R + 67 * K)
        self.BTR = sb("bbT_re", [P, 4, P], R + 69 * K)
        self.BTI = sb("bbT_im", [P, 4, P], R + 71 * K)
        self.CTR = sb("cT_re", [P, ST, 2 * GROUP], R + 73 * K)
        self.CTI = sb("cT_im", [P, ST, 2 * GROUP], R + 75 * K)
        self.SV = sb("ssm_vectors", [P, 32, ST], R + 77 * K)
        self.MG = sb("merged", [P, TT, D], R + 79 * K)
        self.GROW = sb("gate_bias_rows", [P, 2, PANEL], R + 95 * K)
        self.BRE = sb("b_re", [P, ST, GROUP], R + 14 * K)
        self.BIM = sb("b_im", [P, ST, GROUP], R + 15 * K)
        self.BBR = sb("bb_re", [P, ST, 2 * GROUP], R + 16 * K)
        self.BBI = sb("bb_im", [P, ST, 2 * GROUP], R + 18 * K)
        self.CRE = sb("c_twice", [P, 2, 4, P], R + 20 * K)
        self.SROW = sb("log_dt_rows", [ST, P], R + 24 * K)
        self.LDT = sb("log_dt", [ST, 2], R + 24 * K + 512)
        self.GS = sb("ssm_gates", [P, TT, D], R)
        self.GLU = sb("glu", [P, TT, 2 * SSMW], R + 16 * K)
        self.GBR = sb("b_glu_rows", [P, 2 * SSMW], R + 24 * K)
        self.SH = sb("ssmT_hi", [P, 4, S], R + 53 * K, F32R)
        self.SL = sb("ssmT_lo", [P, 4, S], R + 57 * K, F32R)
        self.MH2 = sb("merged2T_hi", [P, KD, S], R + 16 * K, F32R)
        self.ML2 = sb("merged2T_lo", [P, KD, S], R + 32 * K, F32R)
        self.FF1 = sb("ffn_gate", [P, TT, PANEL], R + 88 * K)
        self.FF2 = sb("ffn_hidden", [P, TT, PANEL], R + 92 * K)
        psum = lambda n: self.ctx.enter_context(self.nc.psum_tensor(n, [P, 4, PANEL], F32))
        self.ACC, self.SIDE = psum("panels"), psum("side")
        self.R = R

    def repeat(self, turns, body, per):
        per = {c: per.get(c, 0) for c in self.counters}
        start = {c: c.n for c in self.counters}
        nc = self.nc
        with nc.Fori(0, turns, engines=[e.engine for e in (self.act, self.pe, self.dve, self.sp)]) as i:
            loop = self.loop = Loop(i, turns, per)
            for c in self.counters:
                c.loop = loop
            for b in range(4):
                self.side_free[b] = [self.cact.at(self.cact.n), self.cdve.at(self.cdve.n)]
            self.before = [c.at(c.n) for c in (self.cpe, self.cact, self.cdve)]
            body(i)
        self.loop = None
        for c in self.counters:
            grown = c.n - start[c]
            assert grown == per[c], (c.sem, grown, per[c])
            c.loop = None
            c.n = start[c] + turns * grown
        chunks = per[self.mm]
        for b in range(4):
            self.side_free[b] = [self.cact.at(self.cact.n), self.cdve.at(self.cdve.n)]
        self.g += (turns - 1) * chunks
        self.gs += (turns - 1) * chunks
        self.panel += (turns - 1) * per[self.ev[0]]

    def per(self, chunks, panels, **more):
        p = {c: 16 * chunks // 4 for c in self.loaded}
        p.update({self.hi: 2 * chunks, self.lo: 2 * chunks, self.mm: 2 * chunks,
                  self.ev[0]: panels, self.ev[1]: panels})
        p.update({{"cpe": self.cpe, "cact": self.cact, "cdve": self.cdve}[k]: v for k, v in more.items()})
        return p

    def load_chunk(self, w, k0, nk, col, width):
        g = self.g // 2
        slot = g % SLOTS
        wait(self.sp, self.lo.at(2 * g + 2))
        self.sp.sem_inc(self.tick, 1)
        src = w[k0 * P:(k0 + nk) * P, ds(col, width)].rearrange("(k p) n -> p k n", p=P)
        dst = self.RAW[:, slot, :].rearrange("p (k n) -> p k n", n=PANEL)
        dst = dst[:, 0:CK:2, 0:width] if nk == 2 else dst[:, 0:nk, 0:width]
        self.loaded[slot](self.sp.dma_start(dst, src))

    def split_piece(self, size=2):
        g = self.gs
        slot, part, ring = g // 2 % SLOTS, g % 2, g % PIECES
        n = size * PANEL
        raw = self.RAW[:, slot, part * 2 * PANEL:part * 2 * PANEL + n]
        if part == 0:
            wait(self.act, self.loaded[slot].at(16 * (g // 2 // SLOTS + 1)))
        if g >= PIECES or self.loop:
            wait(self.act, self.mm.at(g + 1))
        self.hi(self.act.activation(self.HI[:, ring, 0:n], raw, ACT.Copy))
        wait(self.dve, self.hi.at(g + 1))
        self.lo(self.dve.tensor_tensor(self.LO[:, ring, 0:n], raw, self.HI[:, ring, 0:n].bitcast(F32), ALU.subtract))
        self.gs += 1

    def product(self, w, col, width, stat, chunks, evacuate, last=False, side=None, after=2):
        p = self.panel
        hi, lo = stat
        k0 = 0
        total = sum(chunks)
        sizes = [n for nk in chunks for n in ((nk + 1) // 2, nk // 2)] + [after] * AHEAD
        for c, nk in enumerate(chunks):
            self.load_chunk(w, k0, nk, col, width)
            for part, np_ in enumerate(((nk + 1) // 2, nk // 2)):
                g, ring = self.g, self.g % PIECES
                self.g += 1
                if not last or 2 * c + part + AHEAD < 2 * len(chunks):
                    self.split_piece(sizes[2 * c + part + AHEAD])
                wait(self.pe, self.lo.at(g + 1 + 2 * SLOTS))
                for t in range(TT):
                    if k0 == 0:
                        wait(self.pe, self.ev[t].at(p + 1))
                    acc = self.ACC[:, (p % 2) * TT + t, 0:width]
                    for k in range(np_):
                        a, b = (x[:, k0 + k, t * P:(t + 1) * P] for x in (hi, lo))
                        wh, wl = (x[:, ring, k * PANEL:k * PANEL + width] for x in (self.HI, self.LO))
                        first, final = k0 + k == 0, k0 + k == total - 1
                        self.pe.matmul(acc, a, wh, start=first, stop=False)
                        self.pe.matmul(acc, a, wl, start=False, stop=False)
                        inst = self.pe.matmul(acc, b, wh, start=False, stop=final)
                done = self.mm(inst)
                k0 += np_
                if side and 2 * c + part in side:
                    side[2 * c + part]()
                if self.loop is None and self.background:
                    for _ in range(1 + (self.dense and self.g % 4 == 0)):
                        if self.background and next(self.background[0], self) is self:
                            self.background.pop(0)
        self.panel += 1
        for t in range(TT):
            evacuate(t, self.ACC[:, (p % 2) * TT + t, 0:width], done)

    def run(self, work):
        while True:
            try:
                next(work)
            except StopIteration as end:
                return end.value

    def finish_background(self):
        for work in self.background:
            self.run(work)
        self.background = []

    def unrolled(self, turns, body):
        for i in range(turns):
            self.before = [c.at(c.n) for c in (self.cpe, self.cact, self.cdve)]
            body(i)

    def bank(self, b):
        wait(self.pe, *self.side_free[b])
        self.side_free[b] = []
        return self.SIDE[:, b, :]

    def release(self, b, *tokens):
        self.side_free[b] = list(tokens)

    def param(self, dst, src):
        c = self.cdma[self.ndma % len(self.cdma)]
        self.ndma += 1
        if c.n:
            wait(self.act, c.at(c.n))
        return c(self.act.dma_start(dst, src))

    def tr(self, out, in_):
        return self.pe.transpose(out, in_, self.IDENT[0:in_.shape[0], 0:in_.shape[0]])

    def feature_major(self, src, nk, hi, lo, ready, weights=None, at=0):
        wait(self.pe, *ready)
        last = None
        for kp in range(nk // 2):
            b = kp % 4
            ps = self.bank(b)
            for k in range(2):
                for t in range(TT):
                    inst = self.tr(ps[:, k * S + t * P:k * S + (t + 1) * P], src(2 * kp + k, t))
            done = self.cpe(inst)
            wait(self.act, done)
            if weights is None:
                a = self.cact(self.act.activation(hi[:, ds(at + 2 * kp, 2), :], ps[:, :], ACT.Copy))
                wait(self.dve, a)
                last = self.cdve(self.dve.tensor_tensor(lo[:, ds(at + 2 * kp, 2), :], ps[:, :],
                                                        hi[:, ds(at + 2 * kp, 2), :].bitcast(F32), ALU.subtract))
            else:
                for k in range(2):
                    w = weights(2 * kp + k)
                    a = self.cact(self.act.activation(hi[:, at + 2 * kp + k, :], ps[:, k * S:(k + 1) * S],
                                                      ACT.Copy, scale=w))
                for k in range(2):
                    w = weights(2 * kp + k)
                    wait(self.dve, a)
                    last = self.cdve(self.dve.scalar_tensor_tensor(
                        out=lo[:, at + 2 * kp + k, :], in0=ps[:, k * S:(k + 1) * S], scalar=w,
                        in1=hi[:, at + 2 * kp + k, :].bitcast(F32), op0=ALU.mult, op1=ALU.subtract))
            self.release(b, last)
            yield
        return last

    def constants(self):
        pool = self.pool

        def c(inst):
            tok = self.cpool(inst)
            wait(pool, tok)
            return tok

        c(pool.memset(self.IDENT[:, :], 0.0))
        c(pool.memset(self.U[:, :], 1.0 / TAU))
        c(pool.memset(self.LS[:, :], 1.0 / TAU))
        c(pool.memset(self.NHALF[:, :], -0.5))
        c(pool.iota(self.DIST[:, 0:P], [[-1, P]], base=0, channel_multiplier=1, allow_small_or_imprecise_dtypes=True))
        c(pool.iota(self.DIST[:, P:3 * P], [[-1, S]], base=P, channel_multiplier=1,
                    allow_small_or_imprecise_dtypes=True))

        def select(m, pattern, base, cm, op, fill, like=None):
            return c(pool.affine_select(out=m, in_=m if like is None else like, compare_op=op, fill=fill,
                                        base=base, pattern=pattern, channel_multiplier=cm))

        select(self.IDENT[:, :], [[-1, P]], 0, 1, ALU.not_equal, 1.0)
        select(self.U[:, :], [[1, P]], 0, -1, ALU.is_ge, 0.0)
        select(self.LS[:, :], [[-1, P]], 0, 1, ALU.is_gt, 0.0)
        select(self.DIST[:, 0:P], [[-1, P]], 0, 1, ALU.is_ge, NEVER)
        select(self.DIST[:, P:3 * P], [[-1, S]], P, 1, ALU.is_ge, NEVER)
        select(self.U[0:64, 64:P], [[0, 64]], -1, 0, ALU.is_ge, 0.0)
        select(self.LS[64:P, 0:64], [[0, 64]], -1, 0, ALU.is_ge, 0.0)
        c(pool.tensor_copy(self.DIST2[:, 0:P], self.DIST[:, 0:P]))
        return select(self.DIST2[:, P:3 * P], [[1, S]], WINDOW2 - 1 - P, -1, ALU.is_ge, NEVER,
                      like=self.DIST[:, P:3 * P])

    def vectors(self):
        t = self.t
        rows = [self.sb(f"rows{i}", [P, P], 90 * 1024 + self.R + 512 * i) for i in range(4)]
        loads = [[], [], [], []]
        put = lambda i, at, n, src: loads[i].append(self.param(rows[i][at:at + n, :], src))
        vec = lambda x: x.rearrange("(k p) -> k p", p=P)
        at = 0
        for n in ("norm1_w", "norm2_w", "attn_norm_g_2", "ffn_norm_g_2"):
            put(0, at, KD, vec(t[n][0]))
            at += KD
        put(0, at, 2, vec(t["gla_norm_w"][0]))
        put(0, at + 2, 24, t["conv_w"][0].rearrange("j (k p) -> (j k) p", p=P))

        def turn(i, dst, n):
            wait(self.pe, *loads[i], self.const_ready)
            ps = self.bank(i)
            done = self.cpe(self.tr(ps[:, 0:n], rows[i][0:n, :]))
            wait(self.act, done)
            ready = self.cact(self.act.activation(dst, ps[:, 0:n], ACT.Copy))
            self.release(i, ready)
            wait(self.dve, ready)

        def rest():
            cw = t["conv_w_2"][0].rearrange("j (k p) -> (j k) p", p=P)
            put(1, 0, 88, cw[0:88, :])
            put(2, 0, 44, cw[88:132, :])
            put(2, 44, 44, vec(t["conv_b_2"][0]))
            put(3, 0, 14, t["b_in_2"][0, 0:QKVU2].rearrange("(k p) -> k p", p=P))
            put(3, 14, 4, vec(t["ssm_d_2"][0]))
            put(3, 18, ST, t["ssm_a_re_2"][0].rearrange("(s q) p -> s (q p)", q=2))
            put(3, 34, ST, t["ssm_a_im_2"][0].rearrange("(s q) p -> s (q p)", q=2))
            for _ in range(3):
                yield
            for i, (dst, n) in enumerate(((self.V2[:, 0:88], 88), (self.V2[:, 88:176], 88), (self.V3[:, 0:50], 50))):
                turn(i + 1, dst, n)
                yield

        turn(0, self.V1[:, :], 90)
        return rest()

    def power(self, ready, sums, scale, out):
        wait(self.dve, ready)
        d = self.cdve(self.dve.tensor_scalar(self.MS[:, 0:2], sums, scale, EPS, ALU.mult, ALU.add))
        wait(self.pool, d)
        return self.cpool(self.pool.tensor_tensor(out, self.MS[:, 0:2], self.NHALF[:, 0:2], ALU.pow))

    def squares(self, which, p, ready):
        wait(self.act, *ready)
        for t in range(TT):
            a = self.cact(self.act.activation(self.JUNK[:, :], self.X[:, t, p * PANEL:(p + 1) * PANEL], ACT.Square,
                                              accum_out=self.SQ[:, which, t, p:p + 1]))
            wait(self.act, a)
        return a

    def turn_x(self, p, ready, w0):
        n = PANEL // P
        return self.feature_major(
            lambda k, t: self.X[:, t, (n * p + k) * P:(n * p + k + 1) * P], n, self.XH, self.XL, ready,
            weights=lambda k: self.V1[:, w0 + n * p + k:w0 + n * p + k + 1], at=n * p)

    def set_rstd(self, sums):
        r = self.power(sums, self.SS[:, 0:2], 1.0 / D, self.RSTD[:, 0:2])
        wait(self.act, r)
        wait(self.dve, r)

    def first_norm(self, x_ready):
        for p in (2, 3):
            last = yield from self.turn_x(p, x_ready, 0)
            wait(self.pe, last)
            self.squares(0, 2 * p - 4, x_ready)
            sq = self.squares(0, 2 * p - 3, x_ready)
        wait(self.dve, sq)
        self.set_rstd(self.cdve(self.dve.tensor_reduce(self.SS[:, 0:2], self.SQ[:, 0, :, :], AX, ALU.add)))

    def norm_panel(self, p, ready, turn=None, rows=False):
        dve = self.dve
        sq = self.squares(0, p, ready)
        if rows:
            cols = slice(p * PANEL, (p + 1) * PANEL)
            wait(dve, self.rows_ready, sq)
            for t in range(TT):
                v = self.cdve(dve.tensor_tensor(self.X[:, t, cols], self.X[:, t, cols], self.FW[:, cols], ALU.mult))
            yield
            ready = [v]
            if turn is not None:
                sq = self.squares(1, p, ready)
        if turn is not None:
            last = yield from self.turn_x(p, ready, turn)
            wait(self.pe, last)
        if p == D // PANEL - 1:
            wait(dve, sq)
            v = self.cdve(dve.tensor_reduce(self.SS[:, 0:2], self.SQ[:, 0, :, :], AX, ALU.add))
            if turn is None or not rows:
                self.set_rstd(v)
                return
            r = self.power(v, self.SS[:, 0:2], 1.0 / D, self.RX[:, 0:2])
            yield
            wait(dve, r)
            v = self.cdve(dve.tensor_reduce(self.SS[:, 0:2], self.SQ[:, 1, :, :], AX, ALU.add))
            for _ in range(2):
                wait(dve, v)
                v = self.cdve(dve.tensor_tensor(self.SS[:, 0:2], self.SS[:, 0:2], self.RX[:, 0:2], ALU.mult))
            r = self.power(v, self.SS[:, 0:2], 1.0 / D, self.RSTD[:, 0:2])
            wait(dve, r, self.cpe.at(self.cpe.n), sq)
            v = self.cdve(dve.tensor_tensor(self.RSTD[:, 0:2], self.RSTD[:, 0:2], self.RX[:, 0:2], ALU.mult))
            wait(self.act, v)
            wait(dve, v)
            for t in range(TT):
                yield
                self.cdve(dve.tensor_scalar(self.X[:, t, :], self.X[:, t, :], self.RX[:, t:t + 1], None, ALU.mult))

    def norm_rows(self, src):
        self.free_act_dve()
        self.rows_ready = self.param(self.FW[:, :], src.partition_broadcast(P))

    def project(self, w, col0, width, panels, dst, unroll):

        def body(i, first=0):
            for p in range(first * 2, first * 2 + 2):
                def evacuate(t, acc, done, p=p):
                    o = dst[:, t, ds(i * 2 * width + p * width, width)]
                    if t == 0:
                        wait(self.act, done)
                        self.ev[0](self.act.activation(o, acc, ACT.Copy, scale=self.RSTD[:, t:t + 1]))
                    else:
                        wait(self.dve, done)
                        self.ev[1](self.dve.tensor_scalar(o, acc, self.RSTD[:, t:t + 1], None, ALU.mult))
                self.product(w, i * 2 * width + (col0 + p * width), width, (self.XH, self.XL), [CK] * 4, evacuate)
        self.unrolled(unroll, body)
        if unroll < panels // 2:
            self.finish_background()
            self.repeat(panels // 2 - unroll, lambda i: body(i, unroll), self.per(8, 2))
        return self.ev[0].at(self.ev[0].n), self.ev[1].at(self.ev[1].n)

    def a_down(self):
        wait(self.act, self.wad)
        a = self.cact(self.act.activation(self.WADH[:, :, :], self.WAD[:, :, :], ACT.Copy))
        wait(self.dve, a)
        v = self.cdve(self.dve.tensor_tensor(self.WADL[:, :, :], self.WAD[:, :, :],
                                             self.WADH[:, :, :].bitcast(F32), ALU.subtract))
        yield
        wait(self.pe, v)
        ps = self.bank(0)[0:RANK, 0:S]
        for k in range(KD):
            self.pe.matmul(ps, self.WADH[:, k, :], self.XH[:, k, :], start=k == 0, stop=False)
            self.pe.matmul(ps, self.WADL[:, k, :], self.XH[:, k, :], start=False, stop=False)
            inst = self.pe.matmul(ps, self.WADH[:, k, :], self.XL[:, k, :], start=False, stop=k == KD - 1)
            if k % 4 == 3 and k < KD - 1:
                yield
        done = self.cpe(inst)
        yield
        wait(self.act, done)
        self.adt_ready = self.cact(self.act.activation(self.ADT[:, :], ps, ACT.Copy))
        self.release(0, self.adt_ready)

    def conv_branch(self, ready):
        TOK, dve = self.TA, self.dve
        wait(dve, *ready)
        for t in range(TT):
            cu = self.cdve(dve.tensor_tensor(TOK[:, t, BW:2 * BW], TOK[:, t, BW:2 * BW],
                                             TOK[:, t, 2 * BW:3 * BW], ALU.mult))
        yield
        wait(self.pe, *ready, cu)
        free = None
        for kp in range(4):
            b0, b1 = self.bank((2 * kp) % 4), self.bank((2 * kp + 1) % 4)
            for k in range(2):
                for t in range(TT):
                    o = slice(k * S + t * P, k * S + (t + 1) * P)
                    f = (2 * kp + k) * P
                    self.tr(b0[:, o], TOK[:, t, BW + f:BW + f + P])
                    inst = self.tr(b1[:, o], TOK[:, t, f:f + P])
            done = self.cpe(inst)
            wait(self.act, done, free)
            bt = self.cact(self.act.activation(self.BT[:, :, :], b1, ACT.Copy))
            wait(dve, done)
            tap = lambda j, k: self.V1[:, 66 + j * 8 + 2 * kp + k:67 + j * 8 + 2 * kp + k]
            acc = self.CACC
            for k in range(2):
                v = self.cdve(dve.tensor_scalar(acc[:, k, :], b0[:, k * S:(k + 1) * S], tap(2, k), None, ALU.mult))
            yield
            for j in (1, 0):
                s = 2 - j
                wait(dve, v)
                for k in range(2):
                    v = self.cdve(dve.scalar_tensor_tensor(
                        out=acc[:, k, s:S], in0=b0[:, k * S:(k + 1) * S - s], scalar=tap(j, k),
                        in1=acc[:, k, s:S], op0=ALU.mult, op1=ALU.add))
            wait(dve, v, bt)
            y = self.cdve(dve.tensor_tensor(self.CUT[:, :, :], acc[:, :, :], self.BT[:, :, :], ALU.mult))
            self.release((2 * kp) % 4, y)
            self.release((2 * kp + 1) % 4, bt)
            wait(self.act, y)
            a = self.cact(self.act.activation(self.YH[:, 2 * kp:2 * kp + 2, :], self.CUT[:, :, :], ACT.Copy))
            wait(dve, a)
            free = self.cdve(dve.tensor_tensor(self.YL[:, 2 * kp:2 * kp + 2, :], self.CUT[:, :, :],
                                               self.YH[:, 2 * kp:2 * kp + 2, :].bitcast(F32), ALU.subtract))
            yield
            yield

    def attention(self, heads, scores, values, out, dist, slope, scale, sink=None, dh=P, ptile=None,
                  ptT=None, interlude=None):
        pe, act, dve = self.pe, self.act, self.dve
        state = {}
        regions = ((slice(0, P), 0), (slice(P, 3 * P), 1))

        def head_scores(h):
            b = h % 2
            ps = self.bank(b)
            q, k = scores(h)
            self.pe.matmul(ps[:, 0:P], q[:, 0:P], k[:, 0:P], start=True, stop=True)
            done = self.cpe(pe.matmul(ps[:, P:3 * P], q[:, P:S], k[:, 0:S], start=True, stop=True))
            pr = ptile[:, b, :]
            wait(dve, done)
            if h >= 2:
                wait(dve, state[h - 2]["transposed"])
            v = self.cdve(dve.scalar_tensor_tensor(out=pr, in0=dist[:, :], scalar=-slope(h) / scale,
                                                   in1=ps[:, 0:3 * P], op0=ALU.mult, op1=ALU.add))
            self.release(b, v)
            wait(dve, v)
            for cols, t in regions:
                m = self.cdve(dve.tensor_reduce(self.RMAX[:, b, t:t + 1], pr[:, cols], AX, ALU.max))
            wait(dve, m)
            if sink is None:
                nm = self.cdve(dve.tensor_scalar(self.NM[:, b, :], self.RMAX[:, b, :], -scale, None, ALU.mult))
            else:
                s = sink[:, h:h + 1]
                mx = self.cdve(dve.tensor_scalar(self.RMAX[:, b, :], self.RMAX[:, b, :], scale, s, ALU.mult, ALU.max))
                wait(dve, mx)
                nm = self.cdve(dve.tensor_scalar(self.NM[:, b, :], self.RMAX[:, b, :], -1.0, None, ALU.mult))
                wait(act, nm)
                self.cact(act.activation(self.ESINK[:, b, :], self.NM[:, b, :], ACT.Exp, bias=s))
            wait(act, nm)
            for cols, t in regions:
                e = self.cact(act.activation(pr[:, cols], pr[:, cols], ACT.Exp, bias=self.NM[:, b, t:t + 1],
                                             scale=scale, accum_out=self.RSUM[:, b, t:t + 1]))
            wait(dve, e)
            if sink is not None:
                r = self.cdve(dve.tensor_tensor(self.RSUM[:, b, :], self.RSUM[:, b, :], self.ESINK[:, b, :], ALU.add))
                wait(dve, r)
            r = self.cdve(dve.reciprocal(self.RINV[:, b, :], self.RSUM[:, b, :]))
            wait(dve, r)
            for cols, t in regions:
                n = self.cdve(dve.tensor_scalar(pr[:, cols], pr[:, cols], self.RINV[:, b, t:t + 1], None, ALU.mult))
            state[h] = {"normed": n}

        def head_values(h):
            b = h % 2
            pr, pt = ptile[:, b, :], ptT[:, b, :]
            ps = self.bank(2)
            wait(pe, state[h]["normed"])
            self.tr(ps[:, 0:P], pr[:, 0:P])
            self.tr(ps[:, P:2 * P], pr[:, P:2 * P])
            tr = self.cpe(self.tr(ps[:, 2 * P:3 * P], pr[:, 2 * P:3 * P]))
            state[h]["transposed"] = tr
            wait(act, tr)
            if h >= 2:
                wait(act, state[h - 2]["multiplied"])
            c = self.cact(act.activation(pt, ps[:, 0:3 * P], ACT.Copy))
            self.release(2, c)
            state[h]["copied"] = c

        def head_out(h):
            b = h % 2
            pt = ptT[:, b, :]
            lo_part = slice(0, P) if dh == P else slice(dh * (h % 2), dh * (h % 2) + dh)
            if dh == P or h % 2 == 0:
                self.bank(3)
            o = self.SIDE[lo_part, 3, 0:S]
            wait(pe, state[h]["copied"])
            v0, v1 = values(h)
            self.pe.matmul(o, v0, pt[:, 0:2 * P], start=True, stop=True)
            mu = self.cpe(self.pe.matmul(o[:, P:S], v1, pt[:, 2 * P:3 * P], start=False, stop=True,
                                         skip_group_check=True))
            state[h]["multiplied"] = mu
            if dh != P and h % 2 == 0:
                return None
            tile = h if dh == P else h // 2
            wait(act, mu)
            a = self.cact(act.activation(out[0][:, tile, :], self.SIDE[:, 3, 0:S], ACT.Copy))
            wait(dve, a)
            d = self.cdve(dve.tensor_tensor(out[1][:, tile, :], self.SIDE[:, 3, 0:S],
                                            out[0][:, tile, :].bitcast(F32), ALU.subtract))
            self.release(3, d)
            return d

        head_scores(0)
        yield
        for h in range(heads + 1):
            if h + 1 < heads:
                head_scores(h + 1)
            if h:
                head_out(h - 1)
            yield
            if h < heads:
                head_values(h)
                yield
            if interlude and h == interlude[0]:
                yield from interlude[1]()

    def attention1(self, ready):
        TOK = self.TB
        q = yield from self.transposed(lambda k, t: TOK[:, t, k * P:(k + 1) * P], 8, self.QT, ready)
        k = yield from self.transposed(lambda k, t: TOK[:, t, BW + k * P:BW + (k + 1) * P], 8, self.KT, ready)
        wait(self.pe, *q, *k)
        yield from self.attention(
            HEADS, lambda h: (self.QT[:, h, :], self.KT[:, h, :]),
            lambda h: [TOK[:, t, 2 * BW + h * DH:2 * BW + (h + 1) * DH] for t in range(TT)],
            (self.OH, self.OL), self.DIST, lambda h: 2.0 ** (-8.0 * (h + 1) / HEADS), DH ** -0.5,
            ptile=self.PR, ptT=self.PT)

    def transposed(self, src, n, dst, ready, bias=None):
        wait(self.pe, *ready)
        for kp in range(n // 2):
            b = kp % 4
            ps = self.bank(b)
            for k in range(2):
                for t in range(TT):
                    inst = self.tr(ps[:, k * S + t * P:k * S + (t + 1) * P], src(2 * kp + k, t))
            done = self.cpe(inst)
            if bias is None:
                if kp % 2:
                    wait(self.dve, done)
                    last = self.cdve(self.dve.tensor_copy(dst[:, 2 * kp:2 * kp + 2, :], ps))
                else:
                    wait(self.act, done)
                    last = self.cact(self.act.activation(dst[:, 2 * kp:2 * kp + 2, :], ps, ACT.Copy))
            else:
                wait(self.dve, done)
                for k in range(2):
                    last = self.cdve(self.dve.tensor_scalar(dst[:, 2 * kp + k, :], ps[:, k * S:(k + 1) * S],
                                                            bias(2 * kp + k), None, ALU.add))
            self.release(b, last)
            yield
        return [self.cact.at(self.cact.n), self.cdve.at(self.cdve.n)]

    def gla(self, ready):
        pe, act, dve, pool, TOK = self.pe, self.act, self.dve, self.pool, self.TA
        gb = self.param(self.GB[:, :], self.t["gla_b"][0].partition_broadcast(P))
        wu = self.param(self.WUP[:, :], self.t["gla_w_up"][0])
        for _ in range(3):
            yield
        wait(pe, self.adt_ready, wu)
        wait(dve, gb)
        la, absolute = [], []
        for t in range(TT):
            ps = self.bank(1 + t)
            done = self.cpe(pe.matmul(ps, self.ADT[:, t * P:(t + 1) * P], self.WUP[:, :], start=True, stop=True))
            wait(dve, done)
            z = self.cdve(dve.scalar_tensor_tensor(out=self.LA[:, t, :], in0=ps, scalar=self.RSTD[:, t:t + 1],
                                                   in1=self.GB[:, :], op0=ALU.mult, op1=ALU.add))
            self.release(1 + t, z)
            wait(dve, z)
            absolute.append(self.cdve(dve.scalar_tensor_tensor(
                out=self.KDEC[:, t, :], in0=self.LA[:, t, :], scalar=-1.0, in1=self.LA[:, t, :],
                op0=ALU.mult, op1=ALU.max)))
        yield
        wait(act, *absolute)
        e = self.cact(act.activation(self.KDEC[:, :, :], self.KDEC[:, :, :], ACT.Exp, scale=-1.0))
        wait(act, e)
        l = self.cact(act.activation(self.KDEC[:, :, :], self.KDEC[:, :, :], ACT.Ln, bias=1.0))
        yield
        wait(dve, l)
        for t in range(TT):
            la.append(self.cdve(dve.scalar_tensor_tensor(out=self.LA[:, t, :], in0=self.LA[:, t, :], scalar=0.0,
                                                         in1=self.KDEC[:, t, :], op0=ALU.min, op1=ALU.subtract)))
        yield
        wait(pe, *la)
        for t in range(TT):
            ps = self.bank(1 + t)
            done = self.cpe(pe.matmul(ps, self.LS[:, :], self.LA[:, t, :], start=True, stop=True))
            wait(act, done, la[t])
            e = self.cact(act.activation(self.KDEC[:, t, :], ps, ACT.Exp))
            self.release(1 + t, e)
            wait(dve, e, *ready)
            kd = self.cdve(dve.tensor_tensor(self.KDEC[:, t, :], self.KDEC[:, t, :], TOK[:, t, 512:1024], ALU.mult))
        yield
        wait(act, *ready)
        for t in range(TT):
            sr = self.cact(act.activation(TOK[:, t, 2048:3072], TOK[:, t, 2048:3072], ACT.Silu))
        wait(pe, kd, *ready)
        m0 = self.cdve(dve.memset(self.AT[:, :, :], 0.0))
        wait(dve, m0)
        mask = self.U[:, :].bitcast(U32)
        og = None
        for h in range(GH):
            hk, hv = slice(h * GK, (h + 1) * GK), slice(1024 + h * GV, 1024 + (h + 1) * GV)
            b0, b1 = self.bank(0), self.bank(1)
            for t in range(TT):
                pe.matmul(b0[:, t * P:(t + 1) * P], self.LA[:, t, hk], self.U[:, :], start=True, stop=True)
            bt = self.cpe(self.tr(b1[:, 0:P], TOK[:, 0, hk]))
            self.tr(b1[:, P:S], TOK[:, 1, hk])
            for t in range(TT):
                inst = self.tr(b1[:, S + t * P:S + (t + 1) * P], TOK[:, t, 512 + h * GK:512 + (h + 1) * GK])
            qk = self.cpe(inst)
            wait(act, bt)
            if og is not None:
                wait(act, og)
            eb = self.cact(act.activation(self.EB[:, :], b0[:, 0:S], ACT.Exp))
            en = self.cact(act.activation(self.EN[:, :], b0[:, 0:S], ACT.Exp, scale=-1.0))
            self.release(0, en)
            wait(dve, qk, en)
            if og is not None:
                wait(dve, og)
            qi = self.cdve(dve.scalar_tensor_tensor(out=self.QIN[:, :], in0=b1[:, 0:S], scalar=GK ** -0.5,
                                                    in1=self.EB[:, :], op0=ALU.mult, op1=ALU.mult))
            ki = self.cdve(dve.tensor_tensor(self.KIN[:, :], b1[:, S:2 * S], self.EN[:, :], ALU.mult))
            self.release(1, ki)
            yield
            b2 = self.bank(2)
            wait(pe, ki)
            for t in range(TT):
                inst = pe.matmul(b2[:, t * P:(t + 1) * P], self.KIN[:, t * P:(t + 1) * P],
                                 self.QIN[:, t * P:(t + 1) * P], start=True, stop=True)
            sc = self.cpe(inst)
            b0, b1 = self.bank(0), self.bank(1)
            kv = []
            for n in range(3):
                o = (b0[:, 0:256], b1[:, 0:256], b0[:, 256:512])[n]
                r = slice(64 * (n % 2), 64 * (n % 2) + 64)
                kv.append(self.cpe(pe.matmul(o, self.KDEC[r, n // 2, hk], TOK[r, n // 2, hv], start=True, stop=True)))
            yield
            wait(dve, sc)
            for t in range(TT):
                at = self.cdve(dve.copy_predicated(self.AT[:, t, :], mask, b2[:, t * P:(t + 1) * P]))
            self.release(2, at)
            wait(dve, kv[2])
            s = self.cdve(dve.tensor_copy(self.ST[:, 0, :], b0[:, 0:256]))
            for n, o in ((1, b1[:, 0:256]), (2, b0[:, 256:512])):
                wait(dve, s, kv[n])
                s = self.cdve(dve.scalar_tensor_tensor(
                    out=self.ST[:, n, :], in0=self.ST[:, n - 1, :], scalar=self.EB[:, 64 * n + 63:64 * n + 64],
                    in1=o, op0=ALU.mult, op1=ALU.add))
            self.release(0, s)
            self.release(1, s)
            yield
            b3 = self.bank(3)
            wait(pe, at, s)
            for t in range(TT):
                o = b3[:, t * 256:(t + 1) * 256]
                pe.matmul(o, self.AT[:, t, :], TOK[:, t, hv], start=True, stop=True)
                for n in (2 * t, 2 * t + 1):
                    if n:
                        r = slice(64 * (n % 2), 64 * (n % 2) + 64)
                        inst = pe.matmul(o[r, :], self.QIN[:, 64 * n:64 * n + 64], self.ST[:, n - 1, :],
                                         start=False, stop=True, skip_group_check=True)
            done = self.cpe(inst)
            wait(act, done)
            for t in range(TT):
                q = self.cact(act.activation(self.ST[:, t, :], b3[:, t * 256:(t + 1) * 256], ACT.Square,
                                             accum_out=self.SS[:, t:t + 1]))
            r = self.power(q, self.SS[:, 0:2], 1.0 / GV, self.GR[:, 0:2])
            wait(dve, r, sr)
            for t in range(TT):
                og = self.cdve(dve.scalar_tensor_tensor(
                    out=TOK[:, t, hv], in0=b3[:, t * 256:(t + 1) * 256], scalar=self.GR[:, t:t + 1],
                    in1=TOK[:, t, 2048 + h * GV:2048 + (h + 1) * GV], op0=ALU.mult, op1=ALU.mult))
            self.release(3, og)
            yield
        yield from self.feature_major(lambda k, t: TOK[:, t, 1024 + k * P:1024 + (k + 1) * P], 8,
                                      self.GHI, self.GLO, [og],
                                  weights=lambda k: self.V1[:, 64 + k % 2:65 + k % 2])

    def merge_branch(self, w_gate, gate_col, w_branch, stat, nk, mix, first, unroll=False, then=None):
        act, dve = self.act, self.dve
        SIG = self.SIG
        half = nk // 2

        def body(i):
            base = {}
            for p in range(2):
                col = i * 2 * PANEL + p * PANEL

                def gate(t, acc, done, p=p, col=col):
                    sig = SIG[:, t, p, :]
                    wait(act, done, self.ev[t].at(self.ev[t].n), self.before[2])
                    base[t] = self.ev[t](act.activation(sig, acc, ACT.Sigmoid, scale=self.RSTD[:, t:t + 1]))

                def branch(t, acc, done, p=p, col=col):
                    sig, m = SIG[:, t, p, :], mix[:, t, ds(col, PANEL)]
                    wait(dve, done, base[t])
                    if first:
                        self.ev[t](dve.tensor_tensor(m, acc, sig, ALU.mult))
                    else:
                        v = self.ev[t](dve.tensor_tensor(sig, acc, sig, ALU.mult))
                        wait(dve, v)
                        self.cdve(dve.tensor_tensor(m, m, sig, ALU.add))

                self.product(w_gate, i * 2 * PANEL + (gate_col + p * PANEL), PANEL, (self.XH, self.XL), [CK] * 4, gate)
                self.product(w_branch, col, PANEL, stat, [half] * 2, branch)
                if then:
                    then(2 * i + p)

        if unroll:
            self.unrolled(D // PANEL // 2, body)
            return
        self.repeat(D // PANEL // 2, body, self.per(12, 4, cdve=0 if first else 4))

    def residual(self, w, stat, groups, norm, last=False):

        def evacuate(col):
            def f(t, acc, done):
                x = self.X[:, t, col:col + PANEL]
                wait(self.dve, done)
                self.ev[t](self.dve.tensor_tensor(x, x, acc, ALU.add))
            return f

        n = D // PANEL
        for p in range(n):
            self.product(w, p * PANEL, PANEL, stat, groups, evacuate(p * PANEL), last=last and p == n - 1)
            self.finish_background()
            self.background.append(norm(p, [e.at(e.n) for e in self.ev]))

    def turn_mixed(self, mixed, p, hi, lo):
        n = PANEL // P
        ready = [e.at(e.n) for e in self.ev] + [self.cdve.at(self.cdve.n), self.cpool.at(self.cpool.n)]
        yield
        last = yield from self.feature_major(
            lambda k, t: mixed[:, t, (n * p + k) * P:(n * p + k + 1) * P], n, hi, lo,
            ready, at=n * p)
        wait(self.pe, last)

    def ffn(self, w_gate, gate_col, w_up, up_col, rows, second):
        act, dve, FF1, FF2 = self.act, self.dve, self.FF1, self.FF2
        n = FF // PANEL

        def products(i, side, turned):
            evacuated = {}

            def gate(t, acc, done):
                wait(act, done, self.ev[t].at(self.ev[t].n), *turned())
                evacuated[t] = self.ev[t](act.activation(FF1[:, t, :], acc, ACT.Copy if second else ACT.Silu,
                                                         scale=self.RSTD[:, t:t + 1]))

            def up(t, acc, done):
                wait(dve, done, evacuated[t], *turned())
                if second:
                    self.ev[t](dve.tensor_scalar(FF2[:, t, :], acc, self.RSTD[:, t:t + 1], None, ALU.mult))
                else:
                    self.ev[t](dve.scalar_tensor_tensor(out=FF2[:, t, :], in0=acc, scalar=self.RSTD[:, t:t + 1],
                                                        in1=FF1[:, t, :], op0=ALU.mult, op1=ALU.mult))

            self.product(w_gate, i * PANEL + gate_col, PANEL, (self.XH, self.XL), [CK] * 4, gate, side=side)
            self.product(w_up, i * PANEL + up_col, PANEL, (self.XH, self.XL), [CK] * 4, up)

        def turn(i):
            at = i * (PANEL // P)
            ready = [e.at(e.n) for e in self.ev]
            if not second:
                return {n: lambda kp=kp: self.turn_plain(at, kp, ready) for kp, n in enumerate((1, 4))}
            steps = {n: lambda kp=kp: self.turn_conv(at, kp, ready) for kp, n in enumerate((1, 4))}
            steps.update({n: lambda kp=kp: self.gate_conv(at, kp) for kp, n in enumerate((2, 5))})
            return steps

        def body(i):
            products(i + 1, turn(i), lambda: [self.turned])

        products(0, None, lambda: [])
        self.finish_background()
        self.free_act_dve()
        steps = dict(cpe=2, cact=2, cdve=2) if not second else dict(cpe=2, cact=4, cdve=16)
        self.repeat(n - 1, body, self.per(8, 2, **steps))
        steps = turn(n - 1)

        def last_turn():
            for piece in sorted(steps):
                steps[piece]()
                yield
            wait(self.pe, self.cdve.at(self.cdve.n))
            self.norm_rows(rows)

        wait(self.pe, self.cdve.at(self.cdve.n))
        self.background = [last_turn()]

    def turn_plain(self, at, kp, ready):
        b = kp
        ps = self.bank(b)
        wait(self.pe, *ready)
        for k in range(2):
            for t in range(TT):
                f = (2 * kp + k) * P
                inst = self.tr(ps[:, k * S + t * P:k * S + (t + 1) * P], self.FF2[:, t, f:f + P])
        self.turned = self.cpe(inst)
        wait(self.act, self.turned)
        hh, hl = (x[:, ds(at + 2 * kp, 2), :] for x in (self.HH, self.HL))
        a = self.cact(self.act.activation(hh, ps[:, :], ACT.Copy))
        wait(self.dve, a)
        self.release(b, self.cdve(self.dve.tensor_tensor(hl, ps[:, :], hh.bitcast(F32), ALU.subtract)))

    def turn_conv(self, at, kp, ready):
        act, dve, G = self.act, self.dve, self.CG
        wait(self.pe, *ready)
        b0, b1 = self.bank(2 * kp), self.bank(2 * kp + 1)
        for k in range(2):
            for t in range(TT):
                f = (2 * kp + k) * P
                o = slice(k * S + t * P, k * S + (t + 1) * P)
                self.tr(b0[:, o], self.FF1[:, t, f:f + P])
                inst = self.tr(b1[:, o], self.FF2[:, t, f:f + P])
        self.turned = self.cpe(inst)
        wait(dve, self.turned, self.cdve.at(self.cdve.n), self.cact.at(self.cact.n))
        vec = lambda j, k: self.V2[:, ds(at + (j * KF + 2 * kp + k), 1)]
        for k in range(2):
            v = self.cdve(dve.tensor_scalar(G[:, k, :], b0[:, k * S:(k + 1) * S], vec(2, k), vec(3, k),
                                            ALU.mult, ALU.add))
        for j in (1, 0):
            s = 2 - j
            wait(dve, v)
            for k in range(2):
                v = self.cdve(dve.scalar_tensor_tensor(
                    out=G[:, k, s:S], in0=b0[:, k * S:(k + 1) * S - s], scalar=vec(j, k), in1=G[:, k, s:S],
                    op0=ALU.mult, op1=ALU.add))
        self.convolved = v

    def gate_conv(self, at, kp):
        act, dve, G = self.act, self.dve, self.CG
        b0, b1 = self.SIDE[:, 2 * kp, :], self.SIDE[:, 2 * kp + 1, :]
        v = self.convolved
        wait(act, v)
        ge = self.cact(act.activation(G[:, :, :], G[:, :, :], ACT.Gelu))
        wait(dve, ge)
        v = self.cdve(dve.tensor_tensor(G[:, :, :], b1.rearrange("p (k s) -> p k s", k=2), G[:, :, :], ALU.mult))
        self.release(2 * kp, v)
        self.release(2 * kp + 1, v)
        wait(act, v)
        hh, hl = (x[:, ds(at + 2 * kp, 2), :] for x in (self.HH, self.HL))
        a = self.cact(act.activation(hh, G[:, :, :], ACT.Copy))
        wait(dve, a)
        self.cdve(dve.tensor_tensor(hl, G[:, :, :], hh.bitcast(F32), ALU.subtract))

    def ssm_setup(self):
        pe, act, dve, t = self.pe, self.act, self.dve, self.t
        V = lambda n: self.SV[:, n, :]
        (DT, TH, MAG, KK, R1, R2, SIN, COS, ABR, ABI, NR, DEN, RD, Z1, Z2, ZR, ZI, T1, T2) = range(19)
        are, aim = self.V3[:, 18:18 + ST], self.V3[:, 34:34 + ST]
        ld = self.param(self.LDT[:, :], t["ssm_log_dt_2"][0].rearrange("(s q) -> s q", q=2))
        lb = [self.param(self.BRE[:, :, :], t["ssm_b_re_2"][0].rearrange("(s q) p h -> (q p) s h", q=2)),
              self.param(self.BIM[:, :, :], t["ssm_b_im_2"][0].rearrange("(s q) p h -> (q p) s h", q=2))]
        lc = []
        for i, n in enumerate(("ssm_c_re_2", "ssm_c_im_2")):
            for half in range(2):
                lc.append(self.param(self.CRE[:, i, :, 64 * half:64 * half + 64],
                                     t[n][0].rearrange("(u r) h p -> (r h) u p", r=8)))
        for _ in range(3):
            yield
        wait(dve, ld)
        v = self.cdve(dve.tensor_copy(self.SROW[:, :].rearrange("s (q p) -> s q p", q=2),
                                      self.LDT[:, :].unsqueeze(2).to_broadcast([ST, 2, STATE])))
        wait(pe, v)
        ps = self.bank(0)
        done = self.cpe(self.tr(ps[:, 0:ST], self.SROW[:, :]))
        wait(act, done)
        a = self.cact(act.activation(V(DT), ps[:, 0:ST], ACT.Exp))
        self.release(0, a)

        def step(inst):
            tok = self.cdve(inst)
            wait(dve, tok)
            return tok

        tt = lambda o, x, y, op: step(dve.tensor_tensor(V(o), x, y, op))
        ts = lambda o, x, s1, s2, op0, op1: step(dve.tensor_scalar(V(o), x, s1, s2, op0, op1))
        yield
        wait(dve, a)
        tt(TH, V(DT), aim, ALU.mult)
        x = tt(T1, V(DT), are, ALU.mult)
        wait(act, x)
        mag = self.cact(act.activation(V(MAG), V(T1), ACT.Exp))
        big = 1.5 * 2.0 ** 23
        c1, c2 = 6.28125, 0.0019350051879882812
        c3 = TWO_PI - c1 - c2
        for out, shift in ((R1, 0.0), (R2, 0.25)):
            ts(KK, V(TH), 1.0 / TWO_PI, shift, ALU.mult, ALU.add)
            ts(KK, V(KK), big, None, ALU.add, ALU.bypass)
            ts(KK, V(KK), -big, None, ALU.add, ALU.bypass)
            step(dve.scalar_tensor_tensor(out=V(out), in0=V(KK), scalar=-c1, in1=V(TH), op0=ALU.mult, op1=ALU.add))
            step(dve.scalar_tensor_tensor(out=V(out), in0=V(KK), scalar=-c2, in1=V(out), op0=ALU.mult, op1=ALU.add))
            step(dve.scalar_tensor_tensor(out=V(out), in0=V(KK), scalar=-c3, in1=V(out), op0=ALU.mult, op1=ALU.add))
            if shift:
                ts(out, V(out), float(np.pi / 2), None, ALU.add, ALU.bypass)
            r = ts(out, V(out), 3.1415925, -3.1415925, ALU.min, ALU.max)
            yield
        wait(act, r)
        self.cact(act.activation(V(SIN), V(R1), ACT.Sin))
        sc = self.cact(act.activation(V(COS), V(R2), ACT.Sin))
        wait(dve, mag, sc)
        tt(ABR, V(MAG), V(COS), ALU.mult)
        tt(ABI, V(MAG), V(SIN), ALU.mult)
        ts(NR, V(ABR), -1.0, None, ALU.add, ALU.bypass)
        yield
        tt(T1, are, are, ALU.mult)
        tt(T2, aim, aim, ALU.mult)
        tt(DEN, V(T1), V(T2), ALU.add)
        step(dve.reciprocal(V(RD), V(DEN)))
        tt(T1, V(NR), are, ALU.mult)
        tt(T2, V(ABI), aim, ALU.mult)
        tt(T1, V(T1), V(T2), ALU.add)
        tt(ZR, V(T1), V(RD), ALU.mult)
        tt(T1, V(ABI), are, ALU.mult)
        tt(T2, V(NR), aim, ALU.mult)
        tt(T1, V(T1), V(T2), ALU.subtract)
        tt(ZI, V(T1), V(RD), ALU.mult)
        yield
        step(dve.memset(self.BBR[:, :, :], 0.0))
        step(dve.memset(self.BBI[:, :, :], 0.0))
        wait(dve, *lb)
        sc1 = self.SCR[:, 0:256].rearrange("p (s h) -> p s h", h=GROUP)
        sc2 = self.SCR[:, 256:512].rearrange("p (s h) -> p s h", h=GROUP)
        zr, zi = (V(z).unsqueeze(2).to_broadcast([P, ST, GROUP]) for z in (ZR, ZI))
        for dst, x, y, op in ((self.BBR, zr, zi, ALU.subtract), (self.BBI, zi, zr, ALU.add)):
            step(dve.tensor_tensor(sc1, self.BRE[:, :, :], x, ALU.mult))
            step(dve.tensor_tensor(sc2, self.BIM[:, :, :], y, ALU.mult))
            for q in range(2):
                r = slice(64 * q, 64 * q + 64)
                v = step(dve.tensor_tensor(dst[r, :, GROUP * q:GROUP * (q + 1)], sc1[r], sc2[r], op))
            yield
        wait(pe, v)
        b = 0
        for src, dst in ((self.BBR, self.BTR), (self.BBI, self.BTI)):
            ps = self.bank(b)
            for u in range(4):
                inst = self.tr(ps[:, u * P:(u + 1) * P], src[:, 4 * u:4 * u + 4, :])
            done = self.cpe(inst)
            wait(act, done)
            bt = self.cact(act.activation(dst[:, :, :], ps.rearrange("p (u s) -> p u s", u=4), ACT.Copy))
            self.release(b, bt)
            b += 1
            yield
        step(dve.memset(self.CTR[:, :, :], 0.0))
        z = step(dve.memset(self.CTI[:, :, :], 0.0))
        wait(pe, *lc)
        wait(act, z)
        for i, (dst, sign) in enumerate(((self.CTR, 1.0), (self.CTI, -1.0))):
            ps = self.bank(2 + i)
            for u in range(4):
                inst = self.tr(ps[:, u * P:(u + 1) * P], self.CRE[:, i, u, :])
            done = self.cpe(inst)
            wait(act, done)
            for q in range(2):
                r = slice(64 * q, 64 * q + 64)
                src = ps.rearrange("p (s q h) -> p s q h", q=2, h=GROUP)[r, :, q, :]
                ct = self.cact(act.activation(dst[r, :, GROUP * q:GROUP * (q + 1)], src, ACT.Copy, scale=sign))
            self.release(2 + i, ct)
            yield
        self.a_bar = V(ABR), V(ABI)
        yield from self.ssm_powers()

    def ssm_powers(self):
        dve = self.dve

        def step(inst):
            tok = self.cdve(inst)
            wait(dve, tok)
            return tok

        pw = self.POW
        step(dve.tensor_copy(pw[:, 0, :, 0], self.a_bar[0]))
        step(dve.tensor_copy(pw[:, 1, :, 0], self.a_bar[1]))
        n = 1
        while n < BLK:
            lo = lambda ri: pw[:, ri, :, 0:n]
            top = lambda ri: pw[:, ri, :, n - 1:n].to_broadcast([P, ST, n])
            new = lambda ri: pw[:, ri, :, n:2 * n]
            tmp = self.SCR[:, 0:ST * n].rearrange("p (s j) -> p s j", s=ST)
            for ri, x, y, op in ((0, 0, 1, ALU.subtract), (1, 1, 0, ALU.add)):
                step(dve.tensor_tensor(new(ri), lo(0), top(x), ALU.mult))
                step(dve.tensor_tensor(tmp, lo(1), top(y), ALU.mult))
                step(dve.tensor_tensor(new(ri), new(ri), tmp, op))
            n *= 2
            if n == 4:
                yield
        sv = self.SV
        step(dve.tensor_copy(sv[:, 20, :], self.a_bar[0]))
        step(dve.tensor_copy(sv[:, 21, :], self.a_bar[0]))
        step(dve.tensor_scalar(sv[:, 22, :], self.a_bar[1], -1.0, None, ALU.mult))
        step(dve.tensor_copy(sv[:, 23, :], self.a_bar[1]))
        step(dve.tensor_copy(sv[:, 24, :], pw[:, 0, :, BLK - 1]))
        step(dve.tensor_copy(sv[:, 25, :], pw[:, 0, :, BLK - 1]))
        step(dve.tensor_scalar(sv[:, 26, :], pw[:, 1, :, BLK - 1], -1.0, None, ALU.mult))
        step(dve.tensor_copy(sv[:, 27, :], pw[:, 1, :, BLK - 1]))

    def ssm_input(self, half, u_ready):
        pe, act, XS = self.pe, self.act, self.XS
        nt = ST // 2
        s0 = half * nt
        wait(pe, *u_ready)
        wait(act, *u_ready)
        for s in range(nt):
            b = s % 4
            ps = self.bank(b)
            u, r = (s0 + s) // 4, slice(32 * (s % 4), 32 * (s % 4) + 32)
            pe.matmul(ps[:, 0:S], self.BTR[r, u, :], self.UT[r, u, :], start=True, stop=True)
            done = self.cpe(pe.matmul(ps[:, S:2 * S], self.BTI[r, u, :], self.UT[r, u, :], start=True, stop=True))
            wait(act, done)
            a = self.cact(act.activation(XS[:, :, s, :], ps.rearrange("p (c t) -> p c t", c=2), ACT.Copy))
            self.release(b, a)
            if s % 2:
                yield
        self.scan(s0, [a, self.cdve.at(self.cdve.n)])

    def scan(self, s0, ready):
        pool, XS = self.pool, self.XS
        nt = ST // 2
        X5 = XS[:, :, :, :].rearrange("p c s (b j) -> p c s b j", j=BLK)
        wait(pool, *ready)

        def advance(prev, cur, coef, n):
            row = lambda k, m: self.SV[:, coef + k:coef + k + m, s0:s0 + nt].unsqueeze(3).to_broadcast([P, m, nt, n])
            same, cross = self.STEP[:, 0:2, :, 0:n], self.STEP[:, 2:4, :, 0:n]
            v = self.cpool(pool.tensor_tensor(same, prev, row(0, 2), ALU.mult))
            for c in range(2):
                self.cpool(pool.tensor_tensor(cross[:, c:c + 1], prev[:, 1 - c:2 - c], row(2 + c, 1), ALU.mult))
            wait(pool, v)
            v = self.cpool(pool.tensor_tensor(cur, cur, same, ALU.add))
            wait(pool, v)
            wait(pool, self.cpool(pool.tensor_tensor(cur, cur, cross, ALU.add)))

        for j in range(BLK - 1):
            advance(X5[:, :, :, :, j], X5[:, :, :, :, j + 1], 20, NB)
        for b in range(NB - 1):
            advance(X5[:, :, :, b:b + 1, BLK - 1], X5[:, :, :, b + 1:b + 2, BLK - 1], 24, 1)
        nb, nj, ns = NB - 1, BLK - 1, 4
        tmp = self.SCR[:, 0:ns * nb * nj].rearrange("p (s b j) -> p s b j", b=nb, j=nj)
        for q in range(0, nt, ns):
            for ci in range(2):
                cur = X5[:, ci, q:q + ns, 1:NB, 0:nj]
                for y in range(2):
                    pr = self.POW[:, (ci + y) % 2, s0 + q:s0 + q + ns, 0:nj].unsqueeze(2).to_broadcast([P, ns, nb, nj])
                    last = X5[:, y, q:q + ns, 0:nb, BLK - 1:BLK].to_broadcast([P, ns, nb, nj])
                    wait(pool, self.cpool(pool.tensor_tensor(tmp, pr, last, ALU.mult)))
                    op = ALU.subtract if (ci, y) == (0, 1) else ALU.add
                    t = self.cpool(pool.tensor_tensor(cur, cur, tmp, op))
                    wait(pool, t)
        self.scanned = t

    def ssm_output(self, half):
        pe, dve = self.pe, self.dve
        wait(pe, self.scanned)
        for u in (2 * half, 2 * half + 1):
            ps = self.bank(u)
            for j in range(4):
                o = ps[32 * j:32 * j + 32, 0:S]
                s = 4 * u + j
                x = s - half * ST // 2
                pe.matmul(o, self.CTR[:, s, :], self.XS[:, 0, x, :], start=True, stop=False)
                inst = pe.matmul(o, self.CTI[:, s, :], self.XS[:, 1, x, :], start=False, stop=True)
            done = self.cpe(inst)
            wait(dve, done)
            y = self.cdve(dve.scalar_tensor_tensor(out=self.UT[:, u, :], in0=self.UT[:, u, :],
                                                   scalar=self.V3[:, 14 + u:15 + u], in1=ps[:, 0:S],
                                                   op0=ALU.mult, op1=ALU.add))
            self.release(u, y)
            self.y_ready = y
            yield

    def ssm_halves(self):
        yield from self.ssm_output(0)
        yield from self.ssm_input(1, [self.cpe.at(self.cpe.n)])

    def ssm_end(self):
        act, dve = self.act, self.dve
        yield from self.ssm_output(1)
        wait(act, self.y_ready)
        g = self.cact(act.activation(self.UT[:, :, :], self.UT[:, :, :], ACT.Gelu))
        wait(act, g)
        a = self.cact(act.activation(self.GEH[:, :, :], self.UT[:, :, :], ACT.Copy))
        wait(dve, a)
        g = self.cdve(dve.tensor_tensor(self.GEL[:, :, :], self.UT[:, :, :], self.GEH[:, :, :].bitcast(F32),
                                        ALU.subtract))
        wait(self.pe, g)

    def glu(self):
        act, dve, w = self.act, self.dve, self.t["w_glu_2"][0]
        wait(dve, self.glu_rows)
        for p in range(2):
            cols = slice(p * SSMW, (p + 1) * SSMW)

            def evacuate(t, acc, done, cols=cols):
                wait(dve, done)
                self.ev[t](dve.tensor_tensor(self.GLU[:, t, cols], acc, self.GBR[:, cols], ALU.add))
            self.product(w, p * SSMW, SSMW, (self.GEH, self.GEL), [2, 2], evacuate, after=1 if p == 0 else 2)
        self.glu_ready = [e.at(e.n) for e in self.ev]

    def glu_turned(self):
        act, dve = self.act, self.dve
        wait(act, *self.glu_ready)
        for t in range(TT):
            a = self.cact(act.activation(self.GLU[:, t, SSMW:], self.GLU[:, t, SSMW:], ACT.Sigmoid))
        wait(dve, a)
        for t in range(TT):
            v = self.cdve(dve.tensor_tensor(self.GLU[:, t, 0:SSMW], self.GLU[:, t, 0:SSMW], self.GLU[:, t, SSMW:],
                                            ALU.mult))
        yield
        yield from self.feature_major(lambda k, t: self.GLU[:, t, k * P:(k + 1) * P], 4, self.SH, self.SL, [v])

    def build(self):
        act, dve, pe, t = self.act, self.dve, self.pe, self.t
        dve.sem_inc(self.lo.sem, 2 * SLOTS)
        pe.sem_inc(self.mm.sem, PIECES)
        for e in self.ev:
            dve.sem_inc(e.sem, 2)
        self.lo.n, self.mm.n, self.ev[0].n, self.ev[1].n = 2 * SLOTS, PIECES, 2, 2
        xl = [Counter(self.ctx.enter_context(self.nc.semaphore(f"x_load{i}")), 16) for i in range(2)]
        x = t["x"][0].rearrange("(t p) n -> p t n", p=P)
        halves = [slice(h * D // 2, (h + 1) * D // 2) for h in range(2)]
        xl = [c(self.sp.dma_start(self.X[:, :, h], x[:, :, h])) for c, h in zip(xl, halves)]
        wait(self.sp, xl[0])
        self.const_ready = self.constants()
        vectors = self.vectors()
        self.run(self.turn_x(0, xl[0:1], 0))
        self.split_piece()
        last = self.run(self.turn_x(1, xl[0:1], 0))
        wait(pe, last)
        self.split_piece()
        self.split_piece()
        self.background = [self.first_norm(xl), vectors]
        w_in = t["w_in"][0]
        self.wad = self.param(self.WAD[:, :, :],
                              w_in[:, COL_AD:COL_AD + RANK].rearrange("(k p) n -> p k n", p=P))
        r = self.project(w_in, COL_BCU, PANEL, 6, self.TA, unroll=1)
        self.background = [self.conv_branch(r), self.a_down()]
        r = self.project(w_in, COL_QKV, PANEL, 6, self.TB, unroll=3)
        self.finish_background()
        self.settle()
        self.background = [self.attention1(r)]
        r = self.project(w_in, COL_GLA, PANEL, 6, self.TA, unroll=3)
        self.finish_background()
        self.settle()
        self.background = [self.gla(r)]
        self.merge_branch(w_in, COL_MERGE, t["w_br_attn"][0], (self.OH, self.OL), 8, self.MIX, True, unroll=True)
        self.finish_background()
        self.settle()
        self.merge_branch(w_in, COL_MERGE + D, t["w_br_gla"][0], (self.GHI, self.GLO), 8, self.MIX, False)
        self.merge_branch(w_in, COL_MERGE + 2 * D, t["w_br_conv"][0], (self.YH, self.YL), 8, self.MIX, False,
                          unroll=True, then=lambda p: self.background.append(
                              self.turn_mixed(self.MIX, p, self.MH, self.ML)))
        self.out_and_ffn((self.MH, self.ML), t["w_out"][0], KD, t["w_ffn_gate"][0], 0, t["w_ffn_up"][0], 0,
                         t["w_ffn_down"][0], t["final_norm_w"], False)
        self.block2_branches(t["w_in_2"][0])
        self.out_and_ffn((self.MH2, self.ML2), t["w_out_2"][0], 3 * KD, t["w_up_2"][0], FF, t["w_up_2"][0], 0,
                         t["w_down_2"][0], t["final_norm_g_2"], True)
        self.finish_background()
        stored = []
        for h in range(2):
            cols = slice(h * D // 2, (h + 1) * D // 2)
            for i in range(TT):
                x, r = self.X[:, i, cols], self.RSTD[:, i:i + 1]
                v = (self.cact(act.activation(x, x, ACT.Copy, scale=r)) if i == 0 else
                     self.cdve(dve.tensor_scalar(x, x, r, None, ALU.mult)))
                wait(self.sp, v)
                stored.append(self.cdma[2 * h + i](self.sp.dma_start(self.out[0, i * P:(i + 1) * P, cols], x)))
        wait(self.sp, *stored)

    def settle(self):
        steps = [c.at(c.n) for c in (self.cpe, self.cact, self.cdve, self.cpool, *self.ev)] + [self.mm.at(self.mm.n)]
        for e in (self.pe, self.act, self.dve):
            wait(e, *steps)

    def out_and_ffn(self, mixedT, w_out, w_norm, w_gate, gate_col, w_up, up_col, w_down, rows, second):
        self.residual(w_out, mixedT, [CK] * 4, lambda p, ready: self.norm_panel(p, ready, turn=w_norm))
        self.ffn(w_gate, gate_col, w_up, up_col, rows, second)
        self.residual(w_down, (self.HH, self.HL), [4] * 8 + [3] * 4, last=second, norm=lambda p, ready:
                      self.norm_panel(p, ready, turn=None if second else 2 * KD, rows=True))

    def columns2(self, w, col, width):
        def evacuate(t, acc, done):
            wait(self.act, done)
            self.ev[t](self.act.activation(self.TOK2[:, t, col:col + width], acc, ACT.Copy,
                                           scale=self.RSTD[:, t:t + 1]))
        self.product(w, col, width, (self.XH, self.XL), [CK] * 4, evacuate)
        return [e.at(e.n) for e in self.ev]

    def gates2(self, w, first, panel, dst, after=2):
        act, dve = self.act, self.dve
        cols = slice(panel * PANEL, (panel + 1) * PANEL)
        col = QKVU2 + first + panel * PANEL
        rows = self.GROW[:, panel % 2, :]
        wait(act, *[e.at(e.n) for e in self.ev])
        gr = self.param(rows, self.t["b_in_2"][0, col:col + PANEL].partition_broadcast(P))

        def evacuate(t, acc, done):
            wait(dve, done, gr)
            self.ev[t](dve.scalar_tensor_tensor(out=dst[:, t, cols], in0=acc, scalar=self.RSTD[:, t:t + 1],
                                                    in1=rows, op0=ALU.mult, op1=ALU.add))
        self.product(w, col, PANEL, (self.XH, self.XL), [CK] * 4, evacuate, after=after)

    def sigmoid2(self, dst, panel):
        wait(self.act, *[e.at(e.n) for e in self.ev])
        o = dst[:, :, panel * PANEL:(panel + 1) * PANEL]
        self.gated = self.cact(self.act.activation(o, o, ACT.Sigmoid))

    def branch2(self, w, panel, stat, chunks, gates, add, after=2):
        dve = self.dve
        cols = slice(panel * PANEL, (panel + 1) * PANEL)

        def evacuate(t, acc, done):
            g = gates[:, t, cols]
            wait(dve, done, self.gated)
            v = self.ev[t](dve.tensor_tensor(g, acc, g, ALU.mult))
            if add:
                wait(self.pool, v)
                self.cpool(self.pool.tensor_tensor(self.MG[:, t, cols], self.MG[:, t, cols], g, ALU.add))
        self.product(w, panel * PANEL, PANEL, stat, chunks, evacuate, after=after)

    def block2_branches(self, w):
        t, pe = self.t, self.pe
        self.background.append(self.ssm_setup())
        r = self.columns2(w, 1280, SSMW)
        self.background.append(self.ssm_first_half(r))
        self.columns2(w, 0, PANEL)
        self.columns2(w, PANEL, PANEL)
        r = self.columns2(w, 1024, 256)
        self.background.append(self.attention2(r))
        self.dense = True
        for p in range(4):
            self.gates2(w, 0, p, self.MG)
        self.dense = False
        self.finish_background()
        wait(pe, self.cact.at(self.cact.n), self.cdve.at(self.cdve.n))
        for p in range(4):
            self.sigmoid2(self.MG, p)
            self.branch2(t["w_branch_attn_2"][0], p, (self.OH2, self.OL2), [4, 4], self.MG, False)
        self.free_act_dve()
        self.glu_rows = self.param(self.GBR[:, :], t["b_glu_2"][0].partition_broadcast(P))
        for p in range(3):
            if p == 2:
                self.background.append(self.ssm_end())
            self.gates2(w, D, p, self.GS, after=1 if p == 2 else 2)
        self.finish_background()
        self.glu()
        self.background = [self.glu_turned()]
        self.gates2(w, D, 3, self.GS, after=1)
        self.finish_background()
        wait(pe, self.cact.at(self.cact.n), self.cdve.at(self.cdve.n))
        for p in range(4):
            self.sigmoid2(self.GS, p)
            self.branch2(t["w_branch_ssm_2"][0], p, (self.SH, self.SL), [2, 2], self.GS, True, after=1 if p < 3 else 2)
            self.background.append(self.turn_mixed(self.MG, p, self.MH2, self.ML2))

    def free_act_dve(self):
        for e in (self.act, self.dve):
            wait(e, self.cpe.at(self.cpe.n), self.cact.at(self.cact.n), self.cdve.at(self.cdve.n))

    def ssm_first_half(self, ready):
        ucol = 1280
        u = yield from self.transposed(lambda k, t: self.TOK2[:, t, ucol + k * P:ucol + (k + 1) * P], 4, self.UT,
                                       ready, bias=lambda k: self.V3[:, 10 + k:11 + k])
        yield from self.ssm_input(0, [*u])

    def attention2(self, r):
        act, dve, pe, t = self.act, self.dve, self.pe, self.t
        TOK = self.TOK2
        kcol, vcol, ucol = 1024, 1152, 1280
        self.free_act_dve()
        vb = self.param(self.VB[:, :], t["b_in_2"][0, vcol:ucol].partition_broadcast(P))
        sk = self.param(self.SINK[:, :], t["attn_sinks_2"][0].partition_broadcast(P))
        bias = lambda k: self.V3[:, k:k + 1]
        q = yield from self.transposed(lambda k, t: TOK[:, t, k * P:(k + 1) * P], 8, self.QT2, r, bias=bias)
        wait(dve, *r, vb, sk)
        for g in range(KVH2):
            src = TOK[:, :, kcol + g * DH2:kcol + (g + 1) * DH2]
            for half in range(2):
                v = self.cdve(dve.tensor_copy(self.KDUP[:, :, g * P + half * DH2:g * P + (half + 1) * DH2], src))
        vv = self.cdve(dve.tensor_tensor(TOK[:, 0, vcol:ucol], TOK[:, 0, vcol:ucol], self.VB[:, :], ALU.add))
        vv = self.cdve(dve.tensor_tensor(TOK[:, 1, vcol:ucol], TOK[:, 1, vcol:ucol], self.VB[:, :], ALU.add))
        yield
        wait(pe, v)
        ps = self.bank(0)
        for g in range(KVH2):
            for i in range(TT):
                inst = self.tr(ps[:, g * S + i * P:g * S + (i + 1) * P], self.KDUP[:, i, g * P:(g + 1) * P])
        done = self.cpe(inst)
        for g in range(KVH2):
            for half in range(2):
                rows = slice(half * DH2, (half + 1) * DH2)
                c = self.cact(act.activation(self.SV[rows, 28, g:g + 1], self.V3[g * DH2:(g + 1) * DH2, 8:9], ACT.Copy))
        wait(dve, done, c)
        for g in range(KVH2):
            k = self.cdve(dve.tensor_scalar(self.KT2[:, g, :], ps[:, g * S:(g + 1) * S], self.SV[:, 28, g:g + 1], None,
                                            ALU.add))
        self.release(0, k)
        yield
        wait(pe, *q, k, vv)

        def scores(h):
            r = slice(DH2 * (h % 2), DH2 * (h % 2) + DH2)
            return self.QT2[r, h // 2, :], self.KT2[r, h // (HEADS2 // KVH2), :]

        def values(h):
            c = vcol + DH2 * (h // (HEADS2 // KVH2))
            return [TOK[:, i, c:c + DH2] for i in range(TT)]

        yield from self.attention(HEADS2, scores, values, (self.OH2, self.OL2), self.DIST2,
                                  lambda h: 2.0 ** (-8.0 * (h + 1) / HEADS2), DH2 ** -0.5, sink=self.SINK, dh=DH2,
                                  ptile=self.PR2, ptT=self.PT2, interlude=(MIDWAY, self.ssm_halves))


def block_program(nc, tensors, out):
    with ExitStack() as ctx:
        Kernel(nc, ctx, tensors, out).build()


def kernel(**inputs):
    import concourse.bacc as bacc
    from concourse.bass_utils import run_bass_kernel_spmd

    nc = bacc.Bacc("TRN2", target_bir_lowering=False, num_devices=1, dynamic_dma_scratch_size=1024)
    arrays = {f"in_{n}": np.ascontiguousarray(a) for n, a in inputs.items()}
    tensors = {n: nc.dram_tensor(f"in_{n}", a.shape, mybir.dt.from_np(arrays[f"in_{n}"].dtype),
                                 kind="ExternalInput").ap() for n, a in inputs.items()}
    out = nc.dram_tensor("out", (1, S, D), F32, kind="ExternalOutput").ap()
    block_program(nc, tensors, out)
    r = run_bass_kernel_spmd(nc, [arrays], core_ids=[0])
    return r.results[0]["out"]
```
